# Optimizing a Trainium2 kernel written in Bass

```python
import jax, jax.numpy as jnp
from jax import lax
import numpy as np

D_MODEL = 1024
BATCH = 1
SEQ = 512
DEPTH = 2

CHUNK = 64
EPS = 1e-6
ROPE_THETA = 10000.0
A_HEADS = 4
A_DK = 128
A_DV = 128
A_WIDTH = A_HEADS * A_DV
B_HEADS = 4
B_DH = 128
B_WIDTH = B_HEADS * B_DH
Q_LORA = 256
IDX_HEADS = 16
IDX_DIM = 64
TOPK_MAX = 256
Q_BLOCK = 128
D_MIX = A_WIDTH + B_WIDTH
IN_SIZES = (A_WIDTH, A_WIDTH, A_WIDTH, A_WIDTH, Q_LORA, B_WIDTH, B_WIDTH, IDX_DIM, IDX_HEADS)
D_IN = 4 * A_WIDTH + Q_LORA + 2 * B_WIDTH + IDX_DIM + IDX_HEADS
N_MEM = 256
X_HEADS = 4
X_DH = 128
X_WIDTH = X_HEADS * X_DH
N_GROUPS = 4
EXP_PER_GROUP = 4
TOP_K_IN_GROUP = 2
D_EXPERT = 256

kernel_name = "hybrid_hgrn2_dsa_hmoe_block"

def rms_norm(x, gain):
    xf = x.astype(jnp.float32)
    y = xf * lax.rsqrt(jnp.mean(xf * xf, axis=-1, keepdims=True) + EPS)
    return (y * gain.astype(jnp.float32)).astype(x.dtype)

def rope_tables(positions, dim):
    inv = ROPE_THETA ** (-jnp.arange(0, dim, 2, dtype=jnp.float32) / dim)
    ang = positions.astype(jnp.float32)[..., None] * inv
    return jnp.cos(ang), jnp.sin(ang)

def apply_rope(x, cos, sin):
    d2 = x.shape[-1] // 2
    xf = x.astype(jnp.float32)
    x1, x2 = xf[..., :d2], xf[..., d2:]
    c, s = cos[:, :, None, :], sin[:, :, None, :]
    return jnp.concatenate([x1 * c - x2 * s, x2 * c + x1 * s], axis=-1).astype(x.dtype)

def hgrn2_mixer(q_raw, f_raw, i_raw, g_raw, lb, gnorm_gain):
    f32 = jnp.float32
    bsz, seq = q_raw.shape[:2]
    n_chunks = seq // CHUNK
    q = jax.nn.silu(q_raw.astype(f32))
    z = f_raw.astype(f32)
    log_f = jnp.logaddexp(jnp.log(lb), jnp.log1p(-lb) + jax.nn.log_sigmoid(z))
    k = (1.0 - lb) * jax.nn.sigmoid(-z)
    v = i_raw.astype(f32)

    def to_chunks(t):
        return t.reshape(bsz, n_chunks, CHUNK, A_HEADS, t.shape[-1]).transpose(1, 0, 3, 2, 4)

    causal = jnp.tril(jnp.ones((CHUNK, CHUNK), dtype=bool))[:, :, None]

    def step(state, inp):
        qb, kb, vb, lfb = inp
        b = jnp.cumsum(lfb, axis=2)
        o_inter = jnp.einsum('bhtk,bhkv->bhtv', qb * jnp.exp(b), state)
        diff = b[:, :, :, None, :] - b[:, :, None, :, :]
        decay = jnp.exp(jnp.where(causal, diff, -jnp.inf))
        scores = jnp.einsum('bhtk,bhsk,bhtsk->bhts', qb, kb, decay)
        o_intra = jnp.einsum('bhts,bhsv->bhtv', scores, vb)
        b_last = b[:, :, -1:, :]
        new_state = (jnp.exp(b_last[:, :, 0, :])[..., None] * state
                     + jnp.einsum('bhsk,bhsv->bhkv', kb * jnp.exp(b_last - b), vb))
        return new_state, o_inter + o_intra

    s0 = jnp.zeros((bsz, A_HEADS, A_DK, A_DV), f32)
    _, o = lax.scan(step, s0, tuple(map(to_chunks, (q, k, v, log_f))))
    o = o.transpose(1, 0, 3, 2, 4).reshape(bsz, seq, A_HEADS, A_DV)
    g = g_raw.reshape(bsz, seq, A_HEADS, A_DV).astype(f32)
    o = rms_norm(o, gnorm_gain) * jax.nn.silu(g)
    return o.reshape(bsz, seq, A_WIDTH).astype(q_raw.dtype)

def dsa_mixer(q_lat, k_raw, v_raw, kidx_raw, widx, cos_m, sin_m, cos_i, sin_i,
              q_lat_gain, w_qb, w_qidx, qn_gain, kn_gain, kidx_gain):
    f32 = jnp.float32
    bsz, seq = q_lat.shape[:2]
    c = rms_norm(q_lat, q_lat_gain)
    q = rms_norm((c @ w_qb).reshape(bsz, seq, B_HEADS, B_DH), qn_gain)
    q = apply_rope(q, cos_m, sin_m)
    k = apply_rope(rms_norm(k_raw.reshape(bsz, seq, B_HEADS, B_DH), kn_gain), cos_m, sin_m)
    v = v_raw.reshape(bsz, seq, B_HEADS, B_DH)
    q_idx = apply_rope((c @ w_qidx).reshape(bsz, seq, IDX_HEADS, IDX_DIM), cos_i, sin_i)
    k_idx = apply_rope(rms_norm(kidx_raw, kidx_gain)[:, :, None, :], cos_i, sin_i)[:, :, 0, :]
    w_h = widx.astype(f32) * (IDX_HEADS ** -0.5 * IDX_DIM ** -0.5)
    top_k = min(TOPK_MAX, seq // 4)
    n_blocks = seq // Q_BLOCK
    key_pos = jnp.arange(seq, dtype=jnp.int32)
    scale = B_DH ** -0.5
    gather = jax.vmap(lambda kb, ib: kb[ib])

    def block(i):
        start = i * Q_BLOCK
        qi = lax.dynamic_slice_in_dim(q_idx, start, Q_BLOCK, axis=1)
        wi = lax.dynamic_slice_in_dim(w_h, start, Q_BLOCK, axis=1)
        qb = lax.dynamic_slice_in_dim(q, start, Q_BLOCK, axis=1)
        qpos = start + jnp.arange(Q_BLOCK, dtype=jnp.int32)
        limit = (qpos // CHUNK + 1) * CHUNK
        admissible = key_pos[None, :] < limit[:, None]
        idx_logits = jnp.einsum('bqhd,bsd->bqhs', qi, k_idx).astype(f32)
        score = jnp.einsum('bqhs,bqh->bqs', jax.nn.relu(idx_logits), wi)
        score = jnp.where(admissible[None], score, -jnp.inf)
        _, sel = lax.top_k(score, top_k)
        sel_ok = sel < limit[None, :, None]
        k_sel = gather(k, sel)
        v_sel = gather(v, sel)
        logits = jnp.einsum('bqhd,bqkhd->bhqk', qb, k_sel).astype(f32) * scale
        logits = jnp.where(sel_ok[:, None], logits, -jnp.inf)
        p = jax.nn.softmax(logits, axis=-1)
        out = jnp.einsum('bhqk,bqkhd->bqhd', p.astype(v.dtype), v_sel)
        return out.reshape(bsz, Q_BLOCK, B_WIDTH)

    out = lax.map(block, jnp.arange(n_blocks, dtype=jnp.int32))
    return out.transpose(1, 0, 2, 3).reshape(bsz, seq, B_WIDTH)

def memory_cross_attention(h, m, w_q, w_k, w_v, w_o, qn_gain, kn_gain):
    bsz, seq = h.shape[:2]
    n_mem = m.shape[1]
    q = rms_norm((h @ w_q).reshape(bsz, seq, X_HEADS, X_DH), qn_gain)
    k = rms_norm((m @ w_k).reshape(bsz, n_mem, X_HEADS, X_DH), kn_gain)
    v = (m @ w_v).reshape(bsz, n_mem, X_HEADS, X_DH)
    logits = jnp.einsum('bshd,bmhd->bhsm', q, k).astype(jnp.float32) * (X_DH ** -0.5)
    p = jax.nn.softmax(logits, axis=-1)
    o = jnp.einsum('bhsm,bmhd->bshd', p.astype(v.dtype), v).reshape(bsz, seq, X_WIDTH)
    return o @ w_o

def hierarchical_moe(h, w_rg, b_rg, w_re, b_re, w_gu, w_dn):
    f32 = jnp.float32
    bsz, seq, d = h.shape
    t = h.reshape(-1, d)
    g_logits = (t @ w_rg).astype(f32) + b_rg.astype(f32)
    g_prob = jax.nn.softmax(g_logits, axis=-1)
    g_sel = jnp.argmax(g_logits, axis=-1)
    g_w = jnp.take_along_axis(g_prob, g_sel[:, None], axis=-1)
    e_all = jnp.einsum('nd,dge->nge', t, w_re).astype(f32) + b_re.astype(f32)
    e_logits = jnp.take_along_axis(e_all, g_sel[:, None, None], axis=1)[:, 0]
    top_v, top_i = lax.top_k(e_logits, TOP_K_IN_GROUP)
    top_w = jax.nn.softmax(top_v, axis=-1)
    gate_e = jnp.sum(jax.nn.one_hot(top_i, EXP_PER_GROUP, dtype=f32) * top_w[..., None], axis=1)
    gate = (jax.nn.one_hot(g_sel, N_GROUPS, dtype=f32)[:, :, None]
            * gate_e[:, None, :] * g_w[:, :, None])
    out = jnp.zeros_like(t)
    for g in range(N_GROUPS):
        gu = jnp.einsum('nd,edf->nef', t, w_gu[g])
        act = jax.nn.silu(gu[..., :D_EXPERT]) * gu[..., D_EXPERT:]
        act = act * gate[:, g, :, None].astype(act.dtype)
        out = out + jnp.einsum('nef,efd->nd', act, w_dn[g])
    return out.reshape(bsz, seq, d)

def setup_inputs(seed: int = 0) -> dict:
    key = jax.random.key(seed)
    ks = iter(jax.random.split(key, 48))
    f32 = jnp.float32

    def nrm(shape, fan_in):
        return jax.random.normal(next(ks), shape, f32) * (fan_in ** -0.5)

    def gain(shape):
        return 1.0 + 0.02 * jax.random.normal(next(ks), shape, f32)

    L = DEPTH
    x = jax.random.normal(next(ks), (BATCH, SEQ, D_MODEL), f32)
    mem = jax.random.normal(next(ks), (BATCH, N_MEM, D_MODEL), f32)
    offsets = jax.random.randint(next(ks), (BATCH, 1), 0, 16, dtype=jnp.int32) * CHUNK
    positions = (offsets + jnp.arange(SEQ, dtype=jnp.int32)[None, :]).astype(jnp.int32)
    return {
        "x": x,
        "mem": mem,
        "positions": positions,
        "norm_mix": gain((L, D_MODEL)),
        "w_in": nrm((L, D_MODEL, D_IN), D_MODEL),
        "lb_raw": 0.5 * jax.random.normal(next(ks), (L, A_WIDTH), f32),
        "a_gnorm": gain((L, A_DV)),
        "b_qlat_gain": gain((L, Q_LORA)),
        "b_wqb": nrm((L, Q_LORA, B_WIDTH), Q_LORA),
        "b_wqidx": nrm((L, Q_LORA, IDX_HEADS * IDX_DIM), Q_LORA),
        "b_qnorm": gain((L, B_DH)),
        "b_knorm": gain((L, B_DH)),
        "b_kidx_norm": gain((L, IDX_DIM)),
        "w_out": nrm((L, D_MIX, D_MODEL), D_MIX),
        "norm_x": gain((L, D_MODEL)),
        "norm_mem": gain((L, D_MODEL)),
        "x_wq": nrm((L, D_MODEL, X_WIDTH), D_MODEL),
        "x_wk": nrm((L, D_MODEL, X_WIDTH), D_MODEL),
        "x_wv": nrm((L, D_MODEL, X_WIDTH), D_MODEL),
        "x_wo": nrm((L, X_WIDTH, D_MODEL), X_WIDTH),
        "x_qnorm": gain((L, X_DH)),
        "x_knorm": gain((L, X_DH)),
        "norm_ffn": gain((L, D_MODEL)),
        "w_rg": nrm((L, D_MODEL, N_GROUPS), D_MODEL),
        "b_rg": 0.01 * jax.random.normal(next(ks), (L, N_GROUPS), f32),
        "w_re": nrm((L, D_MODEL, N_GROUPS, EXP_PER_GROUP), D_MODEL),
        "b_re": 0.01 * jax.random.normal(next(ks), (L, N_GROUPS, EXP_PER_GROUP), f32),
        "w_gu": nrm((L, N_GROUPS, EXP_PER_GROUP, D_MODEL, 2 * D_EXPERT), D_MODEL),
        "w_dn": nrm((L, N_GROUPS, EXP_PER_GROUP, D_EXPERT, D_MODEL), D_EXPERT),
    }

def reference(x, mem, positions, norm_mix, w_in, lb_raw, a_gnorm, b_qlat_gain, b_wqb,
              b_wqidx, b_qnorm, b_knorm, b_kidx_norm, w_out, norm_x, norm_mem, x_wq, x_wk,
              x_wv, x_wo, x_qnorm, x_knorm, norm_ffn, w_rg, b_rg, w_re, b_re, w_gu, w_dn):
    bsz, seq, _ = x.shape
    cos_m, sin_m = rope_tables(positions, B_DH)
    cos_i, sin_i = rope_tables(positions, IDX_DIM)
    lb_all = jnp.cumsum(jax.nn.softmax(lb_raw.astype(jnp.float32), axis=0), axis=0)
    lb_all = lb_all - lb_all[0:1]
    split_at = np.cumsum(IN_SIZES)[:-1].tolist()
    for l in range(DEPTH):
        h = rms_norm(x, norm_mix[l])
        u = h @ w_in[l]
        a_q, a_f, a_i, a_g, b_ql, b_k, b_v, b_kidx, b_widx = jnp.split(u, split_at, axis=-1)
        heads4 = lambda t: t.reshape(bsz, seq, A_HEADS, A_DK)
        o_a = hgrn2_mixer(heads4(a_q), heads4(a_f), heads4(a_i), a_g,
                          lb_all[l].reshape(A_HEADS, A_DK), a_gnorm[l])
        o_b = dsa_mixer(b_ql, b_k, b_v, b_kidx, b_widx, cos_m, sin_m, cos_i, sin_i,
                        b_qlat_gain[l], b_wqb[l], b_wqidx[l], b_qnorm[l], b_knorm[l],
                        b_kidx_norm[l])
        x = x + jnp.concatenate([o_a, o_b], axis=-1) @ w_out[l]
        h = rms_norm(x, norm_x[l])
        m = rms_norm(mem, norm_mem[l])
        x = x + memory_cross_attention(h, m, x_wq[l], x_wk[l], x_wv[l], x_wo[l],
                                       x_qnorm[l], x_knorm[l])
        h = rms_norm(x, norm_ffn[l])
        x = x + hierarchical_moe(h, w_rg[l], b_rg[l], w_re[l], b_re[l], w_gu[l], w_dn[l])
    return x


_drawn_inputs = setup_inputs


def setup_inputs(seed=0):
    import zlib

    import numpy as np

    out = dict(_drawn_inputs(seed))
    spreads = {}
    factors = {'b_qnorm': 5.37,
     'b_knorm': 4.5,
     'norm_x': 2.796,
     'norm_mem': 2.86,
     'x_qnorm': 3.641,
     'x_knorm': 4.626,
     'b_rg': 2.845,
     'b_re': 2.967}
    for name, (base, spread) in spreads.items():
        noise = np.random.default_rng([zlib.crc32(name.encode()), seed]).standard_normal(out[name].shape)
        drawn = base * np.exp(spread * noise) if base else spread * noise
        out[name] = __import__('jax').numpy.asarray(drawn.astype(out[name].dtype))
    for name, factor in factors.items():
        out[name] = (out[name] * factor).astype(out[name].dtype)
    return out
```

```python
import concourse.bass as bass
from concourse import mybir
from contextlib import ExitStack
import numpy as np

F32 = mybir.dt.float32
I32 = mybir.dt.int32
U8 = mybir.dt.uint8
ALU = mybir.AluOpType
ACT = mybir.ActivationFunctionType
AX = mybir.AxisListType

P = 128
D_MODEL, SEQ, DEPTH = 1024, 512, 2
EPS = 1e-6
ROPE_THETA = 10000.0
HEADS, DH = 4, 128
WIDTH = HEADS * DH
Q_LORA = 256
IDX_HEADS, IDX_DIM = 16, 64
TOPK = min(256, SEQ // 4)
CHUNK = 64
N_MEM = 256
N_GROUPS, EXP_PER_GROUP = 4, 4
N_EXPERTS = N_GROUPS * EXP_PER_GROUP
D_EXPERT = 256
T = SEQ // P
K = D_MODEL // P
M = N_MEM // P
LATER = list(range(1, T))
D_IN = 4 * WIDTH + Q_LORA + 2 * WIDTH + IDX_DIM + IDX_HEADS
C_AQ, C_AF, C_AI, C_AG = (n * WIDTH for n in range(4))
C_QL = 4 * WIDTH
C_BK = C_QL + Q_LORA
C_BV = C_BK + WIDTH
C_KI = C_BV + WIDTH
N_KI = IDX_DIM + IDX_HEADS
N_QL = Q_LORA + N_KI
HALVES = [64, 32, 16, 8, 4, 2, 1]
LEVELS = len(HALVES)
SCALE = DH ** -0.5
W_IDX = IDX_HEADS ** -0.5 * IDX_DIM ** -0.5
REFUSED = -1.0e30
TAKEN = -3.0e38

G_MIX, G_X, G_MEM, G_FFN = (n * K for n in range(4))
G_QLAT = 4 * K
G_AG = G_QLAT + Q_LORA // P
G_XQ = G_AG + 1
G_XK = G_XQ + 1
N_COL = G_XK + 1
R_Q, R_K, R_KI = 0, DH, 2 * DH
R_BIAS = R_KI + IDX_DIM
N_ROUTE = N_GROUPS + N_EXPERTS
N_ROW = R_BIAS + N_ROUTE

UNIT = 4096
RING = 4
UNITS = ["ql", "kx", "vx", "kb", "lora", "vb", "vA", "g", "f", "q", "outA", "outB", "xq", "xo"]
PARTS = {"ql": 2, "lora": 2}
SLOT = {u: n % RING for n, u in enumerate(UNITS)}
MOE_TURNS = 4
TURN = N_EXPERTS // MOE_TURNS
MOE_UNITS = ["gu0", "gu1", "dn0", "gu2", "gu3", "dn1"]
MOE_SLOT = {"gu0": 2, "gu1": 3, "gu2": 0, "gu3": 1, "dn0": RING, "dn1": RING + 1}
U_TURN = len(MOE_UNITS)
U_LAYER = len(UNITS) + MOE_TURNS * U_TURN
SLOTS = RING + 2


def slot_loads(slot):
    return (sum(PARTS.get(u, 1) for u in UNITS if SLOT[u] == slot),
            sum(1 for u in MOE_UNITS if MOE_SLOT[u] == slot))


def loads_so_far(part, where, name):
    return sum(PARTS.get(u, 1) for u in part[:part.index(name) + 1] if where[u] == where[name])


def used_before(name):
    if name in SLOT:
        n = UNITS.index(name)
        earlier = [m for m in range(n) if SLOT[UNITS[m]] == SLOT[name]]
        last = max((m for m, u in enumerate(MOE_UNITS) if MOE_SLOT[u] == SLOT[name]), default=0)
        return U_LAYER + (earlier[-1] + 1 if earlier else last + 1 - U_TURN)
    n = MOE_UNITS.index(name)
    earlier = [m for m, u in enumerate(UNITS) if SLOT[u] == MOE_SLOT[name]]
    first = earlier[-1] if earlier else UNITS.index("outB")
    return U_LAYER + max(first + 1, len(UNITS) + n + 1 - U_TURN)


def products():
    out = [("hT", k) for k in range(K)] + [("ql", t) for t in range(T)]
    out += [("mT", j) for j in range(K // 2)] + [("kx", m) for m in range(M)]
    out += [("cT", c) for c in range(Q_LORA // P)] + [("kiT",)]
    out += [("qi", t, n) for t in LATER for n in range(2)]
    out += [("vx", m) for m in range(M)] + [("kxT", m) for m in range(M)]
    for name in ("kb", "qb"):
        for t in range(T):
            out += [(name, t)] + ([(name + "T", t - 1)] if t else [])
        out += [(name + "T", T - 1)]
    out += [("qiT", t, n) for t in LATER for n in range(2)]
    out += [("si", t, h) for t in LATER for h in range(IDX_HEADS)]
    out += [("vb", t) for t in range(T)] + [("vA", t) for t in range(T)]
    out += [("f", 0), ("q", 0)] + [("g", t) for t in range(T)]
    for h in range(HEADS):
        out += [("lv", h, n) for n in range(LEVELS + 1)]
        if h + 1 < HEADS:
            out += [("f", h + 1), ("q", h + 1)]
        out += [("kdT", h), ("dS", h), ("o", h)]
    out += [("oaT", t) for t in range(T)]
    out += [("lg", m) for m in range(2)]
    for m in range(T * HEADS):
        out += [("pT", m)] + ([("lg", m + 2)] if m + 2 < T * HEADS else []) + ([("pv", m - 1)] if m else [])
    out += [("pv", T * HEADS - 1)]
    out += [("xo", t, n) for t in range(T) for n in range(2)]
    out += [("hxT", k) for k in range(K)]
    for t in range(T):
        out += [("qx", t)] + ([("qxT", t - 1)] if t else [])
    out += [("qxT", T - 1)] + [("lx", m) for m in range(2)]
    for m in range(2 * T):
        out += [("pxT", m)] + ([("lx", m + 2)] if m + 2 < 2 * T else [])
        out += [("px", m // 2 - 1)] if m % 2 == 0 and m else []
    out += [("px", T - 1)]
    out += [("xx", t, n) for t in range(T) for n in range(2)]
    out += [("hfT", k) for k in range(K)] + [("rt",)]
    return out


def moe_products():
    out = []
    for pair in range(TURN // 2):
        both = (2 * pair, 2 * pair + 1)
        out += [("gu", e, f) for e in both for f in (0, 2, 1, 3)]
        out += [("y", e, t, n) for e in both for t in range(T) for n in range(2)]
    return out


BANKS = 8
PRODUCTS = products()
MOE_PRODUCTS = moe_products()
ON_VECTOR = ("q", "lv", "dS", "lg", "pv", "xo", "pxT", "xx", "rt")


def emptied_by(name):
    if name[0] in ("hT", "hxT", "hfT"):
        return ("act", "dve")[name[1] % 2]
    return "dve" if name[0] in ON_VECTOR else "act"


EMPTIED = {e: [p for p in PRODUCTS if emptied_by(p) == e] for e in ("act", "dve")}
for h in range(1, HEADS):
    EMPTIED["dve"].remove(("q", h))
    EMPTIED["dve"].insert(EMPTIED["dve"].index(("dS", h - 1)) + 1, ("q", h))
N_SILU = 2 * TURN
N_Y = TURN * T * 2
Y_EXPERT = T * 2

SIGNALS = [
    "params",
    "mem_in",
    "product",
    "act_emptied",
    "dve_emptied",
    "rn_x", "rn_mem", "rn_ql", "rn_kx", "rn_kb", "rn_qb", "rn_o", "rn_qx",
    "x_scaled", "mem_scaled",
    "c_ready", "ki_ready", "kx_ready", "kb_ready", "qb_ready",
    "qi_ready",
    "relu_ready",
    "relu_used",
    "bias_ready",
    "sigma_g", "g_ready",
    "forget", "queries",
    "b_ready",
    "diff", "decay",
    "qL", "kL",
    "ends",
    "kd_ready", "qe_ready",
    "state",
    "og_ready",
    "logits", "exps", "probs",
    "x_mixed",
    "qx_ready", "max_x", "exps_x", "probs_x",
    "x_crossed",
    "router_exp", "router_exp2", "router_logits", "gates",
    "lb_ready", "levels_zero", "turn_gates", "moe_product", "silu", "hidden", "y_added",
    "dve_own", "act_own", "pool_own",
    "layer_end",
]


class Own:

    def __init__(self, engine, semaphore):
        self.engine, self.semaphore, self.count = engine, semaphore, 0

    def done(self, instruction):
        self.count += 1
        instruction.then_inc(self.semaphore, 1)
        return self.count

    def need(self, count=None):
        self.engine.wait_ge(self.semaphore, self.count if count is None else count)


class Emptier:

    def __init__(self, engine, key, sem, banks):
        self.engine, self.key, self.sem, self.banks, self.count = engine, key, sem, banks, 0

    def take(self, *name):
        n = PRODUCTS.index(name)
        self.engine.wait_ge(self.sem["product"], n + 1)
        return self.banks[n % BANKS]

    def empty(self, instruction, *name):
        assert EMPTIED[self.key][self.count] == name, (self.key, self.count, EMPTIED[self.key][self.count], name)
        self.count += 1
        instruction.then_inc(self.sem[self.key + "_emptied"], 1)


def emptied(engine, sem, *name):
    key = emptied_by(name)
    engine.wait_ge(sem[key + "_emptied"], EMPTIED[key].index(name) + 1)


def over(ap, n):
    return ap.unsqueeze(1).broadcast_to((ap.shape[0], n, ap.shape[1]))


def each(ap, n):
    return ap.unsqueeze(2).broadcast_to((ap.shape[0], ap.shape[1], n))


def hybrid_block(nc, x, mem, positions, w_in, b_wqb, b_wqidx, w_out, x_wq, x_wk, x_wv, x_wo,
                 w_rg, w_re, w_gu, w_dn, colparams, rowparams, lb_raw, freqs, ident, masks, out):
    ctx = ExitStack()
    with ctx:
        def sb(name, shape, dt=F32):
            return ctx.enter_context(nc.sbuf_tensor(name, [P] + shape, dt))[tuple([slice(None)] * (len(shape) + 1))]

        def sem1(name):
            return ctx.enter_context(nc.semaphore(name))

        sem = {name: sem1(name) for name in SIGNALS}
        slot_full = [sem1(f"slot_full{n}") for n in range(SLOTS)]
        w_used = sem1("w_used")
        consts_in = sem1("consts_in")
        ropes = sem1("ropes")
        prologue = sem1("prologue")
        pro_act = sem1("pro_act")
        prologue_own = sem1("prologue_own")
        loads_begun = sem1("loads_begun")
        cleared = sem1("cleared")
        out_done = sem1("out_done")

        X = sb("X", [T, D_MODEL])
        HT = sb("HT", [K, SEQ])
        ring = sb("ring", [RING, UNIT])
        XC = sb("XC", [4096])
        CB = sb("CB", [2048])
        AR = sb("AR", [9216])
        QT = sb("QT", [HEADS, SEQ])
        KT = sb("KT", [HEADS, SEQ])
        KIT = sb("KIT", [SEQ])
        SC = sb("SC", [len(LATER), SEQ])
        TOK = sb("TOK", [2, WIDTH])
        ST = sb("ST", [T, DH])
        KXT = sb("KXT", [HEADS, N_MEM])
        VX = sb("VX", [M, WIDTH])
        JUNK = sb("JUNK", [256])
        ROT = sb("ROT", [512])
        idn = sb("idn", [P])
        mask = sb("mask", [LEVELS + 1, P], U8)
        cos_m = sb("cos_m", [T, DH // 2])
        sin_m = sb("sin_m", [T, 2, DH // 2])
        cos_i = sb("cos_i", [T, IDX_DIM // 2])
        sin_i = sb("sin_i", [T, 2, IDX_DIM // 2])
        bias0 = sb("bias0", [P])
        ones = sb("ones", [P])
        rows = sb("rows", [N_ROW])
        cols = sb("cols", [N_COL])
        lb_all = sb("lb_all", [DEPTH, HEADS])
        lb = sb("lb", [HEADS])
        one_lb = sb("one_lb", [HEADS])
        small = sb("small", [256])
        pos = sb("pos", [T], I32)
        masks_in = ring[:, RING - 1, 0:(LEVELS + 1) * P].bitcast(I32).rearrange("p (n s) -> p n s", s=P)

        XN = XC.rearrange("p (t k d) -> p t k d", t=T, k=K)
        QIT = XC[:, 0:3072].rearrange("p (t g d) -> p t g d", t=len(LATER), g=IDX_HEADS // 2)
        OAB = XC.rearrange("p (k t) -> p k t", k=2 * HEADS)
        E1, L1, L2, S1 = (XC[:, 512 * n:512 * n + 512] for n in range(4))
        G = XC[:, 2048:4096].rearrange("p (t n) -> p t n", t=T)
        C = CB[:, 0:1024].rearrange("p (t c) -> p t c", t=T)
        CT = CB[:, 1024:2048].rearrange("p (c t) -> p c t", c=2)
        EQ, DE, QL, KL = (CB[:, 512 * n:512 * n + 512] for n in range(4))
        PR = CB[:, 0:1024].rearrange("p (n s) -> p n s", n=2)
        PT = CB[:, 1024:2048].rearrange("p (n s) -> p n s", n=2)
        AB, OA, VA, VB = AR[:, 0:3072], AR[:, 3072:5120], AR[:, 5120:7168], AR[:, 7168:9216]
        QI = AB.rearrange("p (t n) -> p t n", t=len(LATER))
        RELU = AB[:, 0:1024].rearrange("p (n s) -> p n s", n=2)
        BB, KK, QQ, SCT, KDT, XX = (AB[:, 512 * n:512 * n + 512] for n in range(6))
        MEMX = OA.rearrange("p (m d) -> p m d", m=M)
        MN = VA.rearrange("p (m k d) -> p m k d", m=M, k=K)
        MT = QT.rearrange("p h t -> p (h t)").rearrange("p (k m) -> p k m", k=K)
        PTMP = OA[:, 0:1024]
        O = OA.rearrange("p (t n) -> p t n", t=T)
        VAt = VA.rearrange("p (t n) -> p t n", t=T)
        VBt = VB.rearrange("p (t n) -> p t n", t=T)
        QLB = ROT
        DN = [AR[:, n * UNIT:(n + 1) * UNIT] for n in range(2)]
        ACTT = QT.rearrange("p h t -> p (h t)").rearrange("p (e f t) -> p e f t", e=2, f=2)
        SILU = KT[:, 0:2, :]
        OXT = KT

        def take_small(n):
            take_small.at += n
            return small[:, take_small.at - n:take_small.at]
        take_small.at = 0
        ss_x = take_small(T)
        rn_x = take_small(T)
        ss_m = take_small(M)
        rn_m = take_small(M)
        ss_ql = take_small(2 * T).rearrange("p (t n) -> p t n", t=T)
        rn_ql = take_small(2 * T).rearrange("p (t n) -> p t n", t=T)
        ss_h = take_small(2 * HEADS).rearrange("p (t n) -> p t n", t=2)
        rn_h = take_small(2 * HEADS).rearrange("p (t n) -> p t n", t=2)
        widx = take_small(T * IDX_HEADS).rearrange("p (t n) -> p t n", t=T)
        top8 = take_small(8 * len(LATER)).rearrange("p (t n) -> p t n", t=len(LATER))
        e_end = take_small(T)
        mx = take_small(8).rearrange("p (n j) -> p n j", n=4)
        sm = take_small(8).rearrange("p (n j) -> p n j", n=4)
        gate = take_small(N_EXPERTS * T).rearrange("p (e t) -> p e t", e=N_EXPERTS)
        gate_now = take_small(TURN * T).rearrange("p (e t) -> p e t", e=TURN)
        rlog = SC[:, 0, 0:T * N_ROUTE].rearrange("p (t n) -> p t n", t=T)
        rw = SC[:, 1, 0:48 * T].rearrange("p (i t n) -> p i t n", t=T, n=4)
        KIN = KIT.rearrange("p (t n) -> p t n", t=T)
        KI = SC[:, 0, 0:T * N_KI].rearrange("p (t n) -> p t n", t=T)
        wr_sb = sb("wr_sb", [K, N_ROUTE])

        banks = [ctx.enter_context(nc.psum_tensor(f"bank{n}", [P, 512], F32))[:, :] for n in range(BANKS)]

        block = ctx.enter_context(nc.Block())

        def weight_view(slot):
            return ring[:, slot, :] if slot < RING else DN[slot - RING]

        @block.sync
        def _(sp):
            sp.dma_start(X, x.rearrange("b (t p) d -> p (b t) d", p=P)).then_inc(consts_in, 16)
            sp.dma_start(idn, ident).then_inc(consts_in, 16)
            sp.dma_start(pos, positions).then_inc(consts_in, 16)
            sp.dma_start(masks_in, masks).then_inc(consts_in, 16)
            sp.dma_start(ROT[:, 0:DH // 2 + IDX_DIM // 2], freqs.partition_broadcast(P)).then_inc(consts_in, 16)
            sp.dma_start(lb_all, lb_raw).then_inc(consts_in, 16)

            in_v = w_in.rearrange("l (p k) n -> (l p) k n", k=K)
            qb_v = b_wqb.rearrange("l (k p) n -> l p k n", p=P)
            qi_v = b_wqidx.rearrange("l (k p) n -> l p k n", p=P)
            out_v = w_out.rearrange("l (s k p) n -> (l s) p k n", s=2, p=P)
            xo_v = x_wo.rearrange("l (k p) n -> l p k n", p=P)
            xq_v, xk_v, xv_v = (w.rearrange("l (p k) n -> (l p) (k n)", k=K) for w in (x_wq, x_wk, x_wv))
            gu_v = w_gu.rearrange("l g e (p k) f -> (l g e p) (k f)", k=K)
            dn_v = w_dn.rearrange("l g (a e) (k p) d -> (l g a) p e k d", e=2, p=P)

            with sp.Fori(0, DEPTH) as L:
                def sources(name):
                    rows_l = bass.ds(L * P, P)

                    def cut(a, n):
                        return in_v[rows_l, :, a:a + n]
                    return {
                        "ql": lambda: [(cut(C_QL, Q_LORA), 0, Q_LORA), (cut(C_KI, N_KI), Q_LORA, N_KI)],
                        "kb": lambda: [(cut(C_BK, WIDTH), 0, WIDTH)],
                        "vb": lambda: [(cut(C_BV, WIDTH), 0, WIDTH)],
                        "vA": lambda: [(cut(C_AI, WIDTH), 0, WIDTH)],
                        "g": lambda: [(cut(C_AG, WIDTH), 0, WIDTH)],
                        "f": lambda: [(cut(C_AF, WIDTH), 0, WIDTH)],
                        "q": lambda: [(cut(C_AQ, WIDTH), 0, WIDTH)],
                    }[name]()

                for name in UNITS:
                    slot = SLOT[name]
                    if slot == RING - 1:
                        sp.wait_ge(prologue, 1)
                    sp.wait_ge(w_used, L * U_LAYER + used_before(name))
                    sp.sem_inc(loads_begun, 1)
                    w = ring[:, slot, :]
                    full = slot_full[slot]
                    if name in ("kx", "vx", "xq"):
                        src = {"kx": xk_v, "vx": xv_v, "xq": xq_v}[name]
                        sp.dma_start(w, src[bass.ds(L * P, P), :]).then_inc(full, 16)
                    elif name == "lora":
                        sp.dma_start(w[:, 0:1024].rearrange("p (k n) -> p k n", k=2),
                                     qb_v[bass.ds(L, 1), :, :, :].rearrange("l p k n -> (l p) k n")).then_inc(full, 16)
                        sp.dma_start(w[:, 1024:3072].rearrange("p (k n) -> p k n", k=2),
                                     qi_v[bass.ds(L, 1), :, :, :].rearrange("l p k n -> (l p) k n")).then_inc(full, 16)
                    elif name in ("outA", "outB"):
                        src = out_v[bass.ds(L * 2 + (name == "outB"), 1), :, :, :].rearrange("l p k n -> (l p) k n")
                        sp.dma_start(w.rearrange("p (k n) -> p k n", k=4), src).then_inc(full, 16)
                    elif name == "xo":
                        src = xo_v[bass.ds(L, 1), :, :, :].rearrange("l p k n -> (l p) k n")
                        sp.dma_start(w.rearrange("p (k n) -> p k n", k=4), src).then_inc(full, 16)
                    else:
                        width = N_QL if name == "ql" else WIDTH
                        wv = w[:, 0:K * width].rearrange("p (k n) -> p k n", k=K)
                        for src, at, n in sources(name):
                            sp.dma_start(wv[:, :, at:at + n], src).then_inc(full, 16)
                with sp.Fori(0, MOE_TURNS) as i:
                    for n, name in enumerate(MOE_UNITS):
                        slot = MOE_SLOT[name]
                        sp.wait_ge(w_used, L * U_LAYER + i * U_TURN + used_before(name))
                        sp.sem_inc(loads_begun, 1)
                        if name[:2] == "gu":
                            e = int(name[2])
                            sp.dma_start(ring[:, slot, :], gu_v[bass.ds(L * (N_EXPERTS * P) + i * (TURN * P) + e * P, P), :])\
                                .then_inc(slot_full[slot], 16)
                        else:
                            a = int(name[2])
                            src = dn_v[bass.ds(L * (N_EXPERTS // 2) + i * (TURN // 2) + a, 1), :, :, :, :]
                            sp.dma_start(DN[slot - RING].rearrange("p (e k d) -> p (e k) d", e=2, k=2),
                                         src.rearrange("a p e k d -> (a p) (e k) d")).then_inc(slot_full[slot], 16)
            sp.wait_ge(cleared, DEPTH)
            sp.dma_start(out.rearrange("b (t p) d -> p (b t) d", p=P), X).then_inc(out_done, 16)
            sp.wait_ge(out_done, 16)

        @block.tensor
        def _(pe):
            pe.sem_inc(w_used, U_LAYER)
            pe.wait_ge(consts_in, 6 * 16)
            with pe.Fori(0, DEPTH) as L:
                state = {"n": 0}

                def full(name):
                    slot = SLOT[name]
                    a, b = slot_loads(slot)
                    pe.wait_ge(slot_full[slot], L * (16 * (a + MOE_TURNS * b))
                               + 16 * loads_so_far(UNITS, SLOT, name))
                    return ring[:, slot, :]

                def open_bank(*name):
                    n = state["n"]
                    assert PRODUCTS[n] == name, (PRODUCTS[n], name)
                    state["n"] = n + 1
                    if n >= BANKS:
                        emptied(pe, sem, *PRODUCTS[n - BANKS])
                    return banks[n % BANKS]

                def close(last):
                    last.then_inc(sem["product"], 1)

                def group(bank, pairs):
                    for n, (a, b) in enumerate(pairs):
                        last = nc.tensor.matmul(bank, a, b, start=n == 0, stop=n == len(pairs) - 1)
                    return last

                def transposes(name, tiles, wait=None, used=None):
                    bank = open_bank(*name)
                    for n, tile in enumerate(tiles):
                        last = nc.tensor.transpose(bank[:, n * P:(n + 1) * P], tile, idn)
                    close(last)

                def used():
                    pe.wait_ge(sem["product"], state["n"])
                    pe.sem_inc(w_used, 1)

                def token_product(name, t, w, width, source=HT, steps=K):
                    bank = open_bank(*name)
                    close(group(bank[:, 0:width],
                                [(source[:, k, t * P:(t + 1) * P], w[:, k, :]) for k in range(steps)]))

                def norm_transposes(key, tiles_before):
                    pe.wait_ge(sem["x_scaled"], tiles_before + T)
                    for k in range(K):
                        transposes((key, k), [XN[:, t, k, :] for t in range(T)])

                def all_emptied(key):
                    emptied(pe, sem, key, K - 2)
                    emptied(pe, sem, key, K - 1)

                norm_transposes("hT", 0)
                all_emptied("hT")
                w = full("ql")[:, 0:K * N_QL].rearrange("p (k n) -> p k n", k=K)
                for t in range(T):
                    token_product(("ql", t), t, w, N_QL)
                used()
                pe.wait_ge(sem["mem_scaled"], M)
                for j in range(K // 2):
                    transposes(("mT", j), [MN[:, m, k, :] for k in (2 * j, 2 * j + 1) for m in range(M)])
                emptied(pe, sem, "mT", K // 2 - 1)
                wk = full("kx").rearrange("p (k n) -> p k n", k=K)
                for m in range(M):
                    token_product(("kx", m), m, wk, WIDTH, MT)
                used()
                pe.wait_ge(sem["c_ready"], T)
                for c in range(2):
                    transposes(("cT", c), [C[:, t, c * P:(c + 1) * P] for t in range(T)])
                pe.wait_ge(sem["ki_ready"], T)
                transposes(("kiT",), [KIN[:, t, :] for t in range(T)])
                wl = full("lora")
                wqb = wl[:, 0:1024].rearrange("p (k n) -> p k n", k=2)
                wqi = wl[:, 1024:3072].rearrange("p (k n) -> p k n", k=2)
                emptied(pe, sem, "cT", 1)
                for t in LATER:
                    for n in range(2):
                        token_product(("qi", t, n), t, wqi[:, :, n * 512:(n + 1) * 512], 512, CT, 2)
                wv = full("vx").rearrange("p (k n) -> p k n", k=K)
                for m in range(M):
                    token_product(("vx", m), m, wv, WIDTH, MT)
                used()
                for m in range(M):
                    pe.wait_ge(sem["kx_ready"], m + 1)
                    transposes(("kxT", m), [TOK[:, m, h * P:(h + 1) * P] for h in range(HEADS)])

                def tok_transposes(key, t):
                    pe.wait_ge(sem[key + "_ready"], t + 1)
                    transposes((key + "T", t), [TOK[:, t % 2, h * P:(h + 1) * P] for h in range(HEADS)])
                wkb = full("kb").rearrange("p (k n) -> p k n", k=K)
                for t in range(T):
                    token_product(("kb", t), t, wkb, WIDTH)
                    if t:
                        tok_transposes("kb", t - 1)
                used()
                tok_transposes("kb", T - 1)
                for t in range(T):
                    token_product(("qb", t), t, wqb, WIDTH, CT, 2)
                    if t:
                        tok_transposes("qb", t - 1)
                used()
                tok_transposes("qb", T - 1)
                for t in LATER:
                    pe.wait_ge(sem["qi_ready"], t)
                    for n in range(2):
                        transposes(("qiT", t, n), [QI[:, t - 1, g * P:(g + 1) * P] for g in range(4 * n, 4 * n + 4)])
                emptied(pe, sem, "kiT")
                for t in LATER:
                    for h in range(IDX_HEADS):
                        if h % 8 == 0:
                            emptied(pe, sem, "qiT", t, h // 8)
                        part = slice(64 * (h % 2), 64 * (h % 2) + 64)
                        bank = open_bank("si", t, h)
                        close(nc.tensor.matmul(bank[:, 0:(t + 1) * P], QIT[part, t - 1, h // 2, :],
                                               KIT[part, 0:(t + 1) * P], start=True, stop=True))
                for name, c0 in (("vb", C_BV), ("vA", C_AI)):
                    w = full(name).rearrange("p (k n) -> p k n", k=K)
                    for t in range(T):
                        token_product((name, t), t, w, WIDTH)
                    used()

                wf = full("f").rearrange("p (k n) -> p k n", k=K)
                wq = full("q").rearrange("p (k n) -> p k n", k=K)

                def channel_product(name, w, h):
                    bank = open_bank(name, h)
                    close(group(bank, [(w[:, k, h * P:(h + 1) * P], HT[:, k, :]) for k in range(K)]))
                channel_product("f", wf, 0)
                channel_product("q", wq, 0)
                wg = full("g").rearrange("p (k n) -> p k n", k=K)
                for t in range(T):
                    token_product(("g", t), t, wg, WIDTH)
                used()
                for h in range(HEADS):
                    for n in range(LEVELS + 1):
                        a, b = (KL, QL) if n < LEVELS else (KK, QQ)
                        if n < LEVELS:
                            pe.wait_ge(sem["qL"], h * LEVELS + n + 1)
                            pe.wait_ge(sem["kL"], h * LEVELS + n + 1)
                        bank = open_bank("lv", h, n)
                        for t in range(T):
                            s = slice(t * P, (t + 1) * P)
                            last = nc.tensor.matmul(bank[:, s], a[:, s], b[:, s], start=True, stop=True)
                        close(last)
                    if h + 1 < HEADS:
                        channel_product("f", wf, h + 1)
                        channel_product("q", wq, h + 1)
                    pe.wait_ge(sem["kd_ready"], h + 1)
                    transposes(("kdT", h), [KL[:, t * P:(t + 1) * P] for t in range(T)])
                    emptied(pe, sem, "kdT", h)
                    bank = open_bank("dS", h)
                    values = [VAt[:, t, h * P:(h + 1) * P] for t in range(T)]
                    for t in range(T - 1):
                        last = nc.tensor.matmul(bank[:, t * P:(t + 1) * P], KDT[:, t * P:(t + 1) * P], values[t],
                                                start=True, stop=True)
                    close(last)
                    bank = open_bank("o", h)
                    pe.wait_ge(sem["qe_ready"], h + 1)
                    emptied(pe, sem, "dS", h)
                    for t in range(T):
                        s = slice(t * P, (t + 1) * P)
                        last = nc.tensor.matmul(bank[:, s], SCT[:, s], values[t], start=True, stop=t == 0)
                        if t:
                            last = nc.tensor.matmul(bank[:, s], QL[:, s], ST[:, t, :], start=False, stop=True)
                    close(last)
                pe.wait_ge(sem["product"], state["n"])
                pe.sem_inc(w_used, 2)
                for t in range(T):
                    pe.wait_ge(sem["og_ready"], t + 1)
                    transposes(("oaT", t), [O[:, t, h * P:(h + 1) * P] for h in range(HEADS)])

                def logits(m):
                    t, h = divmod(m, HEADS)
                    bank = open_bank("lg", m)
                    close(nc.tensor.matmul(bank[:, 0:(t + 1) * P], QT[:, h, t * P:(t + 1) * P],
                                           KT[:, h, 0:(t + 1) * P], start=True, stop=True))

                def attend(m):
                    t, h = divmod(m, HEADS)
                    bank = open_bank("pv", m)
                    emptied(pe, sem, "pT", m)
                    close(group(bank[:, 0:P], [(VBt[:, s, h * P:(h + 1) * P], PT[:, m % 2, s * P:(s + 1) * P])
                                               for s in range(t + 1)]))
                logits(0)
                logits(1)
                for m in range(T * HEADS):
                    pe.wait_ge(sem["probs"], m + 1)
                    transposes(("pT", m), [PR[:, m % 2, s * P:(s + 1) * P] for s in range(m // HEADS + 1)])
                    if m + 2 < T * HEADS:
                        logits(m + 2)
                    if m:
                        attend(m - 1)
                attend(T * HEADS - 1)

                wa = full("outA").rearrange("p (k n) -> p k n", k=4)
                wb = full("outB").rearrange("p (k n) -> p k n", k=4)
                emptied(pe, sem, "oaT", T - 1)
                emptied(pe, sem, "pv", T * HEADS - 1)
                for t in range(T):
                    for n in range(2):
                        bank = open_bank("xo", t, n)
                        close(group(bank, [(OAB[:, k, t * P:(t + 1) * P],
                                            (wa, wb)[k // 4][:, k % 4, n * 512:(n + 1) * 512]) for k in range(K)]))
                pe.wait_ge(sem["product"], state["n"])
                pe.sem_inc(w_used, 2)

                norm_transposes("hxT", T)
                all_emptied("hxT")
                w = full("xq").rearrange("p (k n) -> p k n", k=K)

                def qx_transposes(t):
                    pe.wait_ge(sem["qx_ready"], t + 1)
                    transposes(("qxT", t), [TOK[:, t % 2, h * P:(h + 1) * P] for h in range(HEADS)])
                for t in range(T):
                    token_product(("qx", t), t, w, WIDTH)
                    if t:
                        qx_transposes(t - 1)
                used()
                qx_transposes(T - 1)

                def logits_x(m):
                    t, j = divmod(m, 2)
                    emptied(pe, sem, "qxT", t)
                    bank = open_bank("lx", m)
                    for a in range(2):
                        h = 2 * j + a
                        last = nc.tensor.matmul(bank[:, a * N_MEM:(a + 1) * N_MEM], QT[:, h, t * P:(t + 1) * P],
                                                KXT[:, h, :], start=True, stop=True)
                    close(last)

                def attend_x(t):
                    emptied(pe, sem, "pxT", 2 * t + 1)
                    bank = open_bank("px", t)
                    for h in range(HEADS):
                        j, a = divmod(h, 2)
                        last = group(bank[:, h * P:(h + 1) * P],
                                     [(VX[:, m, h * P:(h + 1) * P], PT[:, j, (2 * a + m) * P:(2 * a + m + 1) * P])
                                      for m in range(M)])
                    close(last)
                logits_x(0)
                logits_x(1)
                for m in range(2 * T):
                    pe.wait_ge(sem["probs_x"], m + 1)
                    transposes(("pxT", m), [PR[:, m % 2, s * P:(s + 1) * P] for s in range(4)])
                    if m + 2 < 2 * T:
                        logits_x(m + 2)
                    if m and m % 2 == 0:
                        attend_x(m // 2 - 1)
                attend_x(T - 1)
                w = full("xo").rearrange("p (k n) -> p k n", k=4)
                for t in range(T):
                    emptied(pe, sem, "px", t)
                    for n in range(2):
                        bank = open_bank("xx", t, n)
                        close(group(bank, [(OXT[:, h, t * P:(t + 1) * P], w[:, h, n * 512:(n + 1) * 512])
                                           for h in range(HEADS)]))
                used()

                norm_transposes("hfT", 2 * T)
                all_emptied("hfT")
                bank = open_bank("rt")
                for t in range(T):
                    last = group(bank[:, t * N_ROUTE:(t + 1) * N_ROUTE],
                                 [(HT[:, k, t * P:(t + 1) * P], wr_sb[:, k, :]) for k in range(K)])
                close(last)
                assert state["n"] == len(PRODUCTS)
                for name in PRODUCTS[-BANKS:]:
                    emptied(pe, sem, *name)

                with pe.Fori(0, MOE_TURNS) as i:
                    turn = {"n": 0}

                    def moe_full(name):
                        slot = MOE_SLOT[name]
                        a, b = slot_loads(slot)
                        pe.wait_ge(slot_full[slot], L * (16 * (a + MOE_TURNS * b)) + i * (16 * b)
                                   + 16 * (a + loads_so_far(MOE_UNITS, MOE_SLOT, name)))

                    def moe_open(*name):
                        n = turn["n"]
                        assert MOE_PRODUCTS[n] == name
                        turn["n"] = n + 1
                        before = MOE_PRODUCTS[n - BANKS]
                        if before[0] == "y":
                            count = [p for p in MOE_PRODUCTS if p[0] == "y"].index(before) + 1
                            pe.wait_ge(sem["y_added"], i * N_Y + count + (N_Y if n >= BANKS else 0))
                        elif before[2] < 2:
                            pe.wait_ge(sem["silu"], i * N_SILU + 2 * before[1] + before[2] + 1)
                        else:
                            pe.wait_ge(sem["hidden"], i * N_SILU + N_SILU + 2 * before[1] + before[2] - 1)
                        return banks[n % BANKS]

                    def moe_used():
                        pe.wait_ge(sem["moe_product"], i * len(MOE_PRODUCTS) + turn["n"])
                        pe.sem_inc(w_used, 1)

                    for pair in range(TURN // 2):
                        for e in (2 * pair, 2 * pair + 1):
                            moe_full(f"gu{e}")
                            w = ring[:, MOE_SLOT[f"gu{e}"], :].rearrange("p (k n) -> p k n", k=K)
                            for f in (0, 2, 1, 3):
                                bank = moe_open("gu", e, f)
                                group(bank, [(w[:, k, f * P:(f + 1) * P], HT[:, k, :]) for k in range(K)])\
                                    .then_inc(sem["moe_product"], 1)
                            moe_used()
                        moe_full(f"dn{pair}")
                        for e in (2 * pair, 2 * pair + 1):
                            w = DN[pair].rearrange("p (e k d) -> p e k d", e=2, k=2)[:, e % 2]
                            pe.wait_ge(sem["hidden"], i * N_SILU + N_SILU + 2 * e + 2)
                            for t in range(T):
                                for n in range(2):
                                    bank = moe_open("y", e, t, n)
                                    group(bank, [(ACTT[:, e % 2, f, t * P:(t + 1) * P], w[:, f, n * 512:(n + 1) * 512])
                                                 for f in range(2)]).then_inc(sem["moe_product"], 1)
                        moe_used()
                pe.sem_inc(sem["layer_end"], 1)
                pe.wait_ge(cleared, L + 1)

        @block.scalar
        def _(act):
            own0 = Own(act, pro_act)
            act.wait_ge(ropes, 1)
            own0.done(nc.scalar.activation(KIN[:, :, 0:96], KIN[:, :, 0:96], ACT.Sin))
            own0.done(nc.scalar.activation(QT[:, :, 0:96], QT[:, :, 0:96], ACT.Sin))
            own0.done(nc.scalar.activation(lb_all, lb_all, ACT.Exp))
            with act.Fori(0, DEPTH) as L:
                own = Own(act, sem["act_own"])
                em = Emptier(act, "act", sem, banks)
                act.dma_start(cols, colparams.rearrange("l p n -> (l p) n")[bass.ds(L * P, P), :]).then_inc(sem["params"], 16)
                act.dma_start(rows, rowparams[bass.ds(L, 1), :].rearrange("l n -> (l n)").partition_broadcast(P))\
                    .then_inc(sem["params"], 16)
                act.dma_start(wr_sb, w_re.rearrange("l (p k) n -> (l p) k n", k=K)[bass.ds(L * P, P), :, :])\
                    .then_inc(sem["params"], 16)
                act.dma_start(MEMX, mem.rearrange("b (m p) d -> p (b m) d", p=P)).then_inc(sem["mem_in"], 16)
                act.wait_ge(consts_in, 6 * 16)
                act.preload_act_table_set("natural_log_exp_and_others")

                def squares(src, scale, dst, junk):
                    own.need()
                    own.done(nc.scalar.activation(junk, src, ACT.Square, scale=scale, accum_out=dst))

                def reciprocal_norm(ss, rn, signal):
                    own.need()
                    own.done(nc.scalar.activation(rn, ss, ACT.Ln, bias=EPS))
                    own.need()
                    nc.scalar.activation(rn, rn, ACT.Exp, scale=-0.5).then_inc(sem[signal], 1)

                def head_norms(src, slot, signal):
                    for h in range(HEADS):
                        squares(src[:, h * P:(h + 1) * P], SCALE, ss_h[:, slot, h:h + 1], JUNK[:, 0:P])
                    reciprocal_norm(ss_h[:, slot, :], rn_h[:, slot, :], signal)

                def token_norms():
                    def tile(t):
                        squares(X[:, t, :], D_MODEL ** -0.5, ss_x[:, t:t + 1], CB[:, 0:1024])
                        reciprocal_norm(ss_x[:, t:t + 1], rn_x[:, t:t + 1], "rn_x")
                    return tile

                def transposed_tokens(key, gain):
                    for k in range(0, K, 2):
                        bank = em.take(key, k)
                        em.empty(nc.scalar.activation(HT[:, k, :], bank, ACT.Identity, scale=cols[:, gain + k:gain + k + 1]),
                                 key, k)

                def copy(dst, bank, *name, scale=None):
                    ins = nc.scalar.activation(dst, bank, ACT.Copy) if scale is None else \
                        nc.scalar.activation(dst, bank, ACT.Identity, scale=scale)
                    em.empty(ins, *name)

                def heads_of(bank):
                    return bank.rearrange("p (h t) -> p h t", h=HEADS)

                norm_tile = token_norms()
                for t in range(T):
                    norm_tile(t)
                act.wait_ge(sem["mem_in"], 16)
                for m in range(M):
                    squares(MEMX[:, m, :], D_MODEL ** -0.5, ss_m[:, m:m + 1], CB[:, 0:1024])
                    reciprocal_norm(ss_m[:, m:m + 1], rn_m[:, m:m + 1], "rn_mem")
                act.wait_ge(sem["params"], 48)
                transposed_tokens("hT", G_MIX)
                act.wait_ge(sem["rn_mem"], M)
                for t in range(T):
                    bank = em.take("ql", t)
                    own.done(nc.scalar.activation(C[:, t, :], bank[:, 0:Q_LORA], ACT.Copy))
                    copy(KI[:, t, :], bank[:, Q_LORA:N_QL], "ql", t)
                    squares(C[:, t, :], Q_LORA ** -0.5, ss_ql[:, t, 0:1], JUNK[:, 0:Q_LORA])
                    act.wait_ge(sem["act_emptied"], em.count)
                    squares(KI[:, t, 0:IDX_DIM], IDX_DIM ** -0.5, ss_ql[:, t, 1:2], JUNK[:, 0:IDX_DIM])
                    reciprocal_norm(ss_ql[:, t, :], rn_ql[:, t, :], "rn_ql")
                for j in range(K // 2):
                    bank = em.take("mT", j)
                    own.done(nc.scalar.activation(MT[:, 2 * j, :], bank[:, 0:N_MEM], ACT.Identity,
                                                  scale=cols[:, G_MEM + 2 * j:G_MEM + 2 * j + 1]))
                    copy(MT[:, 2 * j + 1, :], bank[:, N_MEM:2 * N_MEM], "mT", j,
                         scale=cols[:, G_MEM + 2 * j + 1:G_MEM + 2 * j + 2])

                def head_tile(key, t, slot):
                    bank = em.take(key, t)
                    copy(TOK[:, slot, :], bank, key, t)
                    act.wait_ge(sem["act_emptied"], em.count)
                    head_norms(TOK[:, slot, :], slot, "rn_" + key)
                for m in range(M):
                    head_tile("kx", m, m)
                for c in range(2):
                    copy(CT[:, c, :], em.take("cT", c), "cT", c, scale=cols[:, G_QLAT + c:G_QLAT + c + 1])
                copy(KIT, em.take("kiT"), "kiT")
                for t in LATER:
                    for n in range(2):
                        copy(QI[:, t - 1, n * 512:(n + 1) * 512], em.take("qi", t, n), "qi", t, n)
                for m in range(M):
                    copy(VX[:, m, :], em.take("vx", m), "vx", m)
                for m in range(M):
                    copy(KXT[:, :, m * P:(m + 1) * P], heads_of(em.take("kxT", m)), "kxT", m,
                         scale=cols[:, G_XK:G_XK + 1])
                for key, dst in (("kb", KT), ("qb", QT)):
                    for t in range(T + 1):
                        if t < T:
                            head_tile(key, t, t % 2)
                        if t:
                            copy(dst[:, :, (t - 1) * P:t * P], heads_of(em.take(key + "T", t - 1)), key + "T", t - 1)
                for t in LATER:
                    for n in range(2):
                        copy(QIT[:, t - 1, 4 * n:4 * n + 4, :],
                             em.take("qiT", t, n).rearrange("p (g t) -> p g t", g=4), "qiT", t, n)
                for t in LATER:
                    for h in range(IDX_HEADS):
                        n = (t - 1) * IDX_HEADS + h
                        bank = em.take("si", t, h)
                        if n >= 2:
                            act.wait_ge(sem["relu_used"], n - 1)
                        em.empty(nc.scalar.activation(RELU[:, n % 2, 0:(t + 1) * P], bank[:, 0:(t + 1) * P], ACT.Relu),
                                 "si", t, h)
                for key, dst in (("vb", VBt), ("vA", VAt)):
                    for t in range(T):
                        copy(dst[:, t, :], em.take(key, t), key, t)

                act.wait_ge(sem["lb_ready"], 1)

                def forget(h):
                    bank = em.take("f", h)
                    if h:
                        act.wait_ge(sem["b_ready"], h)
                    em.empty(nc.scalar.activation(E1, bank, ACT.Exp, scale=-1.0), "f", h)
                    act.wait_ge(sem["act_emptied"], em.count)
                    own.done(nc.scalar.activation(L1, E1, ACT.Ln, bias=1.0))
                    own.done(nc.scalar.activation(L2, E1, ACT.Ln, bias=1.0, scale=lb[:, h:h + 1]))
                    own.need()
                    nc.scalar.activation(S1, L1, ACT.Exp, scale=-1.0).then_inc(sem["forget"], 1)

                def queries(h):
                    bank = em.take("q", h)
                    if h:
                        act.wait_ge(sem["kd_ready"], h)
                    own.done(nc.scalar.activation(EQ, bank, ACT.Exp, scale=-1.0))
                    own.need()
                    own.done(nc.scalar.activation(EQ, EQ, ACT.Ln, bias=1.0))
                    own.need()
                    nc.scalar.activation(EQ, EQ, ACT.Exp, scale=-1.0).then_inc(sem["queries"], 1)
                forget(0)
                queries(0)
                for t in range(T):
                    bank = em.take("g", t)
                    if t:
                        act.wait_ge(sem["g_ready"], t)
                    own.done(nc.scalar.activation(XX, bank, ACT.Exp, scale=-1.0))
                    copy(G[:, t, :], bank, "g", t)
                    own.need()
                    own.done(nc.scalar.activation(XX, XX, ACT.Ln, bias=1.0))
                    own.need()
                    nc.scalar.activation(XX, XX, ACT.Exp, scale=-1.0).then_inc(sem["sigma_g"], 1)
                for h in range(HEADS):
                    for n, half in enumerate(HALVES):
                        d = (DE, EQ)[n % 2].rearrange("p (b two i) -> p b two i", two=2, i=half)
                        act.wait_ge(sem["diff"], h * (LEVELS + 1) + n + 1)
                        own.done(nc.scalar.activation(d[:, :, 0, :], d[:, :, 0, :], ACT.Exp, scale=-1.0))
                        nc.scalar.activation(d[:, :, 1, :], d[:, :, 1, :], ACT.Exp).then_inc(sem["decay"], 1)
                    act.wait_ge(sem["diff"], (h + 1) * (LEVELS + 1))
                    act.wait_ge(sem["kL"], (h + 1) * LEVELS)
                    act.wait_ge(sem["qL"], (h + 1) * LEVELS)
                    own.done(nc.scalar.activation(DE, BB, ACT.Exp))
                    own.done(nc.scalar.activation(e_end, BB.rearrange("p (t i) -> p t i", t=T)[:, :, P - 1], ACT.Exp))
                    nc.scalar.activation(EQ, EQ, ACT.Exp, scale=-1.0).then_inc(sem["ends"], 1)
                    if h + 1 < HEADS:
                        forget(h + 1)
                        queries(h + 1)
                    copy(KDT, em.take("kdT", h), "kdT", h)
                    copy(O[:, :, h * P:(h + 1) * P], em.take("o", h).rearrange("p (t n) -> p t n", t=T), "o", h)
                act.wait_ge(sem["act_emptied"], em.count)
                for t in range(T):
                    if t >= 2:
                        act.wait_ge(sem["og_ready"], t - 1)
                    head_norms(O[:, t, :], t % 2, "rn_o")
                for t in range(T):
                    copy(OAB[:, 0:HEADS, t * P:(t + 1) * P], heads_of(em.take("oaT", t)), "oaT", t,
                         scale=cols[:, G_AG:G_AG + 1])

                for m in range(T * HEADS + 1):
                    w = (m // HEADS + 1) * P
                    if m < T * HEADS:
                        act.wait_ge(sem["logits"], m + 1)
                        nc.scalar.activation(PR[:, m % 2, 0:w], PR[:, m % 2, 0:w], ACT.Exp, bias=mx[:, m % 4, 0:1],
                                             accum_out=sm[:, m % 4, 0:1]).then_inc(sem["exps"], 1)
                    if m:
                        w = ((m - 1) // HEADS + 1) * P
                        copy(PT[:, (m - 1) % 2, 0:w], em.take("pT", m - 1)[:, 0:w], "pT", m - 1)
                act.wait_ge(sem["act_emptied"], em.count)

                for t in range(T):
                    emptied(act, sem, "xo", t, 1)
                    if t == 0:
                        act.wait_ge(sem["dve_emptied"], EMPTIED["dve"].index(("pv", T * HEADS - 1)) + 1)
                    norm_tile(t)
                transposed_tokens("hxT", G_X)
                for t in range(T + 1):
                    if t < T:
                        head_tile("qx", t, t % 2)
                    if t:
                        copy(QT[:, :, (t - 1) * P:t * P], heads_of(em.take("qxT", t - 1)), "qxT", t - 1,
                             scale=cols[:, G_XQ:G_XQ + 1])
                px = 0
                for m in range(2 * T):
                    act.wait_ge(sem["max_x"], m + 1)
                    bank = em.take("lx", m)
                    if m >= 2:
                        em.take("pxT", m - 2)
                    for a in range(2):
                        s = slice(a * N_MEM, (a + 1) * N_MEM)
                        ins = nc.scalar.activation(PR[:, m % 2, s], bank[:, s], ACT.Exp, bias=mx[:, m % 4, a:a + 1],
                                                   scale=SCALE, accum_out=sm[:, m % 4, a:a + 1])
                        if a:
                            em.empty(ins, "lx", m)
                        else:
                            own.done(ins)
                    if m >= 4 and m % 2 == 0:
                        copy(OXT[:, :, px * P:(px + 1) * P], heads_of(em.take("px", px)), "px", px)
                        px += 1
                while px < T:
                    copy(OXT[:, :, px * P:(px + 1) * P], heads_of(em.take("px", px)), "px", px)
                    px += 1
                act.wait_ge(sem["act_emptied"], em.count)

                for t in range(T):
                    emptied(act, sem, "xx", t, 1)
                    norm_tile(t)
                transposed_tokens("hfT", G_FFN)
                act.wait_ge(sem["router_logits"], 1)
                nc.scalar.activation(rw[:, 1], rw[:, 1], ACT.Exp).then_inc(sem["router_exp"], 1)
                act.wait_ge(sem["router_logits"], 2)
                nc.scalar.activation(rw[:, 8, :, 0], rw[:, 8, :, 0], ACT.Exp).then_inc(sem["router_exp"], 1)
                assert em.count == len(EMPTIED["act"])
                act.wait_ge(sem["router_exp"], 2)

                with act.Fori(0, MOE_TURNS) as i:
                    for e in range(TURN):
                        for f in range(2):
                            j = 2 * e + f
                            n = MOE_PRODUCTS.index(("gu", e, f))
                            act.wait_ge(sem["moe_product"], i * len(MOE_PRODUCTS) + n + 1)
                            act.wait_ge(sem["hidden"], i * N_SILU + N_SILU + j - 1)
                            nc.scalar.activation(SILU[:, j % 2, :], banks[n % BANKS], ACT.Silu).then_inc(sem["silu"], 1)
                act.wait_ge(sem["silu"], MOE_TURNS * N_SILU)
                act.sem_inc(sem["layer_end"], 1)
                act.wait_ge(cleared, L + 1)

        @block.gpsimd
        def _(pool):
            with pool.Fori(0, DEPTH) as L:
                own = Own(pool, sem["pool_own"])
                pool.wait_ge(prologue, 1)
                for t in LATER:
                    emptied(pool, sem, "qi", t, 1)
                    q = QI[:, t - 1, :].rearrange("p (h two i) -> p h two i", h=IDX_HEADS, two=2)
                    r = PTMP.rearrange("p (h two i) -> p h two i", h=IDX_HEADS, two=2)
                    if t == LATER[0]:
                        pool.wait_ge(sem["mem_scaled"], M)
                    own.need() if own.count else None
                    for a in range(2):
                        own.done(nc.gpsimd.tensor_tensor(r[:, :, a, :], q[:, :, 1 - a, :],
                                                         over(sin_i[:, t, a, :], IDX_HEADS), ALU.mult))
                    own.need()
                    for a in range(2):
                        own.done(nc.gpsimd.tensor_tensor(q[:, :, a, :], q[:, :, a, :],
                                                         over(cos_i[:, t, :], IDX_HEADS), ALU.mult))
                    own.need()
                    nc.gpsimd.tensor_tensor(QI[:, t - 1, :], QI[:, t - 1, :], PTMP, ALU.add).then_inc(sem["qi_ready"], 1)
                    pool.wait_ge(sem["qi_ready"], t)
                for t in range(T):
                    pool.wait_ge(sem["sigma_g"], t + 1)
                    emptied(pool, sem, "g", t)
                    nc.gpsimd.tensor_tensor(G[:, t, :], G[:, t, :], XX, ALU.mult).then_inc(sem["g_ready"], 1)
                for h in range(HEADS):
                    for n, half in enumerate(HALVES):
                        v = [a.rearrange("p (b two i) -> p b two i", two=2, i=half)[:, :, 0, :] for a in (KL, KK, (DE, EQ)[n % 2])]
                        pool.wait_ge(sem["decay"], h * LEVELS + n + 1)
                        pool.wait_ge(sem["b_ready"], h + 1)
                        if n:
                            pool.wait_ge(sem["product"], PRODUCTS.index(("lv", h, n - 1)) + 1)
                        elif h:
                            pool.wait_ge(sem["product"], PRODUCTS.index(("kdT", h - 1)) + 1)
                        if h * LEVELS + n:
                            pool.wait_ge(sem["kL"], h * LEVELS + n)
                        else:
                            pool.wait_ge(sem["levels_zero"], 1)
                        nc.gpsimd.tensor_tensor(v[0], v[1], v[2], ALU.mult).then_inc(sem["kL"], 1)
                    pool.wait_ge(sem["ends"], h + 1)
                    pool.wait_ge(sem["product"], PRODUCTS.index(("lv", h, LEVELS - 1)) + 1)
                    pool.wait_ge(sem["kL"], (h + 1) * LEVELS)
                    nc.gpsimd.tensor_tensor(KL, KK, EQ, ALU.mult).then_inc(sem["kd_ready"], 1)
                    pool.wait_ge(sem["kd_ready"], h + 1)
                pool.wait_ge(sem["layer_end"], 3)
                for name in SIGNALS:
                    pool.sem_clear(sem[name])
                pool.sem_inc(cleared, 1)

        @block.vector
        def _(dve):
            pi, two_pi = float(np.float32(3.1415925)), 2 * np.pi
            c1 = 6.28125
            c2 = float(np.float32(two_pi - c1))
            c3 = float(two_pi - c1 - c2)
            magic = 12582912.0
            own0 = Own(dve, prologue_own)
            dve.wait_ge(consts_in, 6 * 16)
            posf, ang, rounds, sine, cosine = rn_x, QT[:, :, 0:96], KT[:, :, 0:96], KIN[:, :, 0:96], QT[:, :, 0:96]

            def step(ins):
                own0.done(ins)
                own0.need()
            step(nc.vector.tensor_copy(posf, pos))
            for t in range(T):
                step(nc.vector.tensor_scalar(ang[:, t, :], ROT[:, 0:96], posf[:, t:t + 1], None, ALU.mult))
            step(nc.vector.tensor_scalar(rounds, ang, 1 / two_pi, magic, ALU.mult, ALU.add))
            step(nc.vector.tensor_scalar(rounds, rounds, magic, None, ALU.subtract))
            for c in (c1, c2, c3):
                step(nc.vector.scalar_tensor_tensor(ang, rounds, -c, ang, ALU.mult, ALU.add))
            step(nc.vector.tensor_scalar(sine, ang, pi, -pi, ALU.min, ALU.max))
            step(nc.vector.tensor_scalar(ang, ang, pi / 2, None, ALU.add))
            step(nc.vector.tensor_scalar(rounds, ang, pi, -two_pi, ALU.is_gt, ALU.mult))
            step(nc.vector.tensor_tensor(ang, ang, rounds, ALU.add))
            step(nc.vector.tensor_scalar(ang, ang, pi, -pi, ALU.min, ALU.max))
            peak = small[:, 248:248 + HEADS]
            step(nc.vector.tensor_copy(peak, lb_all[:, 0, :]))
            for l in range(1, DEPTH):
                step(nc.vector.tensor_tensor(peak, peak, lb_all[:, l, :], ALU.max))
            own0.done(nc.vector.tensor_tensor(lb_all, lb_all, over(peak, DEPTH), ALU.subtract))
            own0.need()
            dve.sem_inc(ropes, 1)
            dve.wait_ge(pro_act, 3)
            half_m, half_i = DH // 2, IDX_DIM // 2
            step(nc.vector.tensor_copy(cos_m, cosine[:, :, 0:half_m]))
            step(nc.vector.tensor_copy(cos_i, cosine[:, :, half_m:half_m + half_i]))
            step(nc.vector.tensor_copy(sin_m[:, :, 1, :], sine[:, :, 0:half_m]))
            step(nc.vector.tensor_scalar(sin_m[:, :, 0, :], sine[:, :, 0:half_m], -1.0, None, ALU.mult))
            step(nc.vector.tensor_copy(sin_i[:, :, 1, :], sine[:, :, half_m:half_m + half_i]))
            step(nc.vector.tensor_scalar(sin_i[:, :, 0, :], sine[:, :, half_m:half_m + half_i], -1.0, None, ALU.mult))
            total = small[:, 252:252 + HEADS]
            step(nc.vector.tensor_copy(total, lb_all[:, 0, :]))
            for l in range(1, DEPTH):
                step(nc.vector.tensor_tensor(total, total, lb_all[:, l, :], ALU.add))
            step(nc.vector.reciprocal(total, total))
            step(nc.vector.memset(lb_all[:, 0, :], 0.0))
            for l in range(1, DEPTH):
                step(nc.vector.tensor_tensor(lb_all[:, l, :], lb_all[:, l, :], lb_all[:, l - 1, :], ALU.add))
            step(nc.vector.tensor_tensor(lb_all, lb_all, over(total, DEPTH), ALU.mult))
            step(nc.vector.tensor_copy(mask, masks_in))
            step(nc.vector.memset(ones, 1.0))
            step(nc.vector.memset(bias0, 0.0))
            step(nc.vector.memset(bias0[0:CHUNK, CHUNK:P], REFUSED))
            dve.sem_inc(prologue, 1)

            with dve.Fori(0, DEPTH) as L:
                own = Own(dve, sem["dve_own"])
                em = Emptier(dve, "dve", sem, banks)
                own.done(nc.vector.tensor_copy(lb, lb_all.rearrange("p l h -> p (l h)")[:, bass.ds(L * HEADS, HEADS)]))
                own.need()
                nc.vector.tensor_scalar(one_lb, lb, -1.0, 1.0, ALU.mult, ALU.add).then_inc(sem["lb_ready"], 1)

                def scale_tokens(base):
                    for t in range(T):
                        dve.wait_ge(sem["rn_x"], base + t + 1)
                        nc.vector.tensor_scalar(XN[:, t], X[:, t, :].rearrange("p (d k) -> p k d", k=K),
                                                rn_x[:, t:t + 1], None, ALU.mult).then_inc(sem["x_scaled"], 1)

                def transposed_tokens(key, gain):
                    for k in range(1, K, 2):
                        bank = em.take(key, k)
                        em.empty(nc.vector.tensor_scalar(HT[:, k, :], bank, cols[:, gain + k:gain + k + 1], None, ALU.mult),
                                 key, k)
                scale_tokens(0)
                for m in range(M):
                    dve.wait_ge(sem["rn_mem"], m + 1)
                    nc.vector.tensor_scalar(MN[:, m], MEMX[:, m, :].rearrange("p (d k) -> p k d", k=K),
                                            rn_m[:, m:m + 1], None, ALU.mult).then_inc(sem["mem_scaled"], 1)
                dve.wait_ge(sem["params"], 48)
                transposed_tokens("hT", G_MIX)

                rot = ROT
                for t in range(T):
                    dve.wait_ge(sem["rn_ql"], t + 1)
                    nc.vector.tensor_scalar(C[:, t, :], C[:, t, :], rn_ql[:, t, 0:1], None, ALU.mult)\
                        .then_inc(sem["c_ready"], 1)
                for t in range(T):
                    own.done(nc.vector.tensor_scalar(widx[:, t, :], KI[:, t, IDX_DIM:N_KI], W_IDX, None, ALU.mult))
                    ki = KI[:, t, 0:IDX_DIM]
                    own.done(nc.vector.scalar_tensor_tensor(ki, ki, rn_ql[:, t, 1:2], rows[:, R_KI:R_KI + IDX_DIM],
                                                            ALU.mult, ALU.mult))
                    own.need()
                    half = IDX_DIM // 2
                    r = rot[:, 128 * t:128 * t + 128]
                    for a in range(2):
                        own.done(nc.vector.tensor_tensor(r[:, a * half:(a + 1) * half], ki[:, (1 - a) * half:(2 - a) * half],
                                                         sin_i[:, t, a, :], ALU.mult))
                    for a in range(2):
                        own.done(nc.vector.tensor_tensor(r[:, 64 + a * half:64 + (a + 1) * half],
                                                         ki[:, a * half:(a + 1) * half], cos_i[:, t, :], ALU.mult))
                    own.need()
                    nc.vector.tensor_tensor(KIN[:, t, :].rearrange("p (n i) -> p n i", n=2), over(r[:, 64:128], 2),
                                            over(r[:, 0:64], 2), ALU.add).then_inc(sem["ki_ready"], 1)
                for m in range(M):
                    dve.wait_ge(sem["rn_kx"], m + 1)
                    v = TOK[:, m, :].rearrange("p (h d) -> p h d", h=HEADS)
                    nc.vector.tensor_tensor(v, v, each(rn_h[:, m, :], P), ALU.mult).then_inc(sem["kx_ready"], 1)
                for key, gain in (("kb", R_K), ("qb", R_Q)):
                    for t in range(T):
                        s = t % 2
                        dve.wait_ge(sem["rn_" + key], t + 1)
                        for h in range(HEADS):
                            v = TOK[:, s, h * P:(h + 1) * P]
                            own.done(nc.vector.scalar_tensor_tensor(v, v, rn_h[:, s, h:h + 1], rows[:, gain:gain + DH],
                                                                    ALU.mult, ALU.mult))
                        own.need()
                        v = TOK[:, s, :].rearrange("p (h two i) -> p h two i", h=HEADS, two=2)
                        r = rot.rearrange("p (h two i) -> p h two i", h=HEADS, two=2)
                        for a in range(2):
                            own.done(nc.vector.tensor_tensor(r[:, :, a, :], v[:, :, 1 - a, :],
                                                             over(sin_m[:, t, a, :], HEADS), ALU.mult))
                        own.need()
                        vv = TOK[:, s, :].rearrange("p (n i) -> p n i", i=DH // 2)
                        own.done(nc.vector.tensor_tensor(vv, vv, over(cos_m[:, t, :], 2 * HEADS), ALU.mult))
                        own.need()
                        nc.vector.tensor_tensor(TOK[:, s, :], TOK[:, s, :], rot, ALU.add).then_inc(sem[key + "_ready"], 1)
                        dve.wait_ge(sem[key + "_ready"], t + 1)

                for t in LATER:
                    sc = SC[:, t - 1, 0:(t + 1) * P]
                    for h in range(IDX_HEADS):
                        n = (t - 1) * IDX_HEADS + h
                        emptied(dve, sem, "si", t, h)
                        r = RELU[:, n % 2, 0:(t + 1) * P]
                        if h == 0:
                            ins = nc.vector.tensor_scalar(sc, r, widx[:, t, h:h + 1], None, ALU.mult)
                        else:
                            dve.wait_ge(sem["relu_used"], n)
                            ins = nc.vector.scalar_tensor_tensor(sc, r, widx[:, t, h:h + 1], sc, ALU.mult, ALU.add)
                        ins.then_inc(sem["relu_used"], 1)
                    dve.wait_ge(sem["relu_used"], t * IDX_HEADS)
                    last = own.done(nc.vector.memset(sc[0:CHUNK, t * P + CHUNK:(t + 1) * P], REFUSED))
                step_of = {t: last for t in LATER}
                for r in range(TOPK // 8):
                    for t in LATER:
                        own.need(step_of[t])
                        step_of[t] = own.done(nc.vector.max(top8[:, t - 1, :], SC[:, t - 1, 0:(t + 1) * P]))
                    for t in LATER:
                        sc = SC[:, t - 1, 0:(t + 1) * P]
                        own.need(step_of[t])
                        step_of[t] = own.done(nc.vector.match_replace(sc, top8[:, t - 1, :], sc, TAKEN))
                for t in LATER:
                    sc = SC[:, t - 1, 0:(t + 1) * P]
                    own.need(step_of[t])
                    own.done(nc.vector.tensor_scalar(sc, sc, TAKEN / 1.5, REFUSED, ALU.is_ge, ALU.mult))

                nc.vector.memset(CB[:, 1024:2048], 0.0).then_inc(sem["levels_zero"], 1)
                dve.wait_ge(sem["levels_zero"], 1)
                for h in range(HEADS):
                    dve.wait_ge(sem["forget"], h + 1)
                    own.done(nc.vector.tensor_tensor(L2, L2, L1, ALU.subtract))
                    if h:
                        dve.wait_ge(sem["product"], PRODUCTS.index(("lv", h - 1, LEVELS)) + 1)
                        dve.wait_ge(sem["kd_ready"], h)
                    own.done(nc.vector.scalar_tensor_tensor(KK, E1, one_lb[:, h:h + 1], S1, ALU.mult, ALU.mult))
                    own.need(own.count - 1)
                    for t in range(T):
                        s = slice(t * P, (t + 1) * P)
                        own.done(nc.vector.tensor_tensor_scan(BB[:, s], ones, L2[:, s], 0.0, ALU.mult, ALU.add))
                    dve.wait_ge(sem["queries"], h + 1)
                    em.empty(nc.vector.tensor_tensor(QQ, em.take("q", h), EQ, ALU.mult), "q", h)
                    own.need()
                    dve.wait_ge(sem["dve_emptied"], em.count)
                    if h:
                        dve.wait_ge(sem["product"], PRODUCTS.index(("o", h - 1)) + 1)

                    def halves(a, half):
                        return a.rearrange("p (b two i) -> p b two i", two=2, i=half)

                    def diff(n):
                        half = HALVES[n]
                        d = (DE, EQ)[n % 2].rearrange("p (b i) -> p b i", i=2 * half)
                        b = BB.rearrange("p (b i) -> p b i", i=2 * half)
                        ref = b[:, :, half - 1:half].broadcast_to((P, SEQ // (2 * half), 2 * half))
                        return nc.vector.tensor_tensor(d, b, ref, ALU.subtract)

                    def level_queries(n):
                        half = HALVES[n]
                        dve.wait_ge(sem["decay"], h * LEVELS + n + 1)
                        if n:
                            dve.wait_ge(sem["product"], PRODUCTS.index(("lv", h, n - 1)) + 1)
                            dve.wait_ge(sem["qL"], h * LEVELS + n)
                        nc.vector.tensor_tensor(halves(QL, half)[:, :, 1, :], halves(QQ, half)[:, :, 1, :],
                                                halves((DE, EQ)[n % 2], half)[:, :, 1, :], ALU.mult)\
                            .then_inc(sem["qL"], 1)

                    def level_scores(n):
                        bank = em.take("lv", h, n).rearrange("p (t s) -> p t s", t=T)
                        out4 = SCT.rearrange("p (t s) -> p t s", t=T)
                        dve.wait_ge(sem["dve_emptied"], em.count)
                        em.empty(nc.vector.copy_predicated(out4, over(mask[:, n, :], T), bank), "lv", h, n)
                    diff(0).then_inc(sem["b_ready"], 1)
                    dve.wait_ge(sem["b_ready"], h + 1)
                    own.done(nc.vector.memset(SCT, 0.0))
                    own.need()
                    dve.sem_inc(sem["diff"], 1)
                    for n in range(LEVELS):
                        if n + 1 < LEVELS:
                            if n:
                                dve.wait_ge(sem["kL"], h * LEVELS + n)
                                dve.wait_ge(sem["qL"], h * LEVELS + n)
                            diff(n + 1).then_inc(sem["diff"], 1)
                        level_queries(n)
                        if n:
                            level_scores(n - 1)
                    dve.wait_ge(sem["kL"], h * LEVELS + LEVELS - 1)
                    b = BB.rearrange("p (t i) -> p t i", t=T)
                    nc.vector.tensor_tensor(EQ.rearrange("p (t i) -> p t i", t=T), b,
                                            b[:, :, P - 1:P].broadcast_to((P, T, P)), ALU.subtract).then_inc(sem["diff"], 1)
                    level_scores(LEVELS - 1)
                    level_scores(LEVELS)
                    dve.wait_ge(sem["ends"], h + 1)
                    nc.vector.tensor_tensor(QL, QQ, DE, ALU.mult).then_inc(sem["qe_ready"], 1)
                    bank = em.take("dS", h)
                    dve.wait_ge(sem["qe_ready"], h + 1)
                    own.done(nc.vector.tensor_copy(ST[:, 1, :], bank[:, 0:P]))
                    for t in range(1, T - 1):
                        own.need()
                        ins = nc.vector.scalar_tensor_tensor(ST[:, t + 1, :], ST[:, t, :], e_end[:, t:t + 1],
                                                             bank[:, t * P:(t + 1) * P], ALU.mult, ALU.add)
                        if t == T - 2:
                            em.empty(ins, "dS", h)
                        else:
                            own.done(ins)
                for t in range(T):
                    dve.wait_ge(sem["rn_o"], t + 1)
                    dve.wait_ge(sem["g_ready"], t + 1)
                    for h in range(HEADS):
                        s = slice(h * P, (h + 1) * P)
                        ins = nc.vector.scalar_tensor_tensor(O[:, t, s], O[:, t, s], rn_h[:, t % 2, h:h + 1], G[:, t, s],
                                                             ALU.mult, ALU.mult)
                        if h == HEADS - 1:
                            ins.then_inc(sem["og_ready"], 1)
                        else:
                            own.done(ins)

                def masked(m):
                    t, h = divmod(m, HEADS)
                    w = (t + 1) * P
                    bank = em.take("lg", m)
                    if m >= 2:
                        em.take("pT", m - 2)
                    bias = SC[:, t - 1, 0:w] if t else bias0
                    em.empty(nc.vector.scalar_tensor_tensor(PR[:, m % 2, 0:w], bank[:, 0:w], SCALE, bias,
                                                            ALU.mult, ALU.add), "lg", m)
                    dve.wait_ge(sem["dve_emptied"], em.count)
                    nc.vector.tensor_reduce(mx[:, m % 4, 0:1], PR[:, m % 2, 0:w], AX.X, ALU.max, negate=True)\
                        .then_inc(sem["logits"], 1)

                def normalised(m):
                    w = (m // HEADS + 1) * P
                    dve.wait_ge(sem["exps"], m + 1)
                    own.done(nc.vector.reciprocal(sm[:, m % 4, 1:2], sm[:, m % 4, 0:1]))
                    own.need()
                    nc.vector.tensor_scalar(PR[:, m % 2, 0:w], PR[:, m % 2, 0:w], sm[:, m % 4, 1:2], None, ALU.mult)\
                        .then_inc(sem["probs"], 1)

                def attended(m):
                    t, h = divmod(m, HEADS)
                    em.empty(nc.vector.tensor_copy(OAB[:, HEADS + h, t * P:(t + 1) * P], em.take("pv", m)[:, 0:P]), "pv", m)
                dve.wait_ge(sem["og_ready"], T)
                last_m = T * HEADS
                for m in range(last_m + 3):
                    if m < last_m:
                        masked(m)
                    if 0 <= m - 1 < last_m:
                        normalised(m - 1)
                    if m - 3 >= 0:
                        attended(m - 3)

                def add_to_tokens(key):
                    for t in range(T):
                        for n in range(2):
                            s = slice(n * 512, (n + 1) * 512)
                            nc.vector.tensor_tensor(X[:, t, s], X[:, t, s], em.take(key, t, n), ALU.add)\
                                .then_inc(sem["dve_emptied"], 1)
                            assert EMPTIED["dve"][em.count] == (key, t, n)
                            em.count += 1
                add_to_tokens("xo")
                em.take("xo", T - 1, 1)
                scale_tokens(T)
                transposed_tokens("hxT", G_X)

                for t in range(T):
                    dve.wait_ge(sem["rn_qx"], t + 1)
                    v = TOK[:, t % 2, :].rearrange("p (h d) -> p h d", h=HEADS)
                    nc.vector.tensor_tensor(v, v, each(rn_h[:, t % 2, :], P), ALU.mult).then_inc(sem["qx_ready"], 1)

                def peak_x(m):
                    bank = em.take("lx", m).rearrange("p (a s) -> p a s", a=2)
                    own.done(nc.vector.tensor_reduce(mx[:, m % 4, :], bank, AX.X, ALU.max, negate=True))
                    own.need()
                    nc.vector.tensor_scalar(mx[:, m % 4, :], mx[:, m % 4, :], SCALE, None, ALU.mult)\
                        .then_inc(sem["max_x"], 1)

                def normalised_x(m):
                    emptied(dve, sem, "lx", m)
                    own.done(nc.vector.reciprocal(sm[:, m % 4, :], sm[:, m % 4, :]))
                    own.need()
                    v = PR[:, m % 2, :].rearrange("p (a s) -> p a s", a=2)
                    nc.vector.tensor_tensor(v, v, each(sm[:, m % 4, :], N_MEM), ALU.mult).then_inc(sem["probs_x"], 1)

                def transposed_x(m):
                    bank = em.take("pxT", m)
                    if m >= 2 and m % 2 == 0:
                        em.take("px", m // 2 - 1)
                    em.empty(nc.vector.tensor_copy(PT[:, m % 2, :], bank), "pxT", m)
                for m in range(2 * T + 2):
                    if m < 2 * T:
                        peak_x(m)
                    if 0 <= m - 1 < 2 * T:
                        normalised_x(m - 1)
                    if m >= 2:
                        transposed_x(m - 2)
                add_to_tokens("xx")
                scale_tokens(2 * T)
                transposed_tokens("hfT", G_FFN)

                def do(ins):
                    own.done(ins)
                    own.need()
                tt, ts, red = nc.vector.tensor_tensor, nc.vector.tensor_scalar, nc.vector.tensor_reduce
                bank = em.take("rt")
                em.empty(tt(rlog, bank[:, 0:T * N_ROUTE].rearrange("p (t n) -> p t n", t=T),
                            over(rows[:, R_BIAS:N_ROW], T), ALU.add), "rt")
                dve.wait_ge(sem["dve_emptied"], em.count)
                groups = rlog[:, :, 0:N_GROUPS]

                def first_best(scores, best, chosen, free, tmp):
                    do(red(best[:, :, 0:1], scores, AX.X, ALU.max))
                    do(tt(chosen, scores, best[:, :, 0:1].broadcast_to((P, T, 4)), ALU.is_equal))
                    do(ts(free[:, :, 0:1], chosen[:, :, 0:1], -1.0, 1.0, ALU.mult, ALU.add))
                    for g in range(1, 4):
                        do(tt(chosen[:, :, g:g + 1], chosen[:, :, g:g + 1], free[:, :, 0:1], ALU.mult))
                        do(tt(free[:, :, 0:1], free[:, :, 0:1], chosen[:, :, g:g + 1], ALU.subtract))
                first_best(groups, rw[:, 0], rw[:, 2], rw[:, 3], None)
                tt(rw[:, 1], groups, rw[:, 0, :, 0:1].broadcast_to((P, T, 4)), ALU.subtract).then_inc(sem["router_logits"], 1)
                experts = rlog[:, :, N_GROUPS:].rearrange("p t (g e) -> p t g e", g=N_GROUPS)
                do(tt(rw[:, 4], experts[:, :, 0, :], rw[:, 2, :, 0:1].broadcast_to((P, T, 4)), ALU.mult))
                for g in range(1, N_GROUPS):
                    do(tt(rw[:, 5], experts[:, :, g, :], rw[:, 2, :, g:g + 1].broadcast_to((P, T, 4)), ALU.mult))
                    do(tt(rw[:, 4], rw[:, 4], rw[:, 5], ALU.add))
                first_best(rw[:, 4], rw[:, 0], rw[:, 6], rw[:, 3], None)
                do(nc.vector.scalar_tensor_tensor(rw[:, 5], rw[:, 6], REFUSED, rw[:, 4], ALU.mult, ALU.add))
                first_best(rw[:, 5], rw[:, 9], rw[:, 7], rw[:, 3], None)
                tt(rw[:, 8, :, 0:1], rw[:, 9, :, 0:1], rw[:, 0, :, 0:1], ALU.subtract).then_inc(sem["router_logits"], 1)
                dve.wait_ge(sem["router_exp"], 2)
                do(red(rw[:, 10, :, 0:1], rw[:, 1], AX.X, ALU.add))
                do(ts(rw[:, 10, :, 1:2], rw[:, 8, :, 0:1], 1.0, None, ALU.add))
                do(tt(rw[:, 10, :, 0:1], rw[:, 10, :, 0:1], rw[:, 10, :, 1:2], ALU.mult))
                do(nc.vector.reciprocal(rw[:, 10, :, 0:1], rw[:, 10, :, 0:1]))
                do(tt(rw[:, 10, :, 1:2], rw[:, 10, :, 0:1], rw[:, 8, :, 0:1], ALU.mult))
                do(tt(rw[:, 6], rw[:, 6], rw[:, 10, :, 0:1].broadcast_to((P, T, 4)), ALU.mult))
                do(tt(rw[:, 7], rw[:, 7], rw[:, 10, :, 1:2].broadcast_to((P, T, 4)), ALU.mult))
                do(tt(rw[:, 6], rw[:, 6], rw[:, 7], ALU.add))
                for g in range(N_GROUPS):
                    do(tt(gate[:, g * 4:(g + 1) * 4, :].rearrange("p e t -> p t e"), rw[:, 6],
                          rw[:, 2, :, g:g + 1].broadcast_to((P, T, 4)), ALU.mult))
                assert em.count == len(EMPTIED["dve"])

                dve.sem_inc(sem["hidden"], N_SILU)
                dve.sem_inc(sem["y_added"], N_Y)
                with dve.Fori(0, MOE_TURNS) as i:
                    dve.wait_ge(sem["y_added"], i * N_Y + N_Y)
                    nc.vector.tensor_copy(gate_now.rearrange("p e t -> p (e t)"),
                                          gate.rearrange("p e t -> p (e t)")[:, bass.ds(i * (TURN * T), TURN * T)])\
                        .then_inc(sem["turn_gates"], 1)
                    dve.wait_ge(sem["turn_gates"], i + 1)
                    y = 0
                    for pair in range(TURN // 2):
                        for e in (2 * pair, 2 * pair + 1):
                            for f in range(2):
                                j = 2 * e + f
                                n = MOE_PRODUCTS.index(("gu", e, f + 2))
                                dve.wait_ge(sem["silu"], i * N_SILU + j + 1)
                                dve.wait_ge(sem["moe_product"], i * len(MOE_PRODUCTS) + n + 1)
                                nc.vector.tensor_tensor(ACTT[:, e % 2, f, :], SILU[:, j % 2, :], banks[n % BANKS], ALU.mult)\
                                    .then_inc(sem["hidden"], 1)
                        for e in (2 * pair, 2 * pair + 1):
                            for t in range(T):
                                for half in range(2):
                                    n = MOE_PRODUCTS.index(("y", e, t, half))
                                    dve.wait_ge(sem["moe_product"], i * len(MOE_PRODUCTS) + n + 1)
                                    dve.wait_ge(sem["y_added"], i * N_Y + N_Y + y - Y_EXPERT + 1)
                                    xs = X[:, t, half * 512:(half + 1) * 512]
                                    nc.vector.scalar_tensor_tensor(xs, banks[n % BANKS], gate_now[:, e, t:t + 1], xs,
                                                                   ALU.mult, ALU.add).then_inc(sem["y_added"], 1)
                                    y += 1
                dve.wait_ge(sem["y_added"], MOE_TURNS * N_Y + N_Y)
                dve.sem_inc(sem["layer_end"], 1)
                dve.wait_ge(cleared, L + 1)


def kernel(x, mem, positions, norm_mix, w_in, lb_raw, a_gnorm, b_qlat_gain, b_wqb, b_wqidx, b_qnorm, b_knorm,
           b_kidx_norm, w_out, norm_x, norm_mem, x_wq, x_wk, x_wv, x_wo, x_qnorm, x_knorm, norm_ffn, w_rg, b_rg,
           w_re, b_re, w_gu, w_dn):
    import concourse.bacc as bacc
    from concourse.bass_utils import run_bass_kernel_spmd

    a = {k: np.asarray(v) for k, v in locals().items() if k not in ("bacc", "run_bass_kernel_spmd")}
    by_row = lambda v: v.reshape(DEPTH, P, K)
    by_block = lambda v: np.transpose(v.reshape(DEPTH, -1, P), (0, 2, 1))
    col = np.concatenate([by_row(a["norm_mix"]), by_row(a["norm_x"]), by_row(a["norm_mem"]), by_row(a["norm_ffn"]),
                          by_block(a["b_qlat_gain"]), by_block(a["a_gnorm"]), by_block(a["x_qnorm"]),
                          by_block(a["x_knorm"])], axis=2)
    row = np.concatenate([a["b_qnorm"], a["b_knorm"], a["b_kidx_norm"], a["b_rg"], a["b_re"].reshape(DEPTH, -1)], axis=1)
    router = np.concatenate([a["w_rg"], a["w_re"].reshape(DEPTH, D_MODEL, N_EXPERTS)], axis=2)
    lb0 = np.transpose(a["lb_raw"].reshape(DEPTH, HEADS, P), (2, 0, 1))
    freq = np.concatenate([ROPE_THETA ** (-np.arange(0, d, 2) / d) for d in (DH, IDX_DIM)]).astype(np.float32)
    s, t = np.arange(P)[:, None], np.arange(P)[None, :]
    masks = np.stack([(s // (2 * h) == t // (2 * h)) & (s // h < t // h) for h in HALVES] + [s == t], axis=1).astype(np.int32)
    feed = {
        "x": a["x"], "mem": a["mem"], "positions": a["positions"].reshape(T, P).T, "w_in": a["w_in"], "b_wqb": a["b_wqb"],
        "b_wqidx": a["b_wqidx"], "w_out": a["w_out"], "x_wq": a["x_wq"], "x_wk": a["x_wk"], "x_wv": a["x_wv"],
        "x_wo": a["x_wo"], "router": router, "w_gu": a["w_gu"], "w_dn": a["w_dn"], "colparams": col,
        "rowparams": row, "lb_raw": lb0, "freqs": freq, "ident": np.eye(P, dtype=np.float32), "masks": masks,
    }
    feed = {k: np.ascontiguousarray(v) for k, v in feed.items()}
    nc = bacc.Bacc("TRN2", target_bir_lowering=False, num_devices=1)
    ap = {k: nc.dram_tensor("in_" + k, v.shape, mybir.dt.from_np(v.dtype), kind="ExternalInput").ap()
          for k, v in feed.items()}
    out = nc.dram_tensor("out_0", (1, SEQ, D_MODEL), F32, kind="ExternalOutput").ap()
    hybrid_block(nc, ap["x"], ap["mem"], ap["positions"], ap["w_in"], ap["b_wqb"], ap["b_wqidx"], ap["w_out"],
                 ap["x_wq"], ap["x_wk"], ap["x_wv"], ap["x_wo"], None, ap["router"], ap["w_gu"], ap["w_dn"],
                 ap["colparams"], ap["rowparams"], ap["lb_raw"], ap["freqs"], ap["ident"], ap["masks"], out)
    r = run_bass_kernel_spmd(nc, [{"in_" + k: v for k, v in feed.items()}], core_ids=[0])
    return r.results[0]["out_0"]
```

```python
import concourse.bass as bass
from concourse import mybir
from contextlib import ExitStack
import numpy as np

F32 = mybir.dt.float32
I32 = mybir.dt.int32
U8 = mybir.dt.uint8
ALU = mybir.AluOpType
ACT = mybir.ActivationFunctionType
AX = mybir.AxisListType

P = 128
D_MODEL, SEQ, DEPTH = 1024, 512, 2
EPS = 1e-6
ROPE_THETA = 10000.0
HEADS, DH = 4, 128
WIDTH = HEADS * DH
Q_LORA = 256
IDX_HEADS, IDX_DIM = 16, 64
TOPK = min(256, SEQ // 4)
CHUNK = 64
N_MEM = 256
N_GROUPS, EXP_PER_GROUP = 4, 4
N_EXPERTS = N_GROUPS * EXP_PER_GROUP
D_EXPERT = 256
T = SEQ // P
K = D_MODEL // P
M = N_MEM // P
LATER = list(range(1, T))
D_IN = 4 * WIDTH + Q_LORA + 2 * WIDTH + IDX_DIM + IDX_HEADS
C_AQ, C_AF, C_AI, C_AG = (n * WIDTH for n in range(4))
C_QL = 4 * WIDTH
C_BK = C_QL + Q_LORA
C_BV = C_BK + WIDTH
C_KI = C_BV + WIDTH
N_KI = IDX_DIM + IDX_HEADS
N_QL = Q_LORA + N_KI
HALVES = [64, 32, 16, 8, 4, 2, 1]
LEVELS = len(HALVES)
SCALE = DH ** -0.5
W_IDX = IDX_HEADS ** -0.5 * IDX_DIM ** -0.5
REFUSED = -1.0e30
TAKEN = -3.0e38

G_MIX, G_X, G_MEM, G_FFN = (n * K for n in range(4))
G_QLAT = 4 * K
G_AG = G_QLAT + Q_LORA // P
G_XQ = G_AG + 1
G_XK = G_XQ + 1
N_COL = G_XK + 1
R_Q, R_K, R_KI = 0, DH, 2 * DH
R_BIAS = R_KI + IDX_DIM
N_ROUTE = N_GROUPS + N_EXPERTS
N_ROW = R_BIAS + N_ROUTE

UNIT = 4096
RING = 4
UNITS = ["ql", "kx", "vx", "kb", "lora", "vb", "vA", "g", "f", "q", "outA", "outB", "xq", "xo"]
PARTS = {"ql": 2, "lora": 2}
SLOT = {u: n % RING for n, u in enumerate(UNITS)}
TURN = 4
MOE_TURNS = N_EXPERTS // TURN
ACTIVE = 2
OVERFLOW = (ACTIVE * SEQ - 1) // P
MAX_EXTRA = -(-OVERFLOW // TURN)
TILES = N_EXPERTS + MAX_EXTRA * TURN
MOE_UNITS = ["gu0", "gu1", "gu2", "dn0", "gu3", "dn1"]
MOE_SLOT = {"gu0": 2, "gu1": 3, "gu2": 0, "gu3": 1, "dn0": RING, "dn1": RING + 1}
MOE_PARTS = {"dn0": 2, "dn1": 2}
MOE_DONE = {"gu0": 1, "gu1": 2, "gu2": 3, "dn0": 4, "gu3": 5, "dn1": 7}
U_TURN = len(MOE_UNITS)
U_LAYER = len(UNITS) + MOE_TURNS * U_TURN
SLOTS = RING + 2


def slot_loads(slot):
    return (sum(PARTS.get(u, 1) for u in UNITS if SLOT[u] == slot),
            sum(MOE_PARTS.get(u, 1) for u in MOE_UNITS if MOE_SLOT[u] == slot))


def loads_so_far(part, where, name):
    parts = {**PARTS, **MOE_PARTS}
    return sum(parts.get(u, 1) for u in part[:part.index(name) + 1] if where[u] == where[name])


def used_before(name):
    if name in SLOT:
        n = UNITS.index(name)
        earlier = [m for m in range(n) if SLOT[UNITS[m]] == SLOT[name]]
        last = max(MOE_DONE[u] for u in MOE_UNITS if MOE_SLOT[u] == SLOT[name])
        return U_LAYER + (earlier[-1] + 1 if earlier else last - U_TURN)
    earlier = [m for m, u in enumerate(UNITS) if SLOT[u] == MOE_SLOT[name]]
    first = earlier[-1] if earlier else UNITS.index("outB")
    return U_LAYER + max(first + 1, len(UNITS) + MOE_DONE[name] - U_TURN)


TAB_TURNS, TAB_EXTRA = 8, 9
TAB_BEFORE = 10


def products():
    out = [("hT", k) for k in range(K)] + [("ql", t) for t in range(T)]
    out += [("mT", j) for j in range(K // 2)] + [("kx", m) for m in range(M)]
    out += [("cT", c) for c in range(Q_LORA // P)] + [("kiT",)]
    out += [("qi", t, n) for t in LATER for n in range(2)]
    out += [("vx", m) for m in range(M)] + [("kxT", m) for m in range(M)]
    for name in ("kb", "qb"):
        for t in range(T):
            out += [(name, t)] + ([(name + "T", t - 1)] if t else [])
        out += [(name + "T", T - 1)]
    out += [("qiT", t, n) for t in LATER for n in range(2)]
    out += [("si", t, h) for t in LATER for h in range(IDX_HEADS)]
    out += [("vb", t) for t in range(T)] + [("vA", t) for t in range(T)]
    out += [("f", 0), ("q", 0)] + [("g", t) for t in range(T)]
    for h in range(HEADS):
        out += [("lv", h, n) for n in range(LEVELS + 1)]
        if h + 1 < HEADS:
            out += [("f", h + 1), ("q", h + 1)]
        out += [("kdT", h), ("dS", h), ("o", h)]
    out += [("oaT", t) for t in range(T)]
    out += [("lg", m) for m in range(2)]
    for m in range(T * HEADS):
        out += [("pT", m)] + ([("lg", m + 2)] if m + 2 < T * HEADS else []) + ([("pv", m - 1)] if m else [])
    out += [("pv", T * HEADS - 1)]
    out += [("xo", t, n) for t in range(T) for n in range(2)]
    out += [("hxT", k) for k in range(K)]
    for t in range(T):
        out += [("qx", t)] + ([("qxT", t - 1)] if t else [])
    out += [("qxT", T - 1)] + [("lx", m) for m in range(2)]
    for m in range(2 * T):
        out += [("pxT", m)] + ([("lx", m + 2)] if m + 2 < 2 * T else [])
        out += [("px", m // 2 - 1)] if m % 2 == 0 and m else []
    out += [("px", T - 1)]
    out += [("xx", t, n) for t in range(T) for n in range(2)]
    out += [("hfT", k) for k in range(K)] + [("rt",), ("rank",)]
    return out


BANKS = 8
PRODUCTS = products()
ON_VECTOR = ("q", "lv", "dS", "lg", "pv", "xo", "pxT", "xx", "rt", "rank")


def emptied_by(name):
    if name[0] in ("hT", "hxT", "hfT"):
        return ("act", "dve")[name[1] % 2]
    return "dve" if name[0] in ON_VECTOR else "act"


EMPTIED = {e: [p for p in PRODUCTS if emptied_by(p) == e] for e in ("act", "dve")}
for h in range(1, HEADS):
    EMPTIED["dve"].remove(("q", h))
    EMPTIED["dve"].insert(EMPTIED["dve"].index(("dS", h - 1)) + 1, ("q", h))

PER_TILE = 6
D_TILE = 4
A_TILE = 2
A_AHEAD = 4
MOE_D = {"xT0": 0, "xT1": 1, "gu": 3, "hT": 6}

SIGNALS = [
    "params",
    "mem_in",
    "product",
    "act_emptied",
    "dve_emptied",
    "rn_x", "rn_mem", "rn_ql", "rn_kx", "rn_kb", "rn_qb", "rn_o", "rn_qx",
    "x_scaled", "mem_scaled",
    "c_ready", "ki_ready", "kx_ready", "kb_ready", "qb_ready",
    "qi_ready",
    "relu_ready",
    "relu_used",
    "bias_ready",
    "sigma_g", "g_ready",
    "forget", "queries",
    "b_ready",
    "diff", "decay",
    "qL", "kL",
    "ends",
    "kd_ready", "qe_ready",
    "state",
    "og_ready",
    "logits", "exps", "probs",
    "x_mixed",
    "qx_ready", "max_x", "exps_x", "probs_x",
    "x_crossed",
    "router_exp", "router_exp2", "router_logits", "gates",
    "chosen",
    "slots_ready",
    "lb_ready", "levels_zero",
    "moe_loads",
    "moe_product",
    "silu",
    "moe_dve_emptied", "moe_act_emptied",
    "dve_own", "act_own", "pool_own",
    "layer_end",
]


class Own:

    def __init__(self, engine, semaphore):
        self.engine, self.semaphore, self.count = engine, semaphore, 0

    def done(self, instruction):
        self.count += 1
        instruction.then_inc(self.semaphore, 1)
        return self.count

    def need(self, count=None):
        self.engine.wait_ge(self.semaphore, self.count if count is None else count)


class Emptier:

    def __init__(self, engine, key, sem, banks):
        self.engine, self.key, self.sem, self.banks, self.count = engine, key, sem, banks, 0

    def take(self, *name):
        n = PRODUCTS.index(name)
        self.engine.wait_ge(self.sem["product"], n + 1)
        return self.banks[n % BANKS]

    def empty(self, instruction, *name):
        assert EMPTIED[self.key][self.count] == name, (self.key, self.count, EMPTIED[self.key][self.count], name)
        self.count += 1
        instruction.then_inc(self.sem[self.key + "_emptied"], 1)


def emptied(engine, sem, *name):
    key = emptied_by(name)
    engine.wait_ge(sem[key + "_emptied"], EMPTIED[key].index(name) + 1)


def over(ap, n):
    return ap.unsqueeze(1).broadcast_to((ap.shape[0], n, ap.shape[1]))


def each(ap, n):
    return ap.unsqueeze(2).broadcast_to((ap.shape[0], ap.shape[1], n))


def hybrid_block(nc, x, mem, positions, w_in, b_wqb, b_wqidx, w_out, x_wq, x_wk, x_wv, x_wo,
                 w_re, w_gu, w_dn, colparams, rowparams, lb_raw, freqs, ident, masks, zeros, out):
    ctx = ExitStack()
    with ctx:
        def sb(name, shape, dt=F32):
            return ctx.enter_context(nc.sbuf_tensor(name, [P] + shape, dt))[tuple([slice(None)] * (len(shape) + 1))]

        def sem1(name):
            return ctx.enter_context(nc.semaphore(name))

        sem = {name: sem1(name) for name in SIGNALS}
        slot_full = [sem1(f"slot_full{n}") for n in range(SLOTS)]
        w_used = sem1("w_used")
        consts_in = sem1("consts_in")
        ropes = sem1("ropes")
        prologue = sem1("prologue")
        pro_act = sem1("pro_act")
        prologue_own = sem1("prologue_own")
        loads_begun = sem1("loads_begun")
        cleared = sem1("cleared")
        out_done = sem1("out_done")
        table_in = sem1("table_in")
        scattered = sem1("scattered")
        x_in = [sem1(f"x_in{n}") for n in range(TURN)]
        y_out = [sem1(f"y_out{n}") for n in range(2)]
        gathered = [sem1(f"gathered{t}") for t in range(T)]
        zero_tile = sem1("zero_tile")
        zero_filled = sem1("zero_filled")

        XG = nc.dram_tensor("expert_tokens", (TILES * P, D_MODEL), F32, kind="Internal").ap()
        YG = nc.dram_tensor("expert_outputs", (TILES * P, D_MODEL), F32, kind="Internal").ap()

        X = sb("X", [T, D_MODEL])
        HT = sb("HT", [K, SEQ])
        ring = sb("ring", [RING, UNIT])
        XC = sb("XC", [4096])
        CB = sb("CB", [2048])
        AR = sb("AR", [9216])
        QT = sb("QT", [HEADS, SEQ])
        KT = sb("KT", [HEADS, SEQ])
        KIT = sb("KIT", [SEQ])
        SC = sb("SC", [len(LATER), SEQ])
        TOK = sb("TOK", [2, WIDTH])
        ST = sb("ST", [T, DH])
        KXT = sb("KXT", [HEADS, N_MEM])
        VX = sb("VX", [M, WIDTH])
        JUNK = sb("JUNK", [256])
        ROT = sb("ROT", [512])
        idn = sb("idn", [P])
        mask = sb("mask", [LEVELS + 2, P], U8)
        cos_m = sb("cos_m", [T, DH // 2])
        sin_m = sb("sin_m", [T, 2, DH // 2])
        cos_i = sb("cos_i", [T, IDX_DIM // 2])
        sin_i = sb("sin_i", [T, 2, IDX_DIM // 2])
        bias0 = sb("bias0", [P])
        ones = sb("ones", [P])
        rows = sb("rows", [N_ROW])
        cols = sb("cols", [N_COL])
        lb_all = sb("lb_all", [DEPTH, HEADS])
        lb = sb("lb", [HEADS])
        one_lb = sb("one_lb", [HEADS])
        small = sb("small", [256])
        pos = sb("pos", [T], I32)
        table = sb("table", [16], I32)
        slots = sb("slots", [ACTIVE, T], I32)
        masks_in = ring[:, RING - 1, 0:(LEVELS + 2) * P].bitcast(I32).rearrange("p (n s) -> p n s", s=P)

        XN = XC.rearrange("p (t k d) -> p t k d", t=T, k=K)
        QIT = XC[:, 0:3072].rearrange("p (t g d) -> p t g d", t=len(LATER), g=IDX_HEADS // 2)
        OAB = XC.rearrange("p (k t) -> p k t", k=2 * HEADS)
        E1, L1, L2, S1 = (XC[:, 512 * n:512 * n + 512] for n in range(4))
        G = XC[:, 2048:4096].rearrange("p (t n) -> p t n", t=T)
        C = CB[:, 0:1024].rearrange("p (t c) -> p t c", t=T)
        CT = CB[:, 1024:2048].rearrange("p (c t) -> p c t", c=2)
        EQ, DE, QL, KL = (CB[:, 512 * n:512 * n + 512] for n in range(4))
        PR = CB[:, 0:1024].rearrange("p (n s) -> p n s", n=2)
        PT = CB[:, 1024:2048].rearrange("p (n s) -> p n s", n=2)
        AB, OA, VA, VB = AR[:, 0:3072], AR[:, 3072:5120], AR[:, 5120:7168], AR[:, 7168:9216]
        QI = AB.rearrange("p (t n) -> p t n", t=len(LATER))
        RELU = AB[:, 0:1024].rearrange("p (n s) -> p n s", n=2)
        BB, KK, QQ, SCT, KDT, XX = (AB[:, 512 * n:512 * n + 512] for n in range(6))
        MEMX = OA.rearrange("p (m d) -> p m d", m=M)
        MN = VA.rearrange("p (m k d) -> p m k d", m=M, k=K)
        MT = QT.rearrange("p h t -> p (h t)").rearrange("p (k m) -> p k m", k=K)
        PTMP = OA[:, 0:1024]
        O = OA.rearrange("p (t n) -> p t n", t=T)
        VAt = VA.rearrange("p (t n) -> p t n", t=T)
        VBt = VB.rearrange("p (t n) -> p t n", t=T)
        DN = [AR[:, n * UNIT:(n + 1) * UNIT] for n in range(2)]
        XB = XC.rearrange("p (s d) -> p s d", s=4)
        HF = HT.rearrange("p k t -> p (k t)")
        XT = HF[:, 0:2048].rearrange("p (s k t) -> p s k t", s=2, k=K)
        YB = HF[:, 2048:4096].rearrange("p (s d) -> p s d", s=2)
        HID = QT[:, 0, :].rearrange("p (s f) -> p s f", s=2)
        HIDT = QT[:, 1, :].rearrange("p (s f t) -> p s f t", s=2, f=2)
        SILU = KT[:, 0, :].rearrange("p (s f) -> p s f", s=2)
        GOT = [XB, HF.rearrange("p (t d) -> p t d", t=T)]
        OXT = KT

        def take_small(n):
            take_small.at += n
            return small[:, take_small.at - n:take_small.at]
        take_small.at = 0
        ss_x = take_small(T)
        rn_x = take_small(T)
        ss_m = take_small(M)
        rn_m = take_small(M)
        ss_ql = take_small(2 * T).rearrange("p (t n) -> p t n", t=T)
        rn_ql = take_small(2 * T).rearrange("p (t n) -> p t n", t=T)
        ss_h = take_small(2 * HEADS).rearrange("p (t n) -> p t n", t=2)
        rn_h = take_small(2 * HEADS).rearrange("p (t n) -> p t n", t=2)
        widx = take_small(T * IDX_HEADS).rearrange("p (t n) -> p t n", t=T)
        top8 = take_small(8 * len(LATER)).rearrange("p (t n) -> p t n", t=len(LATER))
        e_end = take_small(T)
        mx = take_small(8).rearrange("p (n j) -> p n j", n=4)
        sm = take_small(8).rearrange("p (n j) -> p n j", n=4)
        iota = take_small(N_EXPERTS)
        extra_sum = take_small(1)
        rlog = SC[:, 0, 0:T * N_ROUTE].rearrange("p (t n) -> p t n", t=T)
        rw = SC[:, 1, 0:48 * T].rearrange("p (i t n) -> p i t n", t=T, n=4)
        tri = SC[:, 0, P:2 * P]
        chosen1, chosen2, chosen, rank, base, place = (
            SC[:, 2, 64 * n:64 * n + 64].rearrange("p (t e) -> p t e", t=T) for n in range(6))
        total, over_e, cum, shift = (SC[:, 1, 192 + 16 * n:208 + 16 * n] for n in range(4))
        before_j = SC[:, 1, 256:256 + 8 * N_EXPERTS].rearrange("p (j e) -> p j e", e=N_EXPERTS)
        expert_j, extra, placef = SC[:, 1, 384:392], SC[:, 1, 392:393], SC[:, 1, 400:400 + ACTIVE * T]
        KIN = KIT.rearrange("p (t n) -> p t n", t=T)
        KI = SC[:, 0, 0:T * N_KI].rearrange("p (t n) -> p t n", t=T)
        wr_sb = sb("wr_sb", [K, N_ROUTE])

        banks = [ctx.enter_context(nc.psum_tensor(f"bank{n}", [P, 512], F32))[:, :] for n in range(BANKS)]

        block = ctx.enter_context(nc.Block())

        def weight_view(slot):
            return ring[:, slot, :] if slot < RING else DN[slot - RING]

        @block.sync
        def _(sp):
            sp.dma_start(table, zeros).then_inc(table_in, 16)
            sp.dma_start(X, x.rearrange("b (t p) d -> p (b t) d", p=P)).then_inc(consts_in, 16)
            sp.dma_start(idn, ident).then_inc(consts_in, 16)
            sp.dma_start(pos, positions).then_inc(consts_in, 16)
            sp.dma_start(masks_in, masks).then_inc(consts_in, 16)
            sp.dma_start(ROT[:, 0:DH // 2 + IDX_DIM // 2 + N_EXPERTS], freqs.partition_broadcast(P)).then_inc(consts_in, 16)
            sp.dma_start(lb_all, lb_raw).then_inc(consts_in, 16)

            in_v = w_in.rearrange("l (p k) n -> (l p) k n", k=K)
            qb_v = b_wqb.rearrange("l (k p) n -> l p k n", p=P)
            qi_v = b_wqidx.rearrange("l (k p) n -> l p k n", p=P)
            out_v = w_out.rearrange("l (s k p) n -> (l s) p k n", s=2, p=P)
            xo_v = x_wo.rearrange("l (k p) n -> l p k n", p=P)
            xq_v, xk_v, xv_v = (w.rearrange("l (p k) n -> (l p) (k n)", k=K) for w in (x_wq, x_wk, x_wv))
            gu_v = w_gu.rearrange("l g e (p k) f -> (l g e p) (k f)", k=K)
            dn_v = w_dn.rearrange("l g e (k p) d -> (l g e) p k d", p=P)

            sp.wait_ge(table_in, 16)
            with sp.Fori(0, DEPTH) as L:
                extra_before = sp.value_load(table[0:1, bass.ds(L + TAB_BEFORE, 1)], min_val=0, max_val=DEPTH * MAX_EXTRA)

                def sources(name):
                    rows_l = bass.ds(L * P, P)

                    def cut(a, n):
                        return in_v[rows_l, :, a:a + n]
                    return {
                        "ql": lambda: [(cut(C_QL, Q_LORA), 0, Q_LORA), (cut(C_KI, N_KI), Q_LORA, N_KI)],
                        "kb": lambda: [(cut(C_BK, WIDTH), 0, WIDTH)],
                        "vb": lambda: [(cut(C_BV, WIDTH), 0, WIDTH)],
                        "vA": lambda: [(cut(C_AI, WIDTH), 0, WIDTH)],
                        "g": lambda: [(cut(C_AG, WIDTH), 0, WIDTH)],
                        "f": lambda: [(cut(C_AF, WIDTH), 0, WIDTH)],
                        "q": lambda: [(cut(C_AQ, WIDTH), 0, WIDTH)],
                    }[name]()

                for name in UNITS:
                    slot = SLOT[name]
                    if slot == RING - 1:
                        sp.wait_ge(prologue, 1)
                    sp.wait_ge(w_used, L * U_LAYER + extra_before * U_TURN + used_before(name))
                    sp.sem_inc(loads_begun, 1)
                    w = ring[:, slot, :]
                    full = slot_full[slot]
                    if name in ("kx", "vx", "xq"):
                        src = {"kx": xk_v, "vx": xv_v, "xq": xq_v}[name]
                        sp.dma_start(w, src[bass.ds(L * P, P), :]).then_inc(full, 16)
                    elif name == "lora":
                        sp.dma_start(w[:, 0:1024].rearrange("p (k n) -> p k n", k=2),
                                     qb_v[bass.ds(L, 1), :, :, :].rearrange("l p k n -> (l p) k n")).then_inc(full, 16)
                        sp.dma_start(w[:, 1024:3072].rearrange("p (k n) -> p k n", k=2),
                                     qi_v[bass.ds(L, 1), :, :, :].rearrange("l p k n -> (l p) k n")).then_inc(full, 16)
                    elif name in ("outA", "outB"):
                        src = out_v[bass.ds(L * 2 + (name == "outB"), 1), :, :, :].rearrange("l p k n -> (l p) k n")
                        sp.dma_start(w.rearrange("p (k n) -> p k n", k=4), src).then_inc(full, 16)
                    elif name == "xo":
                        src = xo_v[bass.ds(L, 1), :, :, :].rearrange("l p k n -> (l p) k n")
                        sp.dma_start(w.rearrange("p (k n) -> p k n", k=4), src).then_inc(full, 16)
                    else:
                        width = N_QL if name == "ql" else WIDTH
                        wv = w[:, 0:K * width].rearrange("p (k n) -> p k n", k=K)
                        for src, at, n in sources(name):
                            sp.dma_start(wv[:, :, at:at + n], src).then_inc(full, 16)

                def turn_loads(i, expert):
                    for name in MOE_UNITS:
                        slot, n = MOE_SLOT[name], int(name[2])
                        sp.wait_ge(w_used, L * U_LAYER + extra_before * U_TURN + i * U_TURN + used_before(name))
                        sp.sem_inc(loads_begun, 1)
                        if name[:2] == "gu":
                            sp.dma_start(ring[:, slot, :], gu_v[bass.ds(expert(n) * P, P), :]).then_inc(slot_full[slot], 16)
                        else:
                            for a in range(2):
                                src = dn_v[bass.ds(expert(2 * n + a), 1), :, :, :].rearrange("e p k d -> (e p) k d")
                                dst = DN[slot - RING][:, a * 2048:(a + 1) * 2048].rearrange("p (k d) -> p k d", k=2)
                                sp.dma_start(dst, src).then_inc(slot_full[slot], 16)
                with sp.Fori(0, MOE_TURNS) as i:
                    turn_loads(i, lambda q: L * N_EXPERTS + i * TURN + q)
                sp.wait_ge(sem["slots_ready"], 1)
                extra_turns = sp.value_load(table[0:1, TAB_EXTRA:TAB_EXTRA + 1], min_val=0, max_val=MAX_EXTRA)
                with sp.If(extra_turns > 0):
                    with sp.Fori(0, extra_turns) as j:
                        experts_of = [sp.value_load(table[0:1, bass.ds(j * TURN + q, 1)], min_val=0, max_val=N_EXPERTS - 1)
                                      for q in range(TURN)]
                        turn_loads(j + MOE_TURNS, lambda q: L * N_EXPERTS + experts_of[q])
                sp.sem_inc(sem["layer_end"], 1)
            sp.wait_ge(cleared, DEPTH)
            sp.dma_start(out.rearrange("b (t p) d -> p (b t) d", p=P), X).then_inc(out_done, 16)
            sp.wait_ge(out_done, 16)

        @block.tensor
        def _(pe):
            pe.sem_inc(w_used, U_LAYER)
            pe.wait_ge(consts_in, 6 * 16)
            pe.wait_ge(table_in, 16)
            with pe.Fori(0, DEPTH) as L:
                state = {"n": 0}
                extra_before = pe.value_load(table[0:1, bass.ds(L + TAB_BEFORE, 1)], min_val=0, max_val=DEPTH * MAX_EXTRA)

                def full(name):
                    slot = SLOT[name]
                    a, b = slot_loads(slot)
                    pe.wait_ge(slot_full[slot], L * (16 * (a + MOE_TURNS * b)) + extra_before * (16 * b)
                               + 16 * loads_so_far(UNITS, SLOT, name))
                    return ring[:, slot, :]

                def open_bank(*name):
                    n = state["n"]
                    assert PRODUCTS[n] == name, (PRODUCTS[n], name)
                    state["n"] = n + 1
                    if n >= BANKS:
                        emptied(pe, sem, *PRODUCTS[n - BANKS])
                    return banks[n % BANKS]

                def close(last):
                    last.then_inc(sem["product"], 1)

                def group(bank, pairs):
                    for n, (a, b) in enumerate(pairs):
                        last = nc.tensor.matmul(bank, a, b, start=n == 0, stop=n == len(pairs) - 1)
                    return last

                def transposes(name, tiles, wait=None, used=None):
                    bank = open_bank(*name)
                    for n, tile in enumerate(tiles):
                        last = nc.tensor.transpose(bank[:, n * P:(n + 1) * P], tile, idn)
                    close(last)

                def used():
                    pe.wait_ge(sem["product"], state["n"])
                    pe.sem_inc(w_used, 1)

                def token_product(name, t, w, width, source=HT, steps=K):
                    bank = open_bank(*name)
                    close(group(bank[:, 0:width],
                                [(source[:, k, t * P:(t + 1) * P], w[:, k, :]) for k in range(steps)]))

                def norm_transposes(key, tiles_before):
                    pe.wait_ge(sem["x_scaled"], tiles_before + T)
                    for k in range(K):
                        transposes((key, k), [XN[:, t, k, :] for t in range(T)])

                def all_emptied(key):
                    emptied(pe, sem, key, K - 2)
                    emptied(pe, sem, key, K - 1)

                norm_transposes("hT", 0)
                all_emptied("hT")
                w = full("ql")[:, 0:K * N_QL].rearrange("p (k n) -> p k n", k=K)
                for t in range(T):
                    token_product(("ql", t), t, w, N_QL)
                used()
                pe.wait_ge(sem["mem_scaled"], M)
                for j in range(K // 2):
                    transposes(("mT", j), [MN[:, m, k, :] for k in (2 * j, 2 * j + 1) for m in range(M)])
                emptied(pe, sem, "mT", K // 2 - 1)
                wk = full("kx").rearrange("p (k n) -> p k n", k=K)
                for m in range(M):
                    token_product(("kx", m), m, wk, WIDTH, MT)
                used()
                pe.wait_ge(sem["c_ready"], T)
                for c in range(2):
                    transposes(("cT", c), [C[:, t, c * P:(c + 1) * P] for t in range(T)])
                pe.wait_ge(sem["ki_ready"], T)
                transposes(("kiT",), [KIN[:, t, :] for t in range(T)])
                wl = full("lora")
                wqb = wl[:, 0:1024].rearrange("p (k n) -> p k n", k=2)
                wqi = wl[:, 1024:3072].rearrange("p (k n) -> p k n", k=2)
                emptied(pe, sem, "cT", 1)
                for t in LATER:
                    for n in range(2):
                        token_product(("qi", t, n), t, wqi[:, :, n * 512:(n + 1) * 512], 512, CT, 2)
                wv = full("vx").rearrange("p (k n) -> p k n", k=K)
                for m in range(M):
                    token_product(("vx", m), m, wv, WIDTH, MT)
                used()
                for m in range(M):
                    pe.wait_ge(sem["kx_ready"], m + 1)
                    transposes(("kxT", m), [TOK[:, m, h * P:(h + 1) * P] for h in range(HEADS)])

                def tok_transposes(key, t):
                    pe.wait_ge(sem[key + "_ready"], t + 1)
                    transposes((key + "T", t), [TOK[:, t % 2, h * P:(h + 1) * P] for h in range(HEADS)])
                wkb = full("kb").rearrange("p (k n) -> p k n", k=K)
                for t in range(T):
                    token_product(("kb", t), t, wkb, WIDTH)
                    if t:
                        tok_transposes("kb", t - 1)
                used()
                tok_transposes("kb", T - 1)
                for t in range(T):
                    token_product(("qb", t), t, wqb, WIDTH, CT, 2)
                    if t:
                        tok_transposes("qb", t - 1)
                used()
                tok_transposes("qb", T - 1)
                for t in LATER:
                    pe.wait_ge(sem["qi_ready"], t)
                    for n in range(2):
                        transposes(("qiT", t, n), [QI[:, t - 1, g * P:(g + 1) * P] for g in range(4 * n, 4 * n + 4)])
                emptied(pe, sem, "kiT")
                for t in LATER:
                    for h in range(IDX_HEADS):
                        if h % 8 == 0:
                            emptied(pe, sem, "qiT", t, h // 8)
                        part = slice(64 * (h % 2), 64 * (h % 2) + 64)
                        bank = open_bank("si", t, h)
                        close(nc.tensor.matmul(bank[:, 0:(t + 1) * P], QIT[part, t - 1, h // 2, :],
                                               KIT[part, 0:(t + 1) * P], start=True, stop=True))
                for name, c0 in (("vb", C_BV), ("vA", C_AI)):
                    w = full(name).rearrange("p (k n) -> p k n", k=K)
                    for t in range(T):
                        token_product((name, t), t, w, WIDTH)
                    used()

                wf = full("f").rearrange("p (k n) -> p k n", k=K)
                wq = full("q").rearrange("p (k n) -> p k n", k=K)

                def channel_product(name, w, h):
                    bank = open_bank(name, h)
                    close(group(bank, [(w[:, k, h * P:(h + 1) * P], HT[:, k, :]) for k in range(K)]))
                channel_product("f", wf, 0)
                channel_product("q", wq, 0)
                wg = full("g").rearrange("p (k n) -> p k n", k=K)
                for t in range(T):
                    token_product(("g", t), t, wg, WIDTH)
                used()
                for h in range(HEADS):
                    for n in range(LEVELS + 1):
                        a, b = (KL, QL) if n < LEVELS else (KK, QQ)
                        if n < LEVELS:
                            pe.wait_ge(sem["qL"], h * LEVELS + n + 1)
                            pe.wait_ge(sem["kL"], h * LEVELS + n + 1)
                        bank = open_bank("lv", h, n)
                        for t in range(T):
                            s = slice(t * P, (t + 1) * P)
                            last = nc.tensor.matmul(bank[:, s], a[:, s], b[:, s], start=True, stop=True)
                        close(last)
                    if h + 1 < HEADS:
                        channel_product("f", wf, h + 1)
                        channel_product("q", wq, h + 1)
                    pe.wait_ge(sem["kd_ready"], h + 1)
                    transposes(("kdT", h), [KL[:, t * P:(t + 1) * P] for t in range(T)])
                    emptied(pe, sem, "kdT", h)
                    bank = open_bank("dS", h)
                    values = [VAt[:, t, h * P:(h + 1) * P] for t in range(T)]
                    for t in range(T - 1):
                        last = nc.tensor.matmul(bank[:, t * P:(t + 1) * P], KDT[:, t * P:(t + 1) * P], values[t],
                                                start=True, stop=True)
                    close(last)
                    bank = open_bank("o", h)
                    pe.wait_ge(sem["qe_ready"], h + 1)
                    emptied(pe, sem, "dS", h)
                    for t in range(T):
                        s = slice(t * P, (t + 1) * P)
                        last = nc.tensor.matmul(bank[:, s], SCT[:, s], values[t], start=True, stop=t == 0)
                        if t:
                            last = nc.tensor.matmul(bank[:, s], QL[:, s], ST[:, t, :], start=False, stop=True)
                    close(last)
                pe.wait_ge(sem["product"], state["n"])
                pe.sem_inc(w_used, 2)
                for t in range(T):
                    pe.wait_ge(sem["og_ready"], t + 1)
                    transposes(("oaT", t), [O[:, t, h * P:(h + 1) * P] for h in range(HEADS)])

                def logits(m):
                    t, h = divmod(m, HEADS)
                    bank = open_bank("lg", m)
                    close(nc.tensor.matmul(bank[:, 0:(t + 1) * P], QT[:, h, t * P:(t + 1) * P],
                                           KT[:, h, 0:(t + 1) * P], start=True, stop=True))

                def attend(m):
                    t, h = divmod(m, HEADS)
                    bank = open_bank("pv", m)
                    emptied(pe, sem, "pT", m)
                    close(group(bank[:, 0:P], [(VBt[:, s, h * P:(h + 1) * P], PT[:, m % 2, s * P:(s + 1) * P])
                                               for s in range(t + 1)]))
                logits(0)
                logits(1)
                for m in range(T * HEADS):
                    pe.wait_ge(sem["probs"], m + 1)
                    transposes(("pT", m), [PR[:, m % 2, s * P:(s + 1) * P] for s in range(m // HEADS + 1)])
                    if m + 2 < T * HEADS:
                        logits(m + 2)
                    if m:
                        attend(m - 1)
                attend(T * HEADS - 1)

                wa = full("outA").rearrange("p (k n) -> p k n", k=4)
                wb = full("outB").rearrange("p (k n) -> p k n", k=4)
                emptied(pe, sem, "oaT", T - 1)
                emptied(pe, sem, "pv", T * HEADS - 1)
                for t in range(T):
                    for n in range(2):
                        bank = open_bank("xo", t, n)
                        close(group(bank, [(OAB[:, k, t * P:(t + 1) * P],
                                            (wa, wb)[k // 4][:, k % 4, n * 512:(n + 1) * 512]) for k in range(K)]))
                pe.wait_ge(sem["product"], state["n"])
                pe.sem_inc(w_used, 2)

                norm_transposes("hxT", T)
                all_emptied("hxT")
                w = full("xq").rearrange("p (k n) -> p k n", k=K)

                def qx_transposes(t):
                    pe.wait_ge(sem["qx_ready"], t + 1)
                    transposes(("qxT", t), [TOK[:, t % 2, h * P:(h + 1) * P] for h in range(HEADS)])
                for t in range(T):
                    token_product(("qx", t), t, w, WIDTH)
                    if t:
                        qx_transposes(t - 1)
                used()
                qx_transposes(T - 1)

                def logits_x(m):
                    t, j = divmod(m, 2)
                    emptied(pe, sem, "qxT", t)
                    bank = open_bank("lx", m)
                    for a in range(2):
                        h = 2 * j + a
                        last = nc.tensor.matmul(bank[:, a * N_MEM:(a + 1) * N_MEM], QT[:, h, t * P:(t + 1) * P],
                                                KXT[:, h, :], start=True, stop=True)
                    close(last)

                def attend_x(t):
                    emptied(pe, sem, "pxT", 2 * t + 1)
                    bank = open_bank("px", t)
                    for h in range(HEADS):
                        j, a = divmod(h, 2)
                        last = group(bank[:, h * P:(h + 1) * P],
                                     [(VX[:, m, h * P:(h + 1) * P], PT[:, j, (2 * a + m) * P:(2 * a + m + 1) * P])
                                      for m in range(M)])
                    close(last)
                logits_x(0)
                logits_x(1)
                for m in range(2 * T):
                    pe.wait_ge(sem["probs_x"], m + 1)
                    transposes(("pxT", m), [PR[:, m % 2, s * P:(s + 1) * P] for s in range(4)])
                    if m + 2 < 2 * T:
                        logits_x(m + 2)
                    if m and m % 2 == 0:
                        attend_x(m // 2 - 1)
                attend_x(T - 1)
                w = full("xo").rearrange("p (k n) -> p k n", k=4)
                for t in range(T):
                    emptied(pe, sem, "px", t)
                    for n in range(2):
                        bank = open_bank("xx", t, n)
                        close(group(bank, [(OXT[:, h, t * P:(t + 1) * P], w[:, h, n * 512:(n + 1) * 512])
                                           for h in range(HEADS)]))
                used()

                norm_transposes("hfT", 2 * T)
                all_emptied("hfT")
                bank = open_bank("rt")
                for t in range(T):
                    last = group(bank[:, t * N_ROUTE:(t + 1) * N_ROUTE],
                                 [(HT[:, k, t * P:(t + 1) * P], wr_sb[:, k, :]) for k in range(K)])
                close(last)
                pe.wait_ge(sem["chosen"], 1)
                bank = open_bank("rank")
                picks = chosen.rearrange("p t e -> p (t e)")
                nc.tensor.matmul(bank[:, 0:64], tri, picks, start=True, stop=True)
                close(nc.tensor.matmul(bank[:, 64:128], ones, picks, start=True, stop=True))
                assert state["n"] == len(PRODUCTS)
                for name in PRODUCTS[-BANKS:]:
                    emptied(pe, sem, *name)

                pe.wait_ge(sem["slots_ready"], 1)
                more_turns = pe.value_load(table[0:1, TAB_TURNS:TAB_TURNS + 1], min_val=MOE_TURNS - 1,
                                           max_val=MOE_TURNS - 1 + MAX_EXTRA)
                made = sem["moe_product"]

                def moe_full(i, q, kind):
                    name = f"gu{q}" if kind == "gu" else f"dn{q // 2}"
                    slot = MOE_SLOT[name]
                    a, b = slot_loads(slot)
                    pe.wait_ge(slot_full[slot], L * (16 * (a + MOE_TURNS * b)) + extra_before * (16 * b) + i * (16 * b)
                               + 16 * (a + loads_so_far(MOE_UNITS, MOE_SLOT, name)))
                    return ring[:, slot, :] if kind == "gu" else DN[q // 2][:, (q % 2) * 2048:(q % 2 + 1) * 2048]

                def tokens_transposed(i, q, at):
                    pe.wait_ge(x_in[q % TURN], L * (MOE_TURNS * 16) + extra_before * 16 + i * 16 + (q // TURN + 1) * 16)
                    for n in range(2):
                        if q > 1:
                            pe.wait_ge(sem["moe_dve_emptied"], i * (TURN * D_TILE) + D_TILE * (q - 1)
                                       + (MOE_D["hT"] - 2 * D_TILE, MOE_D["gu"] - D_TILE)[n])
                        bank = banks[(at + n) % BANKS]
                        for k in range(4):
                            last = nc.tensor.transpose(bank[:, k * P:(k + 1) * P],
                                                       XB[:, q % TURN, (4 * n + k) * P:(4 * n + k + 1) * P], idn)
                        last.then_inc(made, 1)

                def first_layer(i, q, at):
                    w = moe_full(i, q % TURN, "gu") if q < TURN else moe_full(i + 1, 0, "gu")
                    w = w.rearrange("p (k n) -> p k n", k=K)
                    pe.wait_ge(sem["moe_dve_emptied"], i * (TURN * D_TILE) + (D_TILE * q + MOE_D["xT1"] if q else 2))
                    if q:
                        pe.wait_ge(sem["moe_act_emptied"], i * (TURN * A_TILE) + A_TILE * (q - 2) + A_AHEAD)
                    group(banks[at % BANKS], [(XT[:, q % 2, k, :], w[:, k, :]) for k in range(K)]).then_inc(made, 1)

                def hidden_transposed(i, q, at):
                    pe.wait_ge(sem["moe_dve_emptied"], i * (TURN * D_TILE) + D_TILE * q + MOE_D["gu"])
                    if q:
                        pe.wait_ge(sem["moe_act_emptied"], i * (TURN * A_TILE) + A_TILE * (q - 2) + 1 + A_AHEAD)
                    for f in range(2):
                        last = nc.tensor.transpose(banks[at % BANKS][:, f * P:(f + 1) * P],
                                                   HID[:, q % 2, f * P:(f + 1) * P], idn)
                    last.then_inc(made, 1)

                def second_layer(i, q, at, last_count):
                    w = moe_full(i, q, "dn").rearrange("p (k d) -> p k d", k=2)
                    pe.wait_ge(sem["moe_dve_emptied"], i * (TURN * D_TILE) + last_count)
                    for n in range(2):
                        group(banks[(at + n) % BANKS], [(HIDT[:, q % 2, f, :], w[:, f, n * 512:(n + 1) * 512])
                                                        for f in range(2)]).then_inc(made, 1)

                def unit_used(i, count):
                    pe.wait_ge(made, i * (TURN * PER_TILE) + count)
                    pe.sem_inc(w_used, 1)

                def tile(i, q, last=False):
                    at = PER_TILE * q if q else 2
                    first_layer(i, q, at)
                    if not last:
                        tokens_transposed(i, q + 1, at + 1)
                    unit_used(i, at + 1)
                    y_at = at + 1 if last else at + 3
                    if q:
                        second_layer(i, q - 1, y_at, D_TILE * (q - 1) + MOE_D["hT"])
                    h_at = y_at + 2 if q else 5
                    hidden_transposed(i, q, h_at)
                    if q and q % 2 == 0:
                        unit_used(i, y_at + 2)
                    if last:
                        second_layer(i, q, h_at + 1, D_TILE * q + MOE_D["hT"] - 2)
                        unit_used(i, PER_TILE * TURN)
                tokens_transposed(0, 0, 0)
                tile(0, 0)
                with pe.Fori(0, more_turns) as i:
                    for q in range(1, TURN + 1):
                        tile(i, q)
                for q in range(1, TURN):
                    tile(more_turns, q, last=q == TURN - 1)
                pe.sem_inc(sem["layer_end"], 1)
                pe.wait_ge(cleared, L + 1)

        @block.scalar
        def _(act):
            own0 = Own(act, pro_act)
            act.wait_ge(ropes, 1)
            own0.done(nc.scalar.activation(KIN[:, :, 0:96], KIN[:, :, 0:96], ACT.Sin))
            own0.done(nc.scalar.activation(QT[:, :, 0:96], QT[:, :, 0:96], ACT.Sin))
            own0.done(nc.scalar.activation(lb_all, lb_all, ACT.Exp))
            act.wait_ge(table_in, 16)
            with act.Fori(0, DEPTH) as L:
                extra_before = act.value_load(table[0:1, bass.ds(L + TAB_BEFORE, 1)], min_val=0, max_val=DEPTH * MAX_EXTRA)
                own = Own(act, sem["act_own"])
                em = Emptier(act, "act", sem, banks)
                act.dma_start(cols, colparams.rearrange("l p n -> (l p) n")[bass.ds(L * P, P), :]).then_inc(sem["params"], 16)
                act.dma_start(rows, rowparams[bass.ds(L, 1), :].rearrange("l n -> (l n)").partition_broadcast(P))\
                    .then_inc(sem["params"], 16)
                act.dma_start(wr_sb, w_re.rearrange("l (p k) n -> (l p) k n", k=K)[bass.ds(L * P, P), :, :])\
                    .then_inc(sem["params"], 16)
                act.dma_start(MEMX, mem.rearrange("b (m p) d -> p (b m) d", p=P)).then_inc(sem["mem_in"], 16)
                act.wait_ge(consts_in, 6 * 16)
                act.preload_act_table_set("natural_log_exp_and_others")

                def squares(src, scale, dst, junk):
                    own.need()
                    own.done(nc.scalar.activation(junk, src, ACT.Square, scale=scale, accum_out=dst))

                def reciprocal_norm(ss, rn, signal):
                    own.need()
                    own.done(nc.scalar.activation(rn, ss, ACT.Ln, bias=EPS))
                    own.need()
                    nc.scalar.activation(rn, rn, ACT.Exp, scale=-0.5).then_inc(sem[signal], 1)

                def head_norms(src, slot, signal):
                    for h in range(HEADS):
                        squares(src[:, h * P:(h + 1) * P], SCALE, ss_h[:, slot, h:h + 1], JUNK[:, 0:P])
                    reciprocal_norm(ss_h[:, slot, :], rn_h[:, slot, :], signal)

                def token_norms():
                    def tile(t):
                        squares(X[:, t, :], D_MODEL ** -0.5, ss_x[:, t:t + 1], CB[:, 0:1024])
                        reciprocal_norm(ss_x[:, t:t + 1], rn_x[:, t:t + 1], "rn_x")
                    return tile

                def transposed_tokens(key, gain):
                    for k in range(0, K, 2):
                        bank = em.take(key, k)
                        em.empty(nc.scalar.activation(HT[:, k, :], bank, ACT.Identity, scale=cols[:, gain + k:gain + k + 1]),
                                 key, k)

                def copy(dst, bank, *name, scale=None):
                    ins = nc.scalar.activation(dst, bank, ACT.Copy) if scale is None else \
                        nc.scalar.activation(dst, bank, ACT.Identity, scale=scale)
                    em.empty(ins, *name)

                def heads_of(bank):
                    return bank.rearrange("p (h t) -> p h t", h=HEADS)

                norm_tile = token_norms()
                for t in range(T):
                    norm_tile(t)
                act.wait_ge(sem["mem_in"], 16)
                for m in range(M):
                    squares(MEMX[:, m, :], D_MODEL ** -0.5, ss_m[:, m:m + 1], CB[:, 0:1024])
                    reciprocal_norm(ss_m[:, m:m + 1], rn_m[:, m:m + 1], "rn_mem")
                act.wait_ge(sem["params"], 48)
                transposed_tokens("hT", G_MIX)
                act.wait_ge(sem["rn_mem"], M)
                for t in range(T):
                    bank = em.take("ql", t)
                    own.done(nc.scalar.activation(C[:, t, :], bank[:, 0:Q_LORA], ACT.Copy))
                    copy(KI[:, t, :], bank[:, Q_LORA:N_QL], "ql", t)
                    squares(C[:, t, :], Q_LORA ** -0.5, ss_ql[:, t, 0:1], JUNK[:, 0:Q_LORA])
                    act.wait_ge(sem["act_emptied"], em.count)
                    squares(KI[:, t, 0:IDX_DIM], IDX_DIM ** -0.5, ss_ql[:, t, 1:2], JUNK[:, 0:IDX_DIM])
                    reciprocal_norm(ss_ql[:, t, :], rn_ql[:, t, :], "rn_ql")
                for j in range(K // 2):
                    bank = em.take("mT", j)
                    own.done(nc.scalar.activation(MT[:, 2 * j, :], bank[:, 0:N_MEM], ACT.Identity,
                                                  scale=cols[:, G_MEM + 2 * j:G_MEM + 2 * j + 1]))
                    copy(MT[:, 2 * j + 1, :], bank[:, N_MEM:2 * N_MEM], "mT", j,
                         scale=cols[:, G_MEM + 2 * j + 1:G_MEM + 2 * j + 2])

                def head_tile(key, t, slot):
                    bank = em.take(key, t)
                    copy(TOK[:, slot, :], bank, key, t)
                    act.wait_ge(sem["act_emptied"], em.count)
                    head_norms(TOK[:, slot, :], slot, "rn_" + key)
                for m in range(M):
                    head_tile("kx", m, m)
                for c in range(2):
                    copy(CT[:, c, :], em.take("cT", c), "cT", c, scale=cols[:, G_QLAT + c:G_QLAT + c + 1])
                copy(KIT, em.take("kiT"), "kiT")
                for t in LATER:
                    for n in range(2):
                        copy(QI[:, t - 1, n * 512:(n + 1) * 512], em.take("qi", t, n), "qi", t, n)
                for m in range(M):
                    copy(VX[:, m, :], em.take("vx", m), "vx", m)
                act.wait_ge(zero_filled, 32)
                for m in range(M):
                    copy(KXT[:, :, m * P:(m + 1) * P], heads_of(em.take("kxT", m)), "kxT", m,
                         scale=cols[:, G_XK:G_XK + 1])
                for key, dst in (("kb", KT), ("qb", QT)):
                    for t in range(T + 1):
                        if t < T:
                            head_tile(key, t, t % 2)
                        if t:
                            copy(dst[:, :, (t - 1) * P:t * P], heads_of(em.take(key + "T", t - 1)), key + "T", t - 1)
                for t in LATER:
                    for n in range(2):
                        copy(QIT[:, t - 1, 4 * n:4 * n + 4, :],
                             em.take("qiT", t, n).rearrange("p (g t) -> p g t", g=4), "qiT", t, n)
                for t in LATER:
                    for h in range(IDX_HEADS):
                        n = (t - 1) * IDX_HEADS + h
                        bank = em.take("si", t, h)
                        if n >= 2:
                            act.wait_ge(sem["relu_used"], n - 1)
                        em.empty(nc.scalar.activation(RELU[:, n % 2, 0:(t + 1) * P], bank[:, 0:(t + 1) * P], ACT.Relu),
                                 "si", t, h)
                for key, dst in (("vb", VBt), ("vA", VAt)):
                    for t in range(T):
                        copy(dst[:, t, :], em.take(key, t), key, t)

                act.wait_ge(sem["lb_ready"], 1)

                def forget(h):
                    bank = em.take("f", h)
                    if h:
                        act.wait_ge(sem["b_ready"], h)
                    em.empty(nc.scalar.activation(E1, bank, ACT.Exp, scale=-1.0), "f", h)
                    act.wait_ge(sem["act_emptied"], em.count)
                    own.done(nc.scalar.activation(L1, E1, ACT.Ln, bias=1.0))
                    own.done(nc.scalar.activation(L2, E1, ACT.Ln, bias=1.0, scale=lb[:, h:h + 1]))
                    own.need()
                    nc.scalar.activation(S1, L1, ACT.Exp, scale=-1.0).then_inc(sem["forget"], 1)

                def queries(h):
                    bank = em.take("q", h)
                    if h:
                        act.wait_ge(sem["kd_ready"], h)
                    own.done(nc.scalar.activation(EQ, bank, ACT.Exp, scale=-1.0))
                    own.need()
                    own.done(nc.scalar.activation(EQ, EQ, ACT.Ln, bias=1.0))
                    own.need()
                    nc.scalar.activation(EQ, EQ, ACT.Exp, scale=-1.0).then_inc(sem["queries"], 1)
                forget(0)
                queries(0)
                for t in range(T):
                    bank = em.take("g", t)
                    if t:
                        act.wait_ge(sem["g_ready"], t)
                    own.done(nc.scalar.activation(XX, bank, ACT.Exp, scale=-1.0))
                    copy(G[:, t, :], bank, "g", t)
                    own.need()
                    own.done(nc.scalar.activation(XX, XX, ACT.Ln, bias=1.0))
                    own.need()
                    nc.scalar.activation(XX, XX, ACT.Exp, scale=-1.0).then_inc(sem["sigma_g"], 1)
                for h in range(HEADS):
                    for n, half in enumerate(HALVES):
                        d = (DE, EQ)[n % 2].rearrange("p (b two i) -> p b two i", two=2, i=half)
                        act.wait_ge(sem["diff"], h * (LEVELS + 1) + n + 1)
                        own.done(nc.scalar.activation(d[:, :, 0, :], d[:, :, 0, :], ACT.Exp, scale=-1.0))
                        nc.scalar.activation(d[:, :, 1, :], d[:, :, 1, :], ACT.Exp).then_inc(sem["decay"], 1)
                    act.wait_ge(sem["diff"], (h + 1) * (LEVELS + 1))
                    act.wait_ge(sem["kL"], (h + 1) * LEVELS)
                    act.wait_ge(sem["qL"], (h + 1) * LEVELS)
                    own.done(nc.scalar.activation(DE, BB, ACT.Exp))
                    own.done(nc.scalar.activation(e_end, BB.rearrange("p (t i) -> p t i", t=T)[:, :, P - 1], ACT.Exp))
                    nc.scalar.activation(EQ, EQ, ACT.Exp, scale=-1.0).then_inc(sem["ends"], 1)
                    if h + 1 < HEADS:
                        forget(h + 1)
                        queries(h + 1)
                    copy(KDT, em.take("kdT", h), "kdT", h)
                    copy(O[:, :, h * P:(h + 1) * P], em.take("o", h).rearrange("p (t n) -> p t n", t=T), "o", h)
                act.wait_ge(sem["act_emptied"], em.count)
                for t in range(T):
                    if t >= 2:
                        act.wait_ge(sem["og_ready"], t - 1)
                    head_norms(O[:, t, :], t % 2, "rn_o")
                for t in range(T):
                    copy(OAB[:, 0:HEADS, t * P:(t + 1) * P], heads_of(em.take("oaT", t)), "oaT", t,
                         scale=cols[:, G_AG:G_AG + 1])

                for m in range(T * HEADS + 1):
                    w = (m // HEADS + 1) * P
                    if m < T * HEADS:
                        act.wait_ge(sem["logits"], m + 1)
                        nc.scalar.activation(PR[:, m % 2, 0:w], PR[:, m % 2, 0:w], ACT.Exp, bias=mx[:, m % 4, 0:1],
                                             accum_out=sm[:, m % 4, 0:1]).then_inc(sem["exps"], 1)
                    if m:
                        w = ((m - 1) // HEADS + 1) * P
                        copy(PT[:, (m - 1) % 2, 0:w], em.take("pT", m - 1)[:, 0:w], "pT", m - 1)
                act.wait_ge(sem["act_emptied"], em.count)

                for t in range(T):
                    emptied(act, sem, "xo", t, 1)
                    if t == 0:
                        act.wait_ge(sem["dve_emptied"], EMPTIED["dve"].index(("pv", T * HEADS - 1)) + 1)
                    norm_tile(t)
                transposed_tokens("hxT", G_X)
                for t in range(T + 1):
                    if t < T:
                        head_tile("qx", t, t % 2)
                    if t:
                        copy(QT[:, :, (t - 1) * P:t * P], heads_of(em.take("qxT", t - 1)), "qxT", t - 1,
                             scale=cols[:, G_XQ:G_XQ + 1])
                px = 0
                for m in range(2 * T):
                    act.wait_ge(sem["max_x"], m + 1)
                    bank = em.take("lx", m)
                    if m >= 2:
                        em.take("pxT", m - 2)
                    for a in range(2):
                        s = slice(a * N_MEM, (a + 1) * N_MEM)
                        ins = nc.scalar.activation(PR[:, m % 2, s], bank[:, s], ACT.Exp, bias=mx[:, m % 4, a:a + 1],
                                                   scale=SCALE, accum_out=sm[:, m % 4, a:a + 1])
                        if a:
                            em.empty(ins, "lx", m)
                        else:
                            own.done(ins)
                    if m >= 4 and m % 2 == 0:
                        copy(OXT[:, :, px * P:(px + 1) * P], heads_of(em.take("px", px)), "px", px)
                        px += 1
                while px < T:
                    copy(OXT[:, :, px * P:(px + 1) * P], heads_of(em.take("px", px)), "px", px)
                    px += 1
                act.wait_ge(sem["act_emptied"], em.count)

                for t in range(T):
                    emptied(act, sem, "xx", t, 1)
                    norm_tile(t)
                transposed_tokens("hfT", G_FFN)
                act.wait_ge(sem["router_logits"], 1)
                nc.scalar.activation(rw[:, 1], rw[:, 1], ACT.Exp).then_inc(sem["router_exp"], 1)
                act.wait_ge(sem["router_logits"], 2)
                nc.scalar.activation(rw[:, 8, :, 0], rw[:, 8, :, 0], ACT.Exp).then_inc(sem["router_exp"], 1)
                assert em.count == len(EMPTIED["act"])
                act.wait_ge(sem["router_exp"], 2)

                act.sem_inc(sem["moe_act_emptied"], A_AHEAD)
                act.wait_ge(sem["slots_ready"], 1)
                more_turns = act.value_load(table[0:1, TAB_TURNS:TAB_TURNS + 1], min_val=MOE_TURNS - 1,
                                            max_val=MOE_TURNS - 1 + MAX_EXTRA)

                def silu(i, q):
                    at = PER_TILE * q if q else 2
                    act.wait_ge(sem["moe_product"], i * (TURN * PER_TILE) + at + 1)
                    nc.scalar.activation(SILU[:, q % 2, :], banks[at % BANKS][:, 0:D_EXPERT], ACT.Silu)\
                        .then_inc(sem["silu"], 1)

                def output(i, q, at):
                    act.wait_ge(y_out[q % 2], L * (MOE_TURNS * 32) + extra_before * 32 + i * 32 + q // 2 * 16)
                    for n in range(2):
                        act.wait_ge(sem["moe_product"], i * (TURN * PER_TILE) + at + n + 1)
                        nc.scalar.activation(YB[:, q % 2, n * 512:(n + 1) * 512], banks[(at + n) % BANKS], ACT.Copy)\
                            .then_inc(sem["moe_act_emptied"], 1)
                silu(0, 0)
                with act.Fori(0, more_turns) as i:
                    for q in range(1, TURN + 1):
                        silu(i, q)
                        output(i, q - 1, PER_TILE * q + 3)
                for q in range(1, TURN):
                    silu(more_turns, q)
                    output(more_turns, q - 1, PER_TILE * q + (1 if q == TURN - 1 else 3))
                output(more_turns, TURN - 1, PER_TILE * (TURN - 1) + 4)
                act.wait_ge(sem["moe_act_emptied"], more_turns * (TURN * A_TILE) + TURN * A_TILE + A_AHEAD)
                act.sem_inc(sem["layer_end"], 1)
                act.wait_ge(cleared, L + 1)

        @block.gpsimd
        def _(pool):
            zeros_tile = KXT.rearrange("p h s -> p (h s)")
            nc.gpsimd.memset(zeros_tile, 0.0).then_inc(zero_tile, 1)
            pool.wait_ge(zero_tile, 1)
            pool.dma_start(XG.rearrange("(n p) d -> p n d", p=P), over(zeros_tile, TILES)).then_inc(zero_filled, 16)
            pool.dma_start(YG[N_EXPERTS * P:, :].rearrange("(n p) d -> p n d", p=P), over(zeros_tile, TILES - N_EXPERTS))\
                .then_inc(zero_filled, 16)
            pool.wait_ge(table_in, 16)
            with pool.Fori(0, DEPTH) as L:
                extra_before = pool.value_load(table[0:1, bass.ds(L + TAB_BEFORE, 1)], min_val=0, max_val=DEPTH * MAX_EXTRA)
                own = Own(pool, sem["pool_own"])
                pool.wait_ge(prologue, 1)
                for t in LATER:
                    emptied(pool, sem, "qi", t, 1)
                    q = QI[:, t - 1, :].rearrange("p (h two i) -> p h two i", h=IDX_HEADS, two=2)
                    r = PTMP.rearrange("p (h two i) -> p h two i", h=IDX_HEADS, two=2)
                    if t == LATER[0]:
                        pool.wait_ge(sem["mem_scaled"], M)
                    own.need() if own.count else None
                    for a in range(2):
                        own.done(nc.gpsimd.tensor_tensor(r[:, :, a, :], q[:, :, 1 - a, :],
                                                         over(sin_i[:, t, a, :], IDX_HEADS), ALU.mult))
                    own.need()
                    for a in range(2):
                        own.done(nc.gpsimd.tensor_tensor(q[:, :, a, :], q[:, :, a, :],
                                                         over(cos_i[:, t, :], IDX_HEADS), ALU.mult))
                    own.need()
                    nc.gpsimd.tensor_tensor(QI[:, t - 1, :], QI[:, t - 1, :], PTMP, ALU.add).then_inc(sem["qi_ready"], 1)
                    pool.wait_ge(sem["qi_ready"], t)
                for t in range(T):
                    pool.wait_ge(sem["sigma_g"], t + 1)
                    emptied(pool, sem, "g", t)
                    nc.gpsimd.tensor_tensor(G[:, t, :], G[:, t, :], XX, ALU.mult).then_inc(sem["g_ready"], 1)
                for h in range(HEADS):
                    for n, half in enumerate(HALVES):
                        v = [a.rearrange("p (b two i) -> p b two i", two=2, i=half)[:, :, 0, :] for a in (KL, KK, (DE, EQ)[n % 2])]
                        pool.wait_ge(sem["decay"], h * LEVELS + n + 1)
                        pool.wait_ge(sem["b_ready"], h + 1)
                        if n:
                            pool.wait_ge(sem["product"], PRODUCTS.index(("lv", h, n - 1)) + 1)
                        elif h:
                            pool.wait_ge(sem["product"], PRODUCTS.index(("kdT", h - 1)) + 1)
                        if h * LEVELS + n:
                            pool.wait_ge(sem["kL"], h * LEVELS + n)
                        else:
                            pool.wait_ge(sem["levels_zero"], 1)
                        nc.gpsimd.tensor_tensor(v[0], v[1], v[2], ALU.mult).then_inc(sem["kL"], 1)
                    pool.wait_ge(sem["ends"], h + 1)
                    pool.wait_ge(sem["product"], PRODUCTS.index(("lv", h, LEVELS - 1)) + 1)
                    pool.wait_ge(sem["kL"], (h + 1) * LEVELS)
                    nc.gpsimd.tensor_tensor(KL, KK, EQ, ALU.mult).then_inc(sem["kd_ready"], 1)
                    pool.wait_ge(sem["kd_ready"], h + 1)
                pool.wait_ge(sem["slots_ready"], 1)
                pool.wait_ge(zero_filled, 32)
                for n in range(ACTIVE):
                    for t in range(T):
                        nc.gpsimd.indirect_dma_start(
                            out=XG, out_offset=bass.IndirectOffsetOnAxis(ap=slots[:, n, t:t + 1], axis=0),
                            in_=XB[:, t, :], in_offset=None).then_inc(scattered, 16)
                more_turns = pool.value_load(table[0:1, TAB_TURNS:TAB_TURNS + 1], min_val=MOE_TURNS - 1,
                                             max_val=MOE_TURNS - 1 + MAX_EXTRA)
                pool.wait_ge(scattered, L * (ACTIVE * T * 16) + ACTIVE * T * 16)
                pool.sem_inc(sem["moe_loads"], 1)
                for q in range(TURN):
                    pool.dma_start(XB[:, q, :], XG[q * P:(q + 1) * P, :]).then_inc(x_in[q], 16)

                def load(i, q):
                    pool.wait_ge(sem["moe_product"], i * (TURN * PER_TILE) + PER_TILE * q + 3)
                    pool.sem_inc(sem["moe_loads"], 1)
                    pool.dma_start(XB[:, q, :], XG[bass.ds(i * (TURN * P) + (TURN + q) * P, P), :])\
                        .then_inc(x_in[q], 16)

                def store(i, q):
                    pool.wait_ge(sem["moe_act_emptied"], i * (TURN * A_TILE) + A_TILE * (q + 1) + A_AHEAD)
                    pool.sem_inc(sem["moe_loads"], 1)
                    pool.dma_start(YG[bass.ds(i * (TURN * P) + q * P, P), :], YB[:, q % 2, :])\
                        .then_inc(y_out[q % 2], 16)
                with pool.Fori(0, more_turns) as i:
                    for q in range(TURN):
                        load(i, q)
                        store(i, q)
                for q in range(TURN):
                    store(more_turns, q)
                for n in range(2):
                    pool.wait_ge(y_out[n], L * (MOE_TURNS * 32) + extra_before * 32 + more_turns * 32 + 32)
                    pool.sem_inc(sem["moe_loads"], 1)
                for t in range(T):
                    for n in range(ACTIVE):
                        nc.gpsimd.indirect_dma_start(
                            out=GOT[n][:, t, :], out_offset=None, in_=YG,
                            in_offset=bass.IndirectOffsetOnAxis(ap=slots[:, n, t:t + 1], axis=0))\
                            .then_inc(gathered[t], 16)
                pool.wait_ge(sem["layer_end"], 4)
                for name in SIGNALS:
                    pool.sem_clear(sem[name])
                pool.sem_inc(cleared, 1)

        @block.vector
        def _(dve):
            pi, two_pi = float(np.float32(3.1415925)), 2 * np.pi
            c1 = 6.28125
            c2 = float(np.float32(two_pi - c1))
            c3 = float(two_pi - c1 - c2)
            magic = 12582912.0
            own0 = Own(dve, prologue_own)
            dve.wait_ge(consts_in, 6 * 16)
            posf, ang, rounds, sine, cosine = rn_x, QT[:, :, 0:96], KT[:, :, 0:96], KIN[:, :, 0:96], QT[:, :, 0:96]

            def step(ins):
                own0.done(ins)
                own0.need()
            dve.wait_ge(table_in, 16)
            step(nc.vector.tensor_copy(posf, pos))
            step(nc.vector.tensor_copy(iota, ROT[:, 96:96 + N_EXPERTS]))
            step(nc.vector.memset(extra_sum, 0.0))
            for t in range(T):
                step(nc.vector.tensor_scalar(ang[:, t, :], ROT[:, 0:96], posf[:, t:t + 1], None, ALU.mult))
            step(nc.vector.tensor_scalar(rounds, ang, 1 / two_pi, magic, ALU.mult, ALU.add))
            step(nc.vector.tensor_scalar(rounds, rounds, magic, None, ALU.subtract))
            for c in (c1, c2, c3):
                step(nc.vector.scalar_tensor_tensor(ang, rounds, -c, ang, ALU.mult, ALU.add))
            step(nc.vector.tensor_scalar(sine, ang, pi, -pi, ALU.min, ALU.max))
            step(nc.vector.tensor_scalar(ang, ang, pi / 2, None, ALU.add))
            step(nc.vector.tensor_scalar(rounds, ang, pi, -two_pi, ALU.is_gt, ALU.mult))
            step(nc.vector.tensor_tensor(ang, ang, rounds, ALU.add))
            step(nc.vector.tensor_scalar(ang, ang, pi, -pi, ALU.min, ALU.max))
            peak = small[:, 248:248 + HEADS]
            step(nc.vector.tensor_copy(peak, lb_all[:, 0, :]))
            for l in range(1, DEPTH):
                step(nc.vector.tensor_tensor(peak, peak, lb_all[:, l, :], ALU.max))
            own0.done(nc.vector.tensor_tensor(lb_all, lb_all, over(peak, DEPTH), ALU.subtract))
            own0.need()
            dve.sem_inc(ropes, 1)
            dve.wait_ge(pro_act, 3)
            half_m, half_i = DH // 2, IDX_DIM // 2
            step(nc.vector.tensor_copy(cos_m, cosine[:, :, 0:half_m]))
            step(nc.vector.tensor_copy(cos_i, cosine[:, :, half_m:half_m + half_i]))
            step(nc.vector.tensor_copy(sin_m[:, :, 1, :], sine[:, :, 0:half_m]))
            step(nc.vector.tensor_scalar(sin_m[:, :, 0, :], sine[:, :, 0:half_m], -1.0, None, ALU.mult))
            step(nc.vector.tensor_copy(sin_i[:, :, 1, :], sine[:, :, half_m:half_m + half_i]))
            step(nc.vector.tensor_scalar(sin_i[:, :, 0, :], sine[:, :, half_m:half_m + half_i], -1.0, None, ALU.mult))
            whole = small[:, 252:252 + HEADS]
            step(nc.vector.tensor_copy(whole, lb_all[:, 0, :]))
            for l in range(1, DEPTH):
                step(nc.vector.tensor_tensor(whole, whole, lb_all[:, l, :], ALU.add))
            step(nc.vector.reciprocal(whole, whole))
            step(nc.vector.memset(lb_all[:, 0, :], 0.0))
            for l in range(1, DEPTH):
                step(nc.vector.tensor_tensor(lb_all[:, l, :], lb_all[:, l, :], lb_all[:, l - 1, :], ALU.add))
            step(nc.vector.tensor_tensor(lb_all, lb_all, over(whole, DEPTH), ALU.mult))
            step(nc.vector.tensor_copy(mask, masks_in))
            step(nc.vector.memset(ones, 1.0))
            step(nc.vector.memset(bias0, 0.0))
            step(nc.vector.memset(bias0[0:CHUNK, CHUNK:P], REFUSED))
            dve.sem_inc(prologue, 1)

            with dve.Fori(0, DEPTH) as L:
                own = Own(dve, sem["dve_own"])
                em = Emptier(dve, "dve", sem, banks)
                own.done(nc.vector.tensor_copy(lb, lb_all.rearrange("p l h -> p (l h)")[:, bass.ds(L * HEADS, HEADS)]))
                own.need()
                nc.vector.tensor_scalar(one_lb, lb, -1.0, 1.0, ALU.mult, ALU.add).then_inc(sem["lb_ready"], 1)

                def scale_tokens(base):
                    for t in range(T):
                        dve.wait_ge(sem["rn_x"], base + t + 1)
                        nc.vector.tensor_scalar(XN[:, t], X[:, t, :].rearrange("p (d k) -> p k d", k=K),
                                                rn_x[:, t:t + 1], None, ALU.mult).then_inc(sem["x_scaled"], 1)

                def transposed_tokens(key, gain):
                    for k in range(1, K, 2):
                        bank = em.take(key, k)
                        em.empty(nc.vector.tensor_scalar(HT[:, k, :], bank, cols[:, gain + k:gain + k + 1], None, ALU.mult),
                                 key, k)
                scale_tokens(0)
                for m in range(M):
                    dve.wait_ge(sem["rn_mem"], m + 1)
                    nc.vector.tensor_scalar(MN[:, m], MEMX[:, m, :].rearrange("p (d k) -> p k d", k=K),
                                            rn_m[:, m:m + 1], None, ALU.mult).then_inc(sem["mem_scaled"], 1)
                dve.wait_ge(sem["params"], 48)
                transposed_tokens("hT", G_MIX)

                rot = ROT
                for t in range(T):
                    dve.wait_ge(sem["rn_ql"], t + 1)
                    nc.vector.tensor_scalar(C[:, t, :], C[:, t, :], rn_ql[:, t, 0:1], None, ALU.mult)\
                        .then_inc(sem["c_ready"], 1)
                for t in range(T):
                    own.done(nc.vector.tensor_scalar(widx[:, t, :], KI[:, t, IDX_DIM:N_KI], W_IDX, None, ALU.mult))
                    ki = KI[:, t, 0:IDX_DIM]
                    own.done(nc.vector.scalar_tensor_tensor(ki, ki, rn_ql[:, t, 1:2], rows[:, R_KI:R_KI + IDX_DIM],
                                                            ALU.mult, ALU.mult))
                    own.need()
                    half = IDX_DIM // 2
                    r = rot[:, 128 * t:128 * t + 128]
                    for a in range(2):
                        own.done(nc.vector.tensor_tensor(r[:, a * half:(a + 1) * half], ki[:, (1 - a) * half:(2 - a) * half],
                                                         sin_i[:, t, a, :], ALU.mult))
                    for a in range(2):
                        own.done(nc.vector.tensor_tensor(r[:, 64 + a * half:64 + (a + 1) * half],
                                                         ki[:, a * half:(a + 1) * half], cos_i[:, t, :], ALU.mult))
                    own.need()
                    nc.vector.tensor_tensor(KIN[:, t, :].rearrange("p (n i) -> p n i", n=2), over(r[:, 64:128], 2),
                                            over(r[:, 0:64], 2), ALU.add).then_inc(sem["ki_ready"], 1)
                for m in range(M):
                    dve.wait_ge(sem["rn_kx"], m + 1)
                    v = TOK[:, m, :].rearrange("p (h d) -> p h d", h=HEADS)
                    nc.vector.tensor_tensor(v, v, each(rn_h[:, m, :], P), ALU.mult).then_inc(sem["kx_ready"], 1)
                for key, gain in (("kb", R_K), ("qb", R_Q)):
                    for t in range(T):
                        s = t % 2
                        dve.wait_ge(sem["rn_" + key], t + 1)
                        for h in range(HEADS):
                            v = TOK[:, s, h * P:(h + 1) * P]
                            own.done(nc.vector.scalar_tensor_tensor(v, v, rn_h[:, s, h:h + 1], rows[:, gain:gain + DH],
                                                                    ALU.mult, ALU.mult))
                        own.need()
                        v = TOK[:, s, :].rearrange("p (h two i) -> p h two i", h=HEADS, two=2)
                        r = rot.rearrange("p (h two i) -> p h two i", h=HEADS, two=2)
                        for a in range(2):
                            own.done(nc.vector.tensor_tensor(r[:, :, a, :], v[:, :, 1 - a, :],
                                                             over(sin_m[:, t, a, :], HEADS), ALU.mult))
                        own.need()
                        vv = TOK[:, s, :].rearrange("p (n i) -> p n i", i=DH // 2)
                        own.done(nc.vector.tensor_tensor(vv, vv, over(cos_m[:, t, :], 2 * HEADS), ALU.mult))
                        own.need()
                        nc.vector.tensor_tensor(TOK[:, s, :], TOK[:, s, :], rot, ALU.add).then_inc(sem[key + "_ready"], 1)
                        dve.wait_ge(sem[key + "_ready"], t + 1)

                for t in LATER:
                    sc = SC[:, t - 1, 0:(t + 1) * P]
                    for h in range(IDX_HEADS):
                        n = (t - 1) * IDX_HEADS + h
                        emptied(dve, sem, "si", t, h)
                        r = RELU[:, n % 2, 0:(t + 1) * P]
                        if h == 0:
                            ins = nc.vector.tensor_scalar(sc, r, widx[:, t, h:h + 1], None, ALU.mult)
                        else:
                            dve.wait_ge(sem["relu_used"], n)
                            ins = nc.vector.scalar_tensor_tensor(sc, r, widx[:, t, h:h + 1], sc, ALU.mult, ALU.add)
                        ins.then_inc(sem["relu_used"], 1)
                    dve.wait_ge(sem["relu_used"], t * IDX_HEADS)
                    last = own.done(nc.vector.memset(sc[0:CHUNK, t * P + CHUNK:(t + 1) * P], REFUSED))
                step_of = {t: last for t in LATER}
                for r in range(TOPK // 8):
                    for t in LATER:
                        own.need(step_of[t])
                        step_of[t] = own.done(nc.vector.max(top8[:, t - 1, :], SC[:, t - 1, 0:(t + 1) * P]))
                    for t in LATER:
                        sc = SC[:, t - 1, 0:(t + 1) * P]
                        own.need(step_of[t])
                        step_of[t] = own.done(nc.vector.match_replace(sc, top8[:, t - 1, :], sc, TAKEN))
                for t in LATER:
                    sc = SC[:, t - 1, 0:(t + 1) * P]
                    own.need(step_of[t])
                    own.done(nc.vector.tensor_scalar(sc, sc, TAKEN / 1.5, REFUSED, ALU.is_ge, ALU.mult))

                nc.vector.memset(CB[:, 1024:2048], 0.0).then_inc(sem["levels_zero"], 1)
                dve.wait_ge(sem["levels_zero"], 1)
                for h in range(HEADS):
                    dve.wait_ge(sem["forget"], h + 1)
                    own.done(nc.vector.tensor_tensor(L2, L2, L1, ALU.subtract))
                    if h:
                        dve.wait_ge(sem["product"], PRODUCTS.index(("lv", h - 1, LEVELS)) + 1)
                        dve.wait_ge(sem["kd_ready"], h)
                    own.done(nc.vector.scalar_tensor_tensor(KK, E1, one_lb[:, h:h + 1], S1, ALU.mult, ALU.mult))
                    own.need(own.count - 1)
                    for t in range(T):
                        s = slice(t * P, (t + 1) * P)
                        own.done(nc.vector.tensor_tensor_scan(BB[:, s], ones, L2[:, s], 0.0, ALU.mult, ALU.add))
                    dve.wait_ge(sem["queries"], h + 1)
                    em.empty(nc.vector.tensor_tensor(QQ, em.take("q", h), EQ, ALU.mult), "q", h)
                    own.need()
                    dve.wait_ge(sem["dve_emptied"], em.count)
                    if h:
                        dve.wait_ge(sem["product"], PRODUCTS.index(("o", h - 1)) + 1)

                    def halves(a, half):
                        return a.rearrange("p (b two i) -> p b two i", two=2, i=half)

                    def diff(n):
                        half = HALVES[n]
                        d = (DE, EQ)[n % 2].rearrange("p (b i) -> p b i", i=2 * half)
                        b = BB.rearrange("p (b i) -> p b i", i=2 * half)
                        ref = b[:, :, half - 1:half].broadcast_to((P, SEQ // (2 * half), 2 * half))
                        return nc.vector.tensor_tensor(d, b, ref, ALU.subtract)

                    def level_queries(n):
                        half = HALVES[n]
                        dve.wait_ge(sem["decay"], h * LEVELS + n + 1)
                        if n:
                            dve.wait_ge(sem["product"], PRODUCTS.index(("lv", h, n - 1)) + 1)
                            dve.wait_ge(sem["qL"], h * LEVELS + n)
                        nc.vector.tensor_tensor(halves(QL, half)[:, :, 1, :], halves(QQ, half)[:, :, 1, :],
                                                halves((DE, EQ)[n % 2], half)[:, :, 1, :], ALU.mult)\
                            .then_inc(sem["qL"], 1)

                    def level_scores(n):
                        bank = em.take("lv", h, n).rearrange("p (t s) -> p t s", t=T)
                        out4 = SCT.rearrange("p (t s) -> p t s", t=T)
                        dve.wait_ge(sem["dve_emptied"], em.count)
                        em.empty(nc.vector.copy_predicated(out4, over(mask[:, n, :], T), bank), "lv", h, n)
                    diff(0).then_inc(sem["b_ready"], 1)
                    dve.wait_ge(sem["b_ready"], h + 1)
                    own.done(nc.vector.memset(SCT, 0.0))
                    own.need()
                    dve.sem_inc(sem["diff"], 1)
                    for n in range(LEVELS):
                        if n + 1 < LEVELS:
                            if n:
                                dve.wait_ge(sem["kL"], h * LEVELS + n)
                                dve.wait_ge(sem["qL"], h * LEVELS + n)
                            diff(n + 1).then_inc(sem["diff"], 1)
                        level_queries(n)
                        if n:
                            level_scores(n - 1)
                    dve.wait_ge(sem["kL"], h * LEVELS + LEVELS - 1)
                    b = BB.rearrange("p (t i) -> p t i", t=T)
                    nc.vector.tensor_tensor(EQ.rearrange("p (t i) -> p t i", t=T), b,
                                            b[:, :, P - 1:P].broadcast_to((P, T, P)), ALU.subtract).then_inc(sem["diff"], 1)
                    level_scores(LEVELS - 1)
                    level_scores(LEVELS)
                    dve.wait_ge(sem["ends"], h + 1)
                    nc.vector.tensor_tensor(QL, QQ, DE, ALU.mult).then_inc(sem["qe_ready"], 1)
                    bank = em.take("dS", h)
                    dve.wait_ge(sem["qe_ready"], h + 1)
                    own.done(nc.vector.tensor_copy(ST[:, 1, :], bank[:, 0:P]))
                    for t in range(1, T - 1):
                        own.need()
                        ins = nc.vector.scalar_tensor_tensor(ST[:, t + 1, :], ST[:, t, :], e_end[:, t:t + 1],
                                                             bank[:, t * P:(t + 1) * P], ALU.mult, ALU.add)
                        if t == T - 2:
                            em.empty(ins, "dS", h)
                        else:
                            own.done(ins)
                for t in range(T):
                    dve.wait_ge(sem["rn_o"], t + 1)
                    dve.wait_ge(sem["g_ready"], t + 1)
                    for h in range(HEADS):
                        s = slice(h * P, (h + 1) * P)
                        ins = nc.vector.scalar_tensor_tensor(O[:, t, s], O[:, t, s], rn_h[:, t % 2, h:h + 1], G[:, t, s],
                                                             ALU.mult, ALU.mult)
                        if h == HEADS - 1:
                            ins.then_inc(sem["og_ready"], 1)
                        else:
                            own.done(ins)

                def masked(m):
                    t, h = divmod(m, HEADS)
                    w = (t + 1) * P
                    bank = em.take("lg", m)
                    if m >= 2:
                        em.take("pT", m - 2)
                    bias = SC[:, t - 1, 0:w] if t else bias0
                    em.empty(nc.vector.scalar_tensor_tensor(PR[:, m % 2, 0:w], bank[:, 0:w], SCALE, bias,
                                                            ALU.mult, ALU.add), "lg", m)
                    dve.wait_ge(sem["dve_emptied"], em.count)
                    nc.vector.tensor_reduce(mx[:, m % 4, 0:1], PR[:, m % 2, 0:w], AX.X, ALU.max, negate=True)\
                        .then_inc(sem["logits"], 1)

                def normalised(m):
                    w = (m // HEADS + 1) * P
                    dve.wait_ge(sem["exps"], m + 1)
                    own.done(nc.vector.reciprocal(sm[:, m % 4, 1:2], sm[:, m % 4, 0:1]))
                    own.need()
                    nc.vector.tensor_scalar(PR[:, m % 2, 0:w], PR[:, m % 2, 0:w], sm[:, m % 4, 1:2], None, ALU.mult)\
                        .then_inc(sem["probs"], 1)

                def attended(m):
                    t, h = divmod(m, HEADS)
                    em.empty(nc.vector.tensor_copy(OAB[:, HEADS + h, t * P:(t + 1) * P], em.take("pv", m)[:, 0:P]), "pv", m)
                dve.wait_ge(sem["og_ready"], T)
                last_m = T * HEADS
                for m in range(last_m + 3):
                    if m < last_m:
                        masked(m)
                    if 0 <= m - 1 < last_m:
                        normalised(m - 1)
                    if m - 3 >= 0:
                        attended(m - 3)

                def add_to_tokens(key):
                    for t in range(T):
                        for n in range(2):
                            s = slice(n * 512, (n + 1) * 512)
                            nc.vector.tensor_tensor(X[:, t, s], X[:, t, s], em.take(key, t, n), ALU.add)\
                                .then_inc(sem["dve_emptied"], 1)
                            assert EMPTIED["dve"][em.count] == (key, t, n)
                            em.count += 1
                add_to_tokens("xo")
                em.take("xo", T - 1, 1)
                scale_tokens(T)
                transposed_tokens("hxT", G_X)

                for t in range(T):
                    dve.wait_ge(sem["rn_qx"], t + 1)
                    v = TOK[:, t % 2, :].rearrange("p (h d) -> p h d", h=HEADS)
                    nc.vector.tensor_tensor(v, v, each(rn_h[:, t % 2, :], P), ALU.mult).then_inc(sem["qx_ready"], 1)

                def peak_x(m):
                    bank = em.take("lx", m).rearrange("p (a s) -> p a s", a=2)
                    own.done(nc.vector.tensor_reduce(mx[:, m % 4, :], bank, AX.X, ALU.max, negate=True))
                    own.need()
                    nc.vector.tensor_scalar(mx[:, m % 4, :], mx[:, m % 4, :], SCALE, None, ALU.mult)\
                        .then_inc(sem["max_x"], 1)

                def normalised_x(m):
                    emptied(dve, sem, "lx", m)
                    own.done(nc.vector.reciprocal(sm[:, m % 4, :], sm[:, m % 4, :]))
                    own.need()
                    v = PR[:, m % 2, :].rearrange("p (a s) -> p a s", a=2)
                    nc.vector.tensor_tensor(v, v, each(sm[:, m % 4, :], N_MEM), ALU.mult).then_inc(sem["probs_x"], 1)

                def transposed_x(m):
                    bank = em.take("pxT", m)
                    if m >= 2 and m % 2 == 0:
                        em.take("px", m // 2 - 1)
                    em.empty(nc.vector.tensor_copy(PT[:, m % 2, :], bank), "pxT", m)
                for m in range(2 * T + 2):
                    if m < 2 * T:
                        peak_x(m)
                    if 0 <= m - 1 < 2 * T:
                        normalised_x(m - 1)
                    if m >= 2:
                        transposed_x(m - 2)
                add_to_tokens("xx")
                scale_tokens(2 * T)
                transposed_tokens("hfT", G_FFN)

                def do(ins):
                    own.done(ins)
                    own.need()
                tt, ts, red = nc.vector.tensor_tensor, nc.vector.tensor_scalar, nc.vector.tensor_reduce
                bank = em.take("rt")
                em.empty(tt(rlog, bank[:, 0:T * N_ROUTE].rearrange("p (t n) -> p t n", t=T),
                            over(rows[:, R_BIAS:N_ROW], T), ALU.add), "rt")
                dve.wait_ge(sem["dve_emptied"], em.count)
                groups = rlog[:, :, 0:N_GROUPS]

                def first_best(scores, best, chosen, free, tmp):
                    do(red(best[:, :, 0:1], scores, AX.X, ALU.max))
                    do(tt(chosen, scores, best[:, :, 0:1].broadcast_to((P, T, 4)), ALU.is_equal))
                    do(ts(free[:, :, 0:1], chosen[:, :, 0:1], -1.0, 1.0, ALU.mult, ALU.add))
                    for g in range(1, 4):
                        do(tt(chosen[:, :, g:g + 1], chosen[:, :, g:g + 1], free[:, :, 0:1], ALU.mult))
                        do(tt(free[:, :, 0:1], free[:, :, 0:1], chosen[:, :, g:g + 1], ALU.subtract))
                first_best(groups, rw[:, 0], rw[:, 2], rw[:, 3], None)
                tt(rw[:, 1], groups, rw[:, 0, :, 0:1].broadcast_to((P, T, 4)), ALU.subtract).then_inc(sem["router_logits"], 1)
                experts = rlog[:, :, N_GROUPS:].rearrange("p t (g e) -> p t g e", g=N_GROUPS)
                do(tt(rw[:, 4], experts[:, :, 0, :], rw[:, 2, :, 0:1].broadcast_to((P, T, 4)), ALU.mult))
                for g in range(1, N_GROUPS):
                    do(tt(rw[:, 5], experts[:, :, g, :], rw[:, 2, :, g:g + 1].broadcast_to((P, T, 4)), ALU.mult))
                    do(tt(rw[:, 4], rw[:, 4], rw[:, 5], ALU.add))
                first_best(rw[:, 4], rw[:, 0], rw[:, 6], rw[:, 3], None)
                do(nc.vector.scalar_tensor_tensor(rw[:, 5], rw[:, 6], REFUSED, rw[:, 4], ALU.mult, ALU.add))
                first_best(rw[:, 5], rw[:, 9], rw[:, 7], rw[:, 3], None)
                tt(rw[:, 8, :, 0:1], rw[:, 9, :, 0:1], rw[:, 0, :, 0:1], ALU.subtract).then_inc(sem["router_logits"], 1)
                for dst, best in ((chosen1, 6), (chosen2, 7)):
                    own.done(tt(dst.rearrange("p t (g e) -> p t g e", g=N_GROUPS),
                                rw[:, 2].unsqueeze(3).broadcast_to((P, T, N_GROUPS, EXP_PER_GROUP)),
                                rw[:, best].unsqueeze(2).broadcast_to((P, T, N_GROUPS, EXP_PER_GROUP)), ALU.mult))
                own.need()
                own.done(nc.vector.tensor_copy(tri, mask[:, LEVELS + 1, :]))
                own.need()
                tt(chosen, chosen1, chosen2, ALU.add).then_inc(sem["chosen"], 1)
                bank = em.take("rank")
                per_tile = bank[:, 64:128].rearrange("p (t e) -> p t e", t=T)
                do(nc.vector.memset(base[:, 0, :], 0.0))
                for t in range(1, T):
                    do(tt(base[:, t, :], base[:, t - 1, :], per_tile[:, t - 1, :], ALU.add))
                do(tt(total, base[:, T - 1, :], per_tile[:, T - 1, :], ALU.add))
                em.empty(tt(rank, base, bank[:, 0:64].rearrange("p (t e) -> p t e", t=T), ALU.add), "rank")
                do(ts(over_e, total, float(P), None, ALU.is_gt))
                for n in range(2, T):
                    do(nc.vector.scalar_tensor_tensor(over_e, total, float(n * P), over_e, ALU.is_gt, ALU.add))
                do(nc.vector.tensor_tensor_scan(cum, ones[:, 0:N_EXPERTS], over_e, 0.0, ALU.mult, ALU.add))
                do(tt(shift, cum, over_e, ALU.subtract))
                do(tt(shift, shift, iota, ALU.subtract))
                do(ts(shift, shift, float(N_EXPERTS - 1), float(P), ALU.add, ALU.mult))
                dve.wait_ge(sem["dve_emptied"], em.count)
                do(nc.vector.scalar_tensor_tensor(place, over(iota, T), float(P), rank, ALU.mult, ALU.add))
                do(nc.vector.scalar_tensor_tensor(rank, rank, float(P), over(shift, T), ALU.is_ge, ALU.mult))
                do(tt(place, place, rank, ALU.add))
                for n, picked in enumerate((chosen1, chosen2)):
                    do(tt(picked, picked, place, ALU.mult))
                    do(red(placef[:, n * T:(n + 1) * T], picked, AX.X, ALU.add))
                do(nc.vector.tensor_copy(slots.rearrange("p n t -> p (n t)"), placef))
                do(tt(before_j, over(cum, 8), each(iota[:, 0:8], N_EXPERTS), ALU.is_le))
                do(red(expert_j, before_j, AX.X, ALU.add))
                do(ts(table[:, 0:8], expert_j, float(N_EXPERTS - 1), None, ALU.min))
                do(ts(extra, cum[:, N_EXPERTS - 1:], 0.0, None, ALU.is_gt))
                for n in range(1, MAX_EXTRA):
                    do(nc.vector.scalar_tensor_tensor(extra, cum[:, N_EXPERTS - 1:], float(n * TURN), extra,
                                                      ALU.is_gt, ALU.add))
                do(nc.vector.tensor_copy(table[:, TAB_EXTRA:TAB_EXTRA + 1], extra))
                do(ts(table[:, TAB_TURNS:TAB_TURNS + 1], extra, float(MOE_TURNS - 1), None, ALU.add))
                do(tt(extra_sum, extra_sum, extra, ALU.add))
                do(nc.vector.tensor_copy(table[:, bass.ds(L + TAB_BEFORE + 1, 1)], extra_sum))
                dve.wait_ge(sem["router_exp"], 2)
                do(red(rw[:, 10, :, 0:1], rw[:, 1], AX.X, ALU.add))
                do(ts(rw[:, 10, :, 1:2], rw[:, 8, :, 0:1], 1.0, None, ALU.add))
                do(tt(rw[:, 10, :, 0:1], rw[:, 10, :, 0:1], rw[:, 10, :, 1:2], ALU.mult))
                do(nc.vector.reciprocal(rw[:, 10, :, 0:1], rw[:, 10, :, 0:1]))
                do(tt(rw[:, 10, :, 1:2], rw[:, 10, :, 0:1], rw[:, 8, :, 0:1], ALU.mult))
                assert em.count == len(EMPTIED["dve"])
                dve.sem_inc(sem["slots_ready"], 1)

                more_turns = dve.value_load(table[0:1, TAB_TURNS:TAB_TURNS + 1], min_val=MOE_TURNS - 1,
                                            max_val=MOE_TURNS - 1 + MAX_EXTRA)

                def made(i, at):
                    dve.wait_ge(sem["moe_product"], i * (TURN * PER_TILE) + at + 1)
                    return banks[at % BANKS]

                def tokens(i, q, at):
                    for n in range(2):
                        gain = cols[:, G_FFN + 4 * n:G_FFN + 4 * n + 4]
                        bank = made(i, at + n).rearrange("p (k t) -> p k t", k=4)
                        tt(XT[:, q % 2, 4 * n:4 * n + 4, :], bank, each(gain, P), ALU.mult)\
                            .then_inc(sem["moe_dve_emptied"], 1)

                def hidden(i, q):
                    at = PER_TILE * q if q else 2
                    dve.wait_ge(sem["silu"], i * TURN + q + 1)
                    tt(HID[:, q % 2, :], SILU[:, q % 2, :], banks[at % BANKS][:, D_EXPERT:2 * D_EXPERT], ALU.mult)\
                        .then_inc(sem["moe_dve_emptied"], 1)

                def tile(i, q, last=False):
                    at = PER_TILE * q
                    hidden(i, q)
                    if not last:
                        tokens(i, q + 1, at + 1 if q else 3)
                    bank = made(i, at + 3 if last else at + 5)[:, 0:2 * P]
                    nc.vector.tensor_copy(HIDT[:, q % 2].rearrange("p f t -> p (f t)"), bank)\
                        .then_inc(sem["moe_dve_emptied"], 1)
                tokens(0, 0, 0)
                tile(0, 0)
                with dve.Fori(0, more_turns) as i:
                    for q in range(1, TURN + 1):
                        tile(i, q)
                for q in range(1, TURN):
                    tile(more_turns, q, last=q == TURN - 1)
                for n in range(ACTIVE):
                    for t in range(T):
                        dve.wait_ge(gathered[t], L * (ACTIVE * 16) + ACTIVE * 16)
                        if n:
                            own.need(added[t])
                        elif t == 0:
                            added = {}
                        added[t] = own.done(nc.vector.scalar_tensor_tensor(
                            X[:, t, :], GOT[n][:, t, :], rw[:, 10, t, n:n + 1], X[:, t, :], ALU.mult, ALU.add))
                own.need()
                dve.sem_inc(sem["layer_end"], 1)
                dve.wait_ge(cleared, L + 1)


def kernel(x, mem, positions, norm_mix, w_in, lb_raw, a_gnorm, b_qlat_gain, b_wqb, b_wqidx, b_qnorm, b_knorm,
           b_kidx_norm, w_out, norm_x, norm_mem, x_wq, x_wk, x_wv, x_wo, x_qnorm, x_knorm, norm_ffn, w_rg, b_rg,
           w_re, b_re, w_gu, w_dn):
    import concourse.bacc as bacc
    from concourse.bass_utils import run_bass_kernel_spmd

    a = {k: np.asarray(v) for k, v in locals().items() if k not in ("bacc", "run_bass_kernel_spmd")}
    by_row = lambda v: v.reshape(DEPTH, P, K)
    by_block = lambda v: np.transpose(v.reshape(DEPTH, -1, P), (0, 2, 1))
    col = np.concatenate([by_row(a["norm_mix"]), by_row(a["norm_x"]), by_row(a["norm_mem"]), by_row(a["norm_ffn"]),
                          by_block(a["b_qlat_gain"]), by_block(a["a_gnorm"]), by_block(a["x_qnorm"]),
                          by_block(a["x_knorm"])], axis=2)
    row = np.concatenate([a["b_qnorm"], a["b_knorm"], a["b_kidx_norm"], a["b_rg"], a["b_re"].reshape(DEPTH, -1)], axis=1)
    router = np.concatenate([a["w_rg"], a["w_re"].reshape(DEPTH, D_MODEL, N_EXPERTS)], axis=2)
    lb0 = np.transpose(a["lb_raw"].reshape(DEPTH, HEADS, P), (2, 0, 1))
    freq = np.concatenate([ROPE_THETA ** (-np.arange(0, d, 2) / d) for d in (DH, IDX_DIM)]
                          + [np.arange(N_EXPERTS)]).astype(np.float32)
    s, t = np.arange(P)[:, None], np.arange(P)[None, :]
    masks = np.stack([(s // (2 * h) == t // (2 * h)) & (s // h < t // h) for h in HALVES] + [s == t, s < t], axis=1).astype(np.int32)
    feed = {
        "x": a["x"], "mem": a["mem"], "positions": a["positions"].reshape(T, P).T, "w_in": a["w_in"], "b_wqb": a["b_wqb"],
        "b_wqidx": a["b_wqidx"], "w_out": a["w_out"], "x_wq": a["x_wq"], "x_wk": a["x_wk"], "x_wv": a["x_wv"],
        "x_wo": a["x_wo"], "router": router, "w_gu": a["w_gu"], "w_dn": a["w_dn"], "colparams": col,
        "rowparams": row, "lb_raw": lb0, "freqs": freq, "ident": np.eye(P, dtype=np.float32), "masks": masks,
        "zeros": np.zeros((P, 16), np.int32),
    }
    feed = {k: np.ascontiguousarray(v) for k, v in feed.items()}
    nc = bacc.Bacc("TRN2", target_bir_lowering=False, num_devices=1)
    ap = {k: nc.dram_tensor("in_" + k, v.shape, mybir.dt.from_np(v.dtype), kind="ExternalInput").ap()
          for k, v in feed.items()}
    out = nc.dram_tensor("out_0", (1, SEQ, D_MODEL), F32, kind="ExternalOutput").ap()
    hybrid_block(nc, ap["x"], ap["mem"], ap["positions"], ap["w_in"], ap["b_wqb"], ap["b_wqidx"], ap["w_out"],
                 ap["x_wq"], ap["x_wk"], ap["x_wv"], ap["x_wo"], ap["router"], ap["w_gu"], ap["w_dn"],
                 ap["colparams"], ap["rowparams"], ap["lb_raw"], ap["freqs"], ap["ident"], ap["masks"], ap["zeros"], out)
    r = run_bass_kernel_spmd(nc, [{"in_" + k: v for k, v in feed.items()}], core_ids=[0])
    return r.results[0]["out_0"]
```

```python
import concourse.bass as bass
from concourse import mybir
from contextlib import ExitStack
import numpy as np

F32 = mybir.dt.float32
I32 = mybir.dt.int32
U8 = mybir.dt.uint8
ALU = mybir.AluOpType
ACT = mybir.ActivationFunctionType
AX = mybir.AxisListType

P = 128
D_MODEL, SEQ, DEPTH = 1024, 512, 2
EPS = 1e-6
ROPE_THETA = 10000.0
HEADS, DH = 4, 128
WIDTH = HEADS * DH
Q_LORA = 256
IDX_HEADS, IDX_DIM = 16, 64
TOPK = min(256, SEQ // 4)
CHUNK = 64
N_MEM = 256
N_GROUPS, EXP_PER_GROUP = 4, 4
N_EXPERTS = N_GROUPS * EXP_PER_GROUP
D_EXPERT = 256
T = SEQ // P
K = D_MODEL // P
M = N_MEM // P
LATER = list(range(1, T))
D_IN = 4 * WIDTH + Q_LORA + 2 * WIDTH + IDX_DIM + IDX_HEADS
C_AQ, C_AF, C_AI, C_AG = (n * WIDTH for n in range(4))
C_QL = 4 * WIDTH
C_BK = C_QL + Q_LORA
C_BV = C_BK + WIDTH
C_KI = C_BV + WIDTH
N_KI = IDX_DIM + IDX_HEADS
N_QL = Q_LORA + N_KI
HALVES = [64, 32, 16, 8, 4, 2, 1]
LEVELS = len(HALVES)
SCALE = DH ** -0.5
W_IDX = IDX_HEADS ** -0.5 * IDX_DIM ** -0.5
REFUSED = -1.0e30
TAKEN = -3.0e38

G_MIX, G_X, G_MEM, G_FFN = (n * K for n in range(4))
G_QLAT = 4 * K
G_AG = G_QLAT + Q_LORA // P
G_XQ = G_AG + 1
G_XK = G_XQ + 1
N_COL = G_XK + 1
R_Q, R_K, R_KI = 0, DH, 2 * DH
R_BIAS = R_KI + IDX_DIM
N_ROUTE = N_GROUPS + N_EXPERTS
N_ROW = R_BIAS + N_ROUTE

UNIT = 4096
RING = 4
UNITS = ["kx", "vx", "ql", "kb", "vb", "lora", "vA", "f", "q", "g", "outA", "outB", "xq", "xo"]
PARTS = {"ql": 2, "lora": 2}
SLOT = {u: n % RING for n, u in enumerate(UNITS)}
TURN = 4
MOE_TURNS = N_EXPERTS // TURN
ACTIVE = 2
OVERFLOW = (ACTIVE * SEQ - 1) // P
MAX_EXTRA = -(-OVERFLOW // TURN)
TILES = N_EXPERTS + MAX_EXTRA * TURN
FILL = 4
FILLS = TILES // FILL
MOE_UNITS = ["gu0", "gu1", "gu2", "dn0", "gu3", "dn1"]
MOE_SLOT = {"gu0": 2, "gu1": 3, "gu2": 0, "gu3": 1, "dn0": RING, "dn1": RING + 1}
MOE_PARTS = {"dn0": 2, "dn1": 2}
MOE_DONE = {"gu0": 1, "gu1": 2, "gu2": 3, "dn0": 4, "gu3": 5, "dn1": 7}
U_TURN = len(MOE_UNITS)
U_LAYER = len(UNITS) + MOE_TURNS * U_TURN
SLOTS = RING + 2


def slot_loads(slot):
    return (sum(PARTS.get(u, 1) for u in UNITS if SLOT[u] == slot),
            sum(MOE_PARTS.get(u, 1) for u in MOE_UNITS if MOE_SLOT[u] == slot))


def loads_so_far(part, where, name):
    parts = {**PARTS, **MOE_PARTS}
    return sum(parts.get(u, 1) for u in part[:part.index(name) + 1] if where[u] == where[name])


def used_before(name):
    if name in SLOT:
        n = UNITS.index(name)
        earlier = [m for m in range(n) if SLOT[UNITS[m]] == SLOT[name]]
        last = max(MOE_DONE[u] for u in MOE_UNITS if MOE_SLOT[u] == SLOT[name])
        return U_LAYER + (earlier[-1] + 1 if earlier else last - U_TURN)
    earlier = [m for m, u in enumerate(UNITS) if SLOT[u] == MOE_SLOT[name]]
    first = earlier[-1] if earlier else UNITS.index("xq")
    return U_LAYER + max(first + 1, len(UNITS) + MOE_DONE[name] - U_TURN)


TAB_TURNS, TAB_EXTRA = 8, 9
TAB_BEFORE = 10


BESIDE = {K // 2 - 1: "f", LEVELS: "q"}

def halves_of(name, t):
    return [(name, t, 0), (name, t, 1)]


def products():
    out = [("mT", j) for j in range(K // 2)] + [("kx", m) for m in range(M)]
    out += [("vx", m) for m in range(M)] + [("kxT", m) for m in range(M)]
    for t in range(T):
        out += halves_of("hT", t) + ([("ql", t - 1)] if t else [])
    out += [("ql", T - 1)]
    out += [("cT", c) for c in range(Q_LORA // P)] + [("kiT",)]
    out += [("qi", t, n) for t in LATER for n in range(2)]
    for t in range(T):
        out += [("kb", t)] + ([("kbT", t - 1)] if t else [])
    out += [("vb", 0), ("kbT", T - 1)]
    for t in range(T):
        out += [("qb", t)] + ([("qbT", t - 1)] if t else []) + ([("vb", t + 1)] if t + 1 < T else [])
    out += [("qiT", t, n) for t in LATER for n in range(2)] + [("qbT", T - 1)]
    out += [("si", t, h) for t in LATER for h in range(IDX_HEADS)]
    out += [("vA", t) for t in range(T)]
    out += [("f", 0), ("q", 0), ("g", 0)]
    for h in range(HEADS):
        for n in range(LEVELS + 1):
            out += ([("kdT", h)] if n == LEVELS else []) + [("lv", h, n)]
            if h + 1 < HEADS and n in BESIDE:
                out += [(BESIDE[n], h + 1)]
        out += [("dS", h), ("o", h)] + ([("g", h + 1)] if h + 1 < HEADS else [])
    out += [("oaT", t) for t in range(T)]
    out += [("lg", m) for m in range(2)]
    for m in range(T * HEADS):
        out += [("pT", m)] + ([("lg", m + 2)] if m + 2 < T * HEADS else []) + ([("pv", m - 1)] if m else [])
        out += [("xa", m)]
    out += [("pv", T * HEADS - 1)]
    for t in range(T):
        out += halves_of("xo", t) + (halves_of("hxT", t - 1) if t else [])
    for t in range(T):
        out += [("qx", t)] + ([("qxT", t - 1)] if t else halves_of("hxT", T - 1))
    out += [("qxT", T - 1)] + [("lx", m) for m in range(2)]
    for m in range(2 * T):
        out += [("pxT", m)] + ([("lx", m + 2)] if m + 2 < 2 * T else [])
        out += [("px", m // 2 - 1)] if m % 2 == 0 and m else []
        out += [("xx",) + divmod(m - 3, 2)] if m >= 3 else []
    out += [("px", T - 1)]
    for t in range(3):
        out += [("xx",) + divmod(2 * T - 3 + t, 2)] + halves_of("hfT", t)
    out += halves_of("hfT", T - 1) + [("rt",), ("rank",)]
    return out


BANKS = 8
PRODUCTS = products()
ON_VECTOR = ("hT", "hxT", "hfT", "q", "lv", "dS", "lg", "pv", "xa", "xo", "pxT", "xx", "rt", "rank")


def emptied_by(name):
    return "dve" if name[0] in ON_VECTOR else "act"


EMPTIED = {e: [p for p in PRODUCTS if emptied_by(p) == e] for e in ("act", "dve")}
for h in range(1, HEADS):
    EMPTIED["dve"].remove(("q", h))
    EMPTIED["dve"].insert(EMPTIED["dve"].index(("dS", h - 1)) + 1, ("q", h))

PER_TILE = 6
D_TILE = 4
A_TILE = 2
A_AHEAD = 4
MOE_D = {"xT0": 0, "xT1": 1, "gu": 3, "hT": 6}

SIGNALS = [
    "params",
    "cols_ready",
    "product",
    "act_emptied",
    "dve_emptied",
    "rn_x", "rn_ql", "rn_kx", "rn_kb", "rn_qb", "rn_o", "rn_qx",
    "x_scaled",
    "c_ready", "ki_ready", "kx_ready", "kb_ready", "qb_ready",
    "qi_ready",
    "relu_ready",
    "relu_used",
    "bias_ready",
    "sigma_g", "g_ready",
    "forget", "queries",
    "b_ready",
    "diff", "decay",
    "qL", "kL",
    "ends",
    "kd_ready", "qe_ready",
    "state",
    "og_ready",
    "logits", "exps", "probs",
    "x_mixed",
    "qx_ready", "max_x", "exps_x", "probs_x",
    "x_crossed",
    "router_exp", "router_exp2", "router_logits", "gates",
    "chosen",
    "slots_ready",
    "lb_ready", "levels_zero",
    "moe_loads",
    "moe_product",
    "silu",
    "moe_dve_emptied", "moe_act_emptied",
    "dve_own", "act_own", "pool_own",
    "in_moe",
    "layer_end",
]
LATE_SIGNALS = ["slots_ready", "in_moe", "moe_loads", "moe_product", "silu", "moe_dve_emptied", "moe_act_emptied",
                "layer_end"]


class Own:

    def __init__(self, engine, semaphore):
        self.engine, self.semaphore, self.count = engine, semaphore, 0

    def done(self, instruction):
        self.count += 1
        instruction.then_inc(self.semaphore, 1)
        return self.count

    def need(self, count=None):
        self.engine.wait_ge(self.semaphore, self.count if count is None else count)


class Emptier:

    def __init__(self, engine, key, sem, banks):
        self.engine, self.key, self.sem, self.banks, self.count = engine, key, sem, banks, 0

    def take(self, *name):
        n = PRODUCTS.index(name)
        self.engine.wait_ge(self.sem["product"], n + 1)
        return self.banks[n % BANKS]

    def empty(self, instruction, *name):
        assert EMPTIED[self.key][self.count] == name, (self.key, self.count, EMPTIED[self.key][self.count], name)
        self.count += 1
        instruction.then_inc(self.sem[self.key + "_emptied"], 1)


def emptied(engine, sem, *name):
    key = emptied_by(name)
    engine.wait_ge(sem[key + "_emptied"], EMPTIED[key].index(name) + 1)


def over(ap, n):
    return ap.unsqueeze(1).broadcast_to((ap.shape[0], n, ap.shape[1]))


def each(ap, n):
    return ap.unsqueeze(2).broadcast_to((ap.shape[0], ap.shape[1], n))


def hybrid_block(nc, x, mem, positions, w_in, b_wqb, b_wqidx, w_out, x_wq, x_wk, x_wv, x_wo,
                 w_re, w_gu, w_dn, colparams, rowparams, lb_raw, freqs, ident, masks, zeros, out):
    ctx = ExitStack()
    with ctx:
        def sb(name, shape, dt=F32):
            return ctx.enter_context(nc.sbuf_tensor(name, [P] + shape, dt))[tuple([slice(None)] * (len(shape) + 1))]

        def sem1(name):
            return ctx.enter_context(nc.semaphore(name))

        sem = {name: sem1(name) for name in SIGNALS}
        slot_full = [sem1(f"slot_full{n}") for n in range(SLOTS)]
        w_used = sem1("w_used")
        consts_in = sem1("consts_in")
        ropes = sem1("ropes")
        prologue = sem1("prologue")
        pro_act = sem1("pro_act")
        prologue_own = sem1("prologue_own")
        loads_begun = sem1("loads_begun")
        cleared = sem1("cleared")
        out_done = sem1("out_done")
        table_in = sem1("table_in")
        scattered = sem1("scattered")
        x_in = [sem1(f"x_in{n}") for n in range(TURN)]
        y_out = [sem1(f"y_out{n}") for n in range(2)]
        gathered = [sem1(f"gathered{t}") for t in range(T)]
        mem_scaled = sem1("mem_scaled")
        mem_in = sem1("mem_in")
        cols_in = sem1("cols_in")
        x_loaded = sem1("x_loaded")
        combined = sem1("combined")
        outputs_stored = sem1("outputs_stored")
        first_added = sem1("first_added")
        zero_tile = sem1("zero_tile")
        zero_filled = sem1("zero_filled")

        XG = nc.dram_tensor("expert_tokens", (TILES * P, D_MODEL), F32, kind="Internal").ap()
        YG = nc.dram_tensor("expert_outputs", (TILES * P, D_MODEL), F32, kind="Internal").ap()

        X = sb("X", [T, D_MODEL])
        HT = sb("HT", [K, SEQ])
        ring = sb("ring", [RING, UNIT])
        XC = sb("XC", [4096])
        CB = sb("CB", [2048])
        AR = sb("AR", [9216])
        QT = sb("QT", [HEADS, SEQ])
        KT = sb("KT", [HEADS, SEQ])
        KIT = sb("KIT", [SEQ])
        SC = sb("SC", [len(LATER), SEQ])
        TOK = sb("TOK", [2, WIDTH])
        ST = sb("ST", [T, DH])
        KXT = sb("KXT", [HEADS, N_MEM])
        VX = sb("VX", [M, WIDTH])
        JUNK = sb("JUNK", [256])
        ROT = sb("ROT", [512])
        idn = sb("idn", [P])
        mask = sb("mask", [LEVELS + 2, P], U8)
        cos_m = sb("cos_m", [T, DH // 2])
        sin_m = sb("sin_m", [T, 2, DH // 2])
        cos_i = sb("cos_i", [T, IDX_DIM // 2])
        sin_i = sb("sin_i", [T, 2, IDX_DIM // 2])
        bias0 = sb("bias0", [P])
        ones = sb("ones", [P])
        rows = sb("rows", [N_ROW])
        cols = sb("cols", [N_COL])
        cols_all = sb("cols_all", [DEPTH, N_COL])
        lb_all = sb("lb_all", [DEPTH, HEADS])
        lb = sb("lb", [HEADS])
        one_lb = sb("one_lb", [HEADS])
        small = sb("small", [256])
        pos = sb("pos", [T], I32)
        table = sb("table", [16], I32)
        slots = sb("slots", [ACTIVE, T], I32)
        masks_in = ring[:, RING - 1, 0:(LEVELS + 2) * P].bitcast(I32).rearrange("p (n s) -> p n s", s=P)

        XN = XC.rearrange("p (t k d) -> p t k d", t=T, k=K)
        XNX = AR[:, 0:4096].rearrange("p (t k d) -> p t k d", t=T, k=K)
        QIT = XC[:, 0:3072].rearrange("p (t g d) -> p t g d", t=len(LATER), g=IDX_HEADS // 2)
        OAB = XC.rearrange("p (k t) -> p k t", k=2 * HEADS)
        E1, L1, L2, S1 = (XC[:, 512 * n:512 * n + 512] for n in range(4))
        G = XC[:, 2048:4096].rearrange("p (t n) -> p t n", t=T)
        C = CB[:, 0:1024].rearrange("p (t c) -> p t c", t=T)
        CT = CB[:, 1024:2048].rearrange("p (c t) -> p c t", c=2)
        EQ, DE, QL, KL = (CB[:, 512 * n:512 * n + 512] for n in range(4))
        PR = CB[:, 0:1024].rearrange("p (n s) -> p n s", n=2)
        PT = CB[:, 1024:2048].rearrange("p (n s) -> p n s", n=2)
        AB, OA, VA, VB = AR[:, 0:3072], AR[:, 3072:5120], AR[:, 5120:7168], AR[:, 7168:9216]
        QI = AB.rearrange("p (t n) -> p t n", t=len(LATER))
        RELU = AB[:, 0:1024].rearrange("p (n s) -> p n s", n=2)
        BB, KK, QQ, SCT, KDT, XX = (AB[:, 512 * n:512 * n + 512] for n in range(6))
        SIGMA = TOK[:, 0, :]
        QLS, KLS = (QL, KDT), (KL, XX)
        MEMX = CB.rearrange("p (m d) -> p m d", m=M)
        MN = [a[:, 2:4, :].rearrange("p h t -> p (h t)").rearrange("p (k d) -> p k d", k=K) for a in (QT, KT)]
        MT = VA.rearrange("p (k m) -> p k m", k=K)
        PTMP = OA[:, 0:1024]
        O = OA.rearrange("p (t n) -> p t n", t=T)
        VAt = VA.rearrange("p (t n) -> p t n", t=T)
        VBt = VB.rearrange("p (t n) -> p t n", t=T)
        DN = [AR[:, n * UNIT:(n + 1) * UNIT] for n in range(2)]
        XB = XC.rearrange("p (s d) -> p s d", s=4)
        HF = HT.rearrange("p k t -> p (k t)")
        XT = HF[:, 0:2048].rearrange("p (s k t) -> p s k t", s=2, k=K)
        YB = HF[:, 2048:4096].rearrange("p (s d) -> p s d", s=2)
        HID = QT[:, 0, :].rearrange("p (s f) -> p s f", s=2)
        HIDT = QT[:, 1, :].rearrange("p (s f t) -> p s f t", s=2, f=2)
        SILU = KT[:, 0, :].rearrange("p (s f) -> p s f", s=2)
        GOT = [XB, HF.rearrange("p (t d) -> p t d", t=T)]
        OXT = KT

        def take_small(n):
            take_small.at += n
            return small[:, take_small.at - n:take_small.at]
        take_small.at = 0
        ss_x = take_small(T)
        rn_x = take_small(T)
        ss_m = take_small(M)
        rn_m = take_small(M)
        ss_ql = take_small(2 * T).rearrange("p (t n) -> p t n", t=T)
        rn_ql = take_small(2 * T).rearrange("p (t n) -> p t n", t=T)
        ss_h = take_small(2 * HEADS).rearrange("p (t n) -> p t n", t=2)
        rn_h = take_small(2 * HEADS).rearrange("p (t n) -> p t n", t=2)
        widx = take_small(T * IDX_HEADS).rearrange("p (t n) -> p t n", t=T)
        top8 = take_small(8 * len(LATER)).rearrange("p (t n) -> p t n", t=len(LATER))
        e_end = take_small(T)
        mx = take_small(8).rearrange("p (n j) -> p n j", n=4)
        sm = take_small(8).rearrange("p (n j) -> p n j", n=4)
        iota = take_small(N_EXPERTS)
        powers = take_small(N_EXPERTS)
        own_shift = take_small(N_EXPERTS)
        extra_sum = take_small(1)
        rlog = SC[:, 0, 0:T * N_ROUTE].rearrange("p (t n) -> p t n", t=T)
        rw = SC[:, 1, 0:48 * T].rearrange("p (i t n) -> p i t n", t=T, n=4)
        tri = SC[:, 0, P:2 * P]
        scores16, marked16 = (SC[:, 0, 256 + 64 * n:320 + 64 * n].rearrange("p (t e) -> p t e", t=T) for n in range(2))
        chosen1, chosen2, chosen, rank, base, place = (
            SC[:, 2, 64 * n:64 * n + 64].rearrange("p (t e) -> p t e", t=T) for n in range(6))
        total, over_e, cum, shift = (SC[:, 1, 192 + 16 * n:208 + 16 * n] for n in range(4))
        before_j = SC[:, 1, 256:256 + 8 * N_EXPERTS].rearrange("p (j e) -> p j e", e=N_EXPERTS)
        expert_j, extra, placef = SC[:, 1, 384:392], SC[:, 1, 392:393], SC[:, 1, 400:400 + ACTIVE * T]
        KIN = KIT.rearrange("p (t n) -> p t n", t=T)
        KI = SC[:, 0, 0:T * N_KI].rearrange("p (t n) -> p t n", t=T)
        wr_sb = sb("wr_sb", [K, N_ROUTE])

        banks = [ctx.enter_context(nc.psum_tensor(f"bank{n}", [P, 512], F32))[:, :] for n in range(BANKS)]

        block = ctx.enter_context(nc.Block())

        def weight_view(slot):
            return ring[:, slot, :] if slot < RING else DN[slot - RING]

        @block.sync
        def _(sp):
            sp.dma_start(table, zeros).then_inc(table_in, 16)
            sp.dma_start(pos, positions).then_inc(consts_in, 16)
            sp.dma_start(ROT[:, 0:DH // 2 + IDX_DIM // 2 + 2 * N_EXPERTS], freqs.partition_broadcast(P)).then_inc(consts_in, 16)
            sp.dma_start(lb_all, lb_raw).then_inc(consts_in, 16)
            sp.dma_start(idn, ident).then_inc(consts_in, 16)
            sp.dma_start(masks_in, masks).then_inc(consts_in, 16)

            in_v = w_in.rearrange("l (p k) n -> (l p) k n", k=K)
            qb_v = b_wqb.rearrange("l (k p) n -> l p k n", p=P)
            qi_v = b_wqidx.rearrange("l (k p) n -> l p k n", p=P)
            out_v = w_out.rearrange("l (s k p) n -> (l s) p k n", s=2, p=P)
            xo_v = x_wo.rearrange("l (k p) n -> l p k n", p=P)
            xq_v, xk_v, xv_v = (w.rearrange("l (p k) n -> (l p) (k n)", k=K) for w in (x_wq, x_wk, x_wv))
            gu_v = w_gu.rearrange("l g e (p k) f -> (l g e p) (k f)", k=K)
            dn_v = w_dn.rearrange("l g e (k p) d -> (l g e) p k d", p=P)

            sp.dma_start(MEMX, mem.rearrange("b (m p) d -> p (b m) d", p=P)).then_inc(mem_in, 16)
            sp.dma_start(cols_all, colparams.rearrange("l p n -> p l n")).then_inc(cols_in, 16)
            sp.wait_ge(table_in, 16)
            with sp.Fori(0, DEPTH) as L:
                extra_before = sp.value_load(table[0:1, bass.ds(L + TAB_BEFORE, 1)], min_val=0, max_val=DEPTH * MAX_EXTRA)

                def sources(name):
                    rows_l = bass.ds(L * P, P)

                    def cut(a, n):
                        return in_v[rows_l, :, a:a + n]
                    return {
                        "ql": lambda: [(cut(C_QL, Q_LORA), 0, Q_LORA), (cut(C_KI, N_KI), Q_LORA, N_KI)],
                        "kb": lambda: [(cut(C_BK, WIDTH), 0, WIDTH)],
                        "vb": lambda: [(cut(C_BV, WIDTH), 0, WIDTH)],
                        "vA": lambda: [(cut(C_AI, WIDTH), 0, WIDTH)],
                        "g": lambda: [(cut(C_AG, WIDTH), 0, WIDTH)],
                        "f": lambda: [(cut(C_AF, WIDTH), 0, WIDTH)],
                        "q": lambda: [(cut(C_AQ, WIDTH), 0, WIDTH)],
                    }[name]()

                for name in UNITS:
                    slot = SLOT[name]
                    if slot == RING - 1:
                        sp.wait_ge(prologue, 1)
                    sp.wait_ge(w_used, L * U_LAYER + extra_before * U_TURN + used_before(name))
                    sp.sem_inc(loads_begun, 1)
                    w = ring[:, slot, :]
                    full = slot_full[slot]
                    if name in ("kx", "vx", "xq"):
                        src = {"kx": xk_v, "vx": xv_v, "xq": xq_v}[name]
                        sp.dma_start(w, src[bass.ds(L * P, P), :]).then_inc(full, 16)
                    elif name == "lora":
                        sp.dma_start(w[:, 0:1024].rearrange("p (k n) -> p k n", k=2),
                                     qb_v[bass.ds(L, 1), :, :, :].rearrange("l p k n -> (l p) k n")).then_inc(full, 16)
                        sp.dma_start(w[:, 1024:3072].rearrange("p (k n) -> p k n", k=2),
                                     qi_v[bass.ds(L, 1), :, :, :].rearrange("l p k n -> (l p) k n")).then_inc(full, 16)
                    elif name in ("outA", "outB"):
                        src = out_v[bass.ds(L * 2 + (name == "outB"), 1), :, :, :].rearrange("l p k n -> (l p) k n")
                        sp.dma_start(w.rearrange("p (k n) -> p k n", k=4), src).then_inc(full, 16)
                    elif name == "xo":
                        src = xo_v[bass.ds(L, 1), :, :, :].rearrange("l p k n -> (l p) k n")
                        sp.dma_start(w.rearrange("p (k n) -> p k n", k=4), src).then_inc(full, 16)
                    else:
                        width = N_QL if name == "ql" else WIDTH
                        wv = w[:, 0:K * width].rearrange("p (k n) -> p k n", k=K)
                        for src, at, n in sources(name):
                            sp.dma_start(wv[:, :, at:at + n], src).then_inc(full, 16)

                def turn_loads(i, expert):
                    for name in MOE_UNITS:
                        slot, n = MOE_SLOT[name], int(name[2])
                        sp.wait_ge(w_used, L * U_LAYER + extra_before * U_TURN + i * U_TURN + used_before(name))
                        sp.sem_inc(loads_begun, 1)
                        if name[:2] == "gu":
                            sp.dma_start(ring[:, slot, :], gu_v[bass.ds(expert(n) * P, P), :]).then_inc(slot_full[slot], 16)
                        else:
                            for a in range(2):
                                src = dn_v[bass.ds(expert(2 * n + a), 1), :, :, :].rearrange("e p k d -> (e p) k d")
                                dst = DN[slot - RING][:, a * 2048:(a + 1) * 2048].rearrange("p (k d) -> p k d", k=2)
                                sp.dma_start(dst, src).then_inc(slot_full[slot], 16)
                with sp.Fori(0, MOE_TURNS) as i:
                    turn_loads(i, lambda q: L * N_EXPERTS + i * TURN + q)
                sp.wait_ge(sem["slots_ready"], 2)
                extra_turns = sp.value_load(table[0:1, TAB_EXTRA:TAB_EXTRA + 1], min_val=0, max_val=MAX_EXTRA)
                with sp.If(extra_turns > 0):
                    with sp.Fori(0, extra_turns) as j:
                        experts_of = [sp.value_load(table[0:1, bass.ds(j * TURN + q, 1)], min_val=0, max_val=N_EXPERTS - 1)
                                      for q in range(TURN)]
                        turn_loads(j + MOE_TURNS, lambda q: L * N_EXPERTS + experts_of[q])
                sp.sem_inc(sem["layer_end"], 1)
            for t in range(T):
                sp.wait_ge(combined, DEPTH * T + t + 1)
                sp.dma_start(out[0, t * P:(t + 1) * P, :], X[:, t, :]).then_inc(out_done, 16)
            sp.wait_ge(out_done, T * 16)

        @block.tensor
        def _(pe):
            pe.sem_inc(w_used, U_LAYER)
            pe.wait_ge(consts_in, 5 * 16)
            pe.wait_ge(table_in, 16)
            with pe.Fori(0, DEPTH) as L:
                state = {"n": 0}
                extra_before = pe.value_load(table[0:1, bass.ds(L + TAB_BEFORE, 1)], min_val=0, max_val=DEPTH * MAX_EXTRA)

                def full(name):
                    slot = SLOT[name]
                    a, b = slot_loads(slot)
                    pe.wait_ge(slot_full[slot], L * (16 * (a + MOE_TURNS * b)) + extra_before * (16 * b)
                               + 16 * loads_so_far(UNITS, SLOT, name))
                    return ring[:, slot, :]

                def open_bank(*name):
                    n = state["n"]
                    assert PRODUCTS[n] == name, (PRODUCTS[n], name)
                    state["n"] = n + 1
                    if n >= BANKS:
                        emptied(pe, sem, *PRODUCTS[n - BANKS])
                    return banks[n % BANKS]

                def close(last):
                    last.then_inc(sem["product"], 1)

                def group(bank, pairs):
                    for n, (a, b) in enumerate(pairs):
                        last = nc.tensor.matmul(bank, a, b, start=n == 0, stop=n == len(pairs) - 1)
                    return last

                def transposes(name, tiles, wait=None, used=None):
                    bank = open_bank(*name)
                    for n, tile in enumerate(tiles):
                        last = nc.tensor.transpose(bank[:, n * P:(n + 1) * P], tile, idn)
                    close(last)

                def used():
                    pe.wait_ge(sem["product"], state["n"])
                    pe.sem_inc(w_used, 1)

                def token_product(name, t, w, width, source=HT, steps=K):
                    bank = open_bank(*name)
                    close(group(bank[:, 0:width],
                                [(source[:, k, t * P:(t + 1) * P], w[:, k, :]) for k in range(steps)]))

                def norm_transposes(key, t, tiles_before, source=XN):
                    pe.wait_ge(sem["x_scaled"], tiles_before + t + 1)
                    for n in range(2):
                        transposes((key, t, n), [source[:, t, 4 * n + k, :] for k in range(4)])

                pe.wait_ge(mem_scaled, L * M + M)
                for j in range(K // 2):
                    transposes(("mT", j), [MN[m][:, k, :] for k in (2 * j, 2 * j + 1) for m in range(M)])
                emptied(pe, sem, "mT", K // 2 - 1)
                wk = full("kx").rearrange("p (k n) -> p k n", k=K)
                for m in range(M):
                    token_product(("kx", m), m, wk, WIDTH, MT)
                used()
                wv = full("vx").rearrange("p (k n) -> p k n", k=K)
                for m in range(M):
                    token_product(("vx", m), m, wv, WIDTH, MT)
                used()
                for m in range(M):
                    pe.wait_ge(sem["kx_ready"], m + 1)
                    transposes(("kxT", m), [TOK[:, m, h * P:(h + 1) * P] for h in range(HEADS)])
                wql = full("ql")[:, 0:K * N_QL].rearrange("p (k n) -> p k n", k=K)

                def latent(t):
                    emptied(pe, sem, "hT", t, 1)
                    token_product(("ql", t), t, wql, N_QL)
                for t in range(T):
                    norm_transposes("hT", t, 0)
                    if t:
                        latent(t - 1)
                latent(T - 1)
                used()
                pe.wait_ge(sem["c_ready"], T)
                for c in range(2):
                    transposes(("cT", c), [C[:, t, c * P:(c + 1) * P] for t in range(T)])
                pe.wait_ge(sem["ki_ready"], T)
                transposes(("kiT",), [KIN[:, t, :] for t in range(T)])
                wl = full("lora")
                wqb = wl[:, 0:1024].rearrange("p (k n) -> p k n", k=2)
                wqi = wl[:, 1024:3072].rearrange("p (k n) -> p k n", k=2)
                emptied(pe, sem, "cT", 1)
                for t in LATER:
                    for n in range(2):
                        token_product(("qi", t, n), t, wqi[:, :, n * 512:(n + 1) * 512], 512, CT, 2)

                def tok_transposes(key, t):
                    pe.wait_ge(sem[key + "_ready"], t + 1)
                    transposes((key + "T", t), [TOK[:, t % 2, h * P:(h + 1) * P] for h in range(HEADS)])
                wkb = full("kb").rearrange("p (k n) -> p k n", k=K)
                for t in range(T):
                    token_product(("kb", t), t, wkb, WIDTH)
                    if t:
                        tok_transposes("kb", t - 1)
                used()
                wvb = full("vb").rearrange("p (k n) -> p k n", k=K)
                token_product(("vb", 0), 0, wvb, WIDTH)
                tok_transposes("kb", T - 1)
                for t in range(T):
                    token_product(("qb", t), t, wqb, WIDTH, CT, 2)
                    if t:
                        tok_transposes("qb", t - 1)
                    if t + 1 < T:
                        token_product(("vb", t + 1), t + 1, wvb, WIDTH)
                pe.wait_ge(sem["product"], state["n"])
                pe.sem_inc(w_used, 2)
                for t in LATER:
                    pe.wait_ge(sem["qi_ready"], t)
                    for n in range(2):
                        transposes(("qiT", t, n), [QI[:, t - 1, g * P:(g + 1) * P] for g in range(4 * n, 4 * n + 4)])
                tok_transposes("qb", T - 1)
                emptied(pe, sem, "kiT")
                for t in LATER:
                    for h in range(IDX_HEADS):
                        if h % 8 == 0:
                            emptied(pe, sem, "qiT", t, h // 8)
                        part = slice(64 * (h % 2), 64 * (h % 2) + 64)
                        bank = open_bank("si", t, h)
                        close(nc.tensor.matmul(bank[:, 0:(t + 1) * P], QIT[part, t - 1, h // 2, :],
                                               KIT[part, 0:(t + 1) * P], start=True, stop=True))
                w = full("vA").rearrange("p (k n) -> p k n", k=K)
                for t in range(T):
                    token_product(("vA", t), t, w, WIDTH)
                used()

                wf = full("f").rearrange("p (k n) -> p k n", k=K)
                wq = full("q").rearrange("p (k n) -> p k n", k=K)

                def channel_product(name, w, h):
                    bank = open_bank(name, h)
                    close(group(bank, [(w[:, k, h * P:(h + 1) * P], HT[:, k, :]) for k in range(K)]))

                def channel_steps(name, w, h, pair):
                    n = PRODUCTS.index((name, h))
                    if pair == 0:
                        emptied(pe, sem, *PRODUCTS[n - BANKS])
                    for k in (2 * pair, 2 * pair + 1):
                        nc.tensor.matmul(banks[n % BANKS], w[:, k, h * P:(h + 1) * P], HT[:, k, :],
                                                start=k == 0, stop=k == K - 1)
                channel_product("f", wf, 0)
                channel_product("q", wq, 0)
                wg = full("g").rearrange("p (k n) -> p k n", k=K)
                token_product(("g", 0), 0, wg, WIDTH)
                for h in range(HEADS):
                    for n in range(LEVELS + 1):
                        a, b = (KLS[n % 2], QLS[n % 2]) if n < LEVELS else (KK, QQ)
                        if h + 1 < HEADS:
                            name, w = (("f", wf), ("q", wq))[n // (K // 2)]
                            channel_steps(name, w, h + 1, n % (K // 2))
                        if n < LEVELS:
                            pe.wait_ge(sem["qL"], h * LEVELS + n + 1)
                            pe.wait_ge(sem["kL"], h * LEVELS + n + 1)
                        if n == LEVELS:
                            pe.wait_ge(sem["kd_ready"], h + 1)
                            transposes(("kdT", h), [XX[:, t * P:(t + 1) * P] for t in range(T)])
                        bank = open_bank("lv", h, n)
                        for t in range(T):
                            s = slice(t * P, (t + 1) * P)
                            last = nc.tensor.matmul(bank[:, s], a[:, s], b[:, s], start=True, stop=True)
                        if h + 1 < HEADS and n in BESIDE:
                            assert PRODUCTS[state["n"]] == (name, h + 1)
                            state["n"] += 1
                            last.then_inc(sem["product"], 2)
                        else:
                            close(last)
                    emptied(pe, sem, "kdT", h)
                    bank = open_bank("dS", h)
                    values = [VAt[:, t, h * P:(h + 1) * P] for t in range(T)]
                    for t in range(T - 1):
                        last = nc.tensor.matmul(bank[:, t * P:(t + 1) * P], KDT[:, t * P:(t + 1) * P], values[t],
                                                start=True, stop=True)
                    close(last)
                    bank = open_bank("o", h)
                    emptied(pe, sem, "lv", h, LEVELS)
                    for t in range(T):
                        s = slice(t * P, (t + 1) * P)
                        nc.tensor.matmul(bank[:, s], SCT[:, s], values[t], start=t == 0, stop=False)
                    pe.wait_ge(sem["qe_ready"], h + 1)
                    emptied(pe, sem, "dS", h)
                    for t in range(1, T):
                        s = slice(t * P, (t + 1) * P)
                        last = nc.tensor.matmul(bank[:, s], QL[:, s], ST[:, t, :], start=False, stop=t == T - 1)
                    close(last)
                    if h + 1 < HEADS:
                        token_product(("g", h + 1), h + 1, wg, WIDTH)
                pe.wait_ge(sem["product"], PRODUCTS.index(("g", T - 1)) + 1)
                pe.sem_inc(w_used, 3)
                for t in range(T):
                    pe.wait_ge(sem["og_ready"], t + 1)
                    transposes(("oaT", t), [O[:, t, h * P:(h + 1) * P] for h in range(HEADS)])

                def logits(m):
                    t, h = divmod(m, HEADS)
                    bank = open_bank("lg", m)
                    close(nc.tensor.matmul(bank[:, 0:(t + 1) * P], QT[:, h, t * P:(t + 1) * P],
                                           KT[:, h, 0:(t + 1) * P], start=True, stop=True))

                def attend(m):
                    t, h = divmod(m, HEADS)
                    bank = open_bank("pv", m)
                    emptied(pe, sem, "pT", m)
                    close(group(bank[:, 0:P], [(VBt[:, s, h * P:(h + 1) * P], PT[:, m % 2, s * P:(s + 1) * P])
                                               for s in range(t + 1)]))

                def project(m):
                    t, n, pair = m // 4, m // 2 % 2, m % 2
                    bank = open_bank("xa", m)
                    close(group(bank, [(OAB[:, k, t * P:(t + 1) * P], wa[:, k, n * 512:(n + 1) * 512])
                                       for k in (2 * pair, 2 * pair + 1)]))
                logits(0)
                logits(1)
                wa = full("outA").rearrange("p (k n) -> p k n", k=4)
                emptied(pe, sem, "oaT", T - 1)
                for m in range(T * HEADS):
                    pe.wait_ge(sem["probs"], m + 1)
                    transposes(("pT", m), [PR[:, m % 2, s * P:(s + 1) * P] for s in range(m // HEADS + 1)])
                    if m + 2 < T * HEADS:
                        logits(m + 2)
                    if m:
                        attend(m - 1)
                    project(m)
                attend(T * HEADS - 1)

                pe.wait_ge(sem["product"], PRODUCTS.index(("xa", T * HEADS - 1)) + 1)
                pe.sem_inc(w_used, 1)
                wb = full("outB").rearrange("p (k n) -> p k n", k=4)
                emptied(pe, sem, "pv", T * HEADS - 1)
                for t in range(T):
                    for n in range(2):
                        bank = open_bank("xo", t, n)
                        close(group(bank, [(OAB[:, HEADS + k, t * P:(t + 1) * P], wb[:, k, n * 512:(n + 1) * 512])
                                           for k in range(HEADS)]))
                    if t:
                        norm_transposes("hxT", t - 1, T, XNX)
                pe.wait_ge(sem["product"], PRODUCTS.index(("xo", T - 1, 1)) + 1)
                pe.sem_inc(w_used, 1)

                w = full("xq").rearrange("p (k n) -> p k n", k=K)

                def qx_transposes(t):
                    pe.wait_ge(sem["qx_ready"], t + 1)
                    transposes(("qxT", t), [TOK[:, t % 2, h * P:(h + 1) * P] for h in range(HEADS)])
                for t in range(T):
                    emptied(pe, sem, "hxT", t, 1)
                    token_product(("qx", t), t, w, WIDTH)
                    if t:
                        qx_transposes(t - 1)
                    else:
                        norm_transposes("hxT", T - 1, T, XNX)
                used()
                qx_transposes(T - 1)

                def logits_x(m):
                    t, j = divmod(m, 2)
                    emptied(pe, sem, "qxT", t)
                    bank = open_bank("lx", m)
                    for a in range(2):
                        h = 2 * j + a
                        last = nc.tensor.matmul(bank[:, a * N_MEM:(a + 1) * N_MEM], QT[:, h, t * P:(t + 1) * P],
                                                KXT[:, h, :], start=True, stop=True)
                    close(last)

                def attend_x(t):
                    emptied(pe, sem, "pxT", 2 * t + 1)
                    bank = open_bank("px", t)
                    for h in range(HEADS):
                        j, a = divmod(h, 2)
                        last = group(bank[:, h * P:(h + 1) * P],
                                     [(VX[:, m, h * P:(h + 1) * P], PT[:, j, (2 * a + m) * P:(2 * a + m + 1) * P])
                                      for m in range(M)])
                    close(last)
                wxo = full("xo").rearrange("p (k n) -> p k n", k=4)

                def project_x(m):
                    t, n = divmod(m, 2)
                    emptied(pe, sem, "px", t)
                    bank = open_bank("xx", t, n)
                    close(group(bank, [(OXT[:, h, t * P:(t + 1) * P], wxo[:, h, n * 512:(n + 1) * 512])
                                       for h in range(HEADS)]))
                logits_x(0)
                logits_x(1)
                for m in range(2 * T):
                    pe.wait_ge(sem["probs_x"], m + 1)
                    transposes(("pxT", m), [PR[:, m % 2, s * P:(s + 1) * P] for s in range(4)])
                    if m + 2 < 2 * T:
                        logits_x(m + 2)
                    if m and m % 2 == 0:
                        attend_x(m // 2 - 1)
                    if m >= 3:
                        project_x(m - 3)
                attend_x(T - 1)
                for t in range(3):
                    project_x(2 * T - 3 + t)
                    norm_transposes("hfT", t, 2 * T)
                pe.wait_ge(sem["product"], PRODUCTS.index(("xx", T - 1, 1)) + 1)
                pe.sem_inc(w_used, 1)

                at = PRODUCTS.index(("rt",))
                emptied(pe, sem, *PRODUCTS[at - BANKS])
                for t in range(T):
                    if t == T - 1:
                        norm_transposes("hfT", t, 2 * T)
                        open_bank("rt")
                    emptied(pe, sem, "hfT", t, 1)
                    last = group(banks[at % BANKS][:, t * N_ROUTE:(t + 1) * N_ROUTE],
                                 [(HT[:, k, t * P:(t + 1) * P], wr_sb[:, k, :]) for k in range(K)])
                close(last)
                pe.wait_ge(sem["chosen"], 1)
                bank = open_bank("rank")
                picks = chosen.rearrange("p t e -> p (t e)")
                nc.tensor.matmul(bank[:, 0:64], tri, picks, start=True, stop=True)
                close(nc.tensor.matmul(bank[:, 64:128], ones, picks, start=True, stop=True))
                assert state["n"] == len(PRODUCTS)
                for name in PRODUCTS[-BANKS:]:
                    emptied(pe, sem, *name)

                pe.wait_ge(sem["slots_ready"], 2)
                pe.sem_inc(sem["in_moe"], 1)
                more_turns = pe.value_load(table[0:1, TAB_TURNS:TAB_TURNS + 1], min_val=MOE_TURNS - 1,
                                           max_val=MOE_TURNS - 1 + MAX_EXTRA)
                made = sem["moe_product"]

                def moe_full(i, q, kind):
                    name = f"gu{q}" if kind == "gu" else f"dn{q // 2}"
                    slot = MOE_SLOT[name]
                    a, b = slot_loads(slot)
                    pe.wait_ge(slot_full[slot], L * (16 * (a + MOE_TURNS * b)) + extra_before * (16 * b) + i * (16 * b)
                               + 16 * (a + loads_so_far(MOE_UNITS, MOE_SLOT, name)))
                    return ring[:, slot, :] if kind == "gu" else DN[q // 2][:, (q % 2) * 2048:(q % 2 + 1) * 2048]

                def tokens_transposed(i, q, at):
                    pe.wait_ge(x_in[q % TURN], L * (MOE_TURNS * 16) + extra_before * 16 + i * 16 + (q // TURN + 1) * 16)
                    for n in range(2):
                        if q > 1:
                            pe.wait_ge(sem["moe_dve_emptied"], i * (TURN * D_TILE) + D_TILE * (q - 1)
                                       + (MOE_D["hT"] - 2 * D_TILE, MOE_D["gu"] - D_TILE)[n])
                        bank = banks[(at + n) % BANKS]
                        for k in range(4):
                            last = nc.tensor.transpose(bank[:, k * P:(k + 1) * P],
                                                       XB[:, q % TURN, (4 * n + k) * P:(4 * n + k + 1) * P], idn)
                        last.then_inc(made, 1)

                def first_layer(i, q, at):
                    w = moe_full(i, q % TURN, "gu") if q < TURN else moe_full(i + 1, 0, "gu")
                    w = w.rearrange("p (k n) -> p k n", k=K)
                    pe.wait_ge(sem["moe_dve_emptied"], i * (TURN * D_TILE) + (D_TILE * q + MOE_D["xT1"] if q else 2))
                    if q:
                        pe.wait_ge(sem["moe_act_emptied"], i * (TURN * A_TILE) + A_TILE * (q - 2) + A_AHEAD)
                    group(banks[at % BANKS], [(XT[:, q % 2, k, :], w[:, k, :]) for k in range(K)]).then_inc(made, 1)

                def hidden_transposed(i, q, at):
                    pe.wait_ge(sem["moe_dve_emptied"], i * (TURN * D_TILE) + D_TILE * q + MOE_D["gu"])
                    if q:
                        pe.wait_ge(sem["moe_act_emptied"], i * (TURN * A_TILE) + A_TILE * (q - 2) + 1 + A_AHEAD)
                    for f in range(2):
                        last = nc.tensor.transpose(banks[at % BANKS][:, f * P:(f + 1) * P],
                                                   HID[:, q % 2, f * P:(f + 1) * P], idn)
                    last.then_inc(made, 1)

                def second_layer(i, q, at, last_count):
                    w = moe_full(i, q, "dn").rearrange("p (k d) -> p k d", k=2)
                    pe.wait_ge(sem["moe_dve_emptied"], i * (TURN * D_TILE) + last_count)
                    for n in range(2):
                        group(banks[(at + n) % BANKS], [(HIDT[:, q % 2, f, :], w[:, f, n * 512:(n + 1) * 512])
                                                        for f in range(2)]).then_inc(made, 1)

                def unit_used(i, count):
                    pe.wait_ge(made, i * (TURN * PER_TILE) + count)
                    pe.sem_inc(w_used, 1)

                def tile(i, q, last=False):
                    at = PER_TILE * q if q else 2
                    first_layer(i, q, at)
                    if not last:
                        tokens_transposed(i, q + 1, at + 1)
                    unit_used(i, at + 1)
                    y_at = at + 1 if last else at + 3
                    if q:
                        second_layer(i, q - 1, y_at, D_TILE * (q - 1) + MOE_D["hT"])
                    h_at = y_at + 2 if q else 5
                    hidden_transposed(i, q, h_at)
                    if q and q % 2 == 0:
                        unit_used(i, y_at + 2)
                    if last:
                        second_layer(i, q, h_at + 1, D_TILE * q + MOE_D["hT"] - 2)
                        unit_used(i, PER_TILE * TURN)
                tokens_transposed(0, 0, 0)
                tile(0, 0)
                with pe.Fori(0, more_turns) as i:
                    for q in range(1, TURN + 1):
                        tile(i, q)
                for q in range(1, TURN):
                    tile(more_turns, q, last=q == TURN - 1)
                pe.sem_inc(sem["layer_end"], 1)
                pe.wait_ge(cleared, L + 1)

        @block.scalar
        def _(act):
            own0 = Own(act, pro_act)
            act.wait_ge(cols_in, 16)
            act.dma_start(X, x.rearrange("b (t p) d -> p (b t) d", p=P)).then_inc(x_loaded, 16)
            act.wait_ge(mem_in, 16)
            for m in range(M):
                own0.done(nc.scalar.activation(PTMP, MEMX[:, m, :], ACT.Square, scale=D_MODEL ** -0.5,
                                               accum_out=ss_m[:, m:m + 1]))
                own0.need()
            own0.done(nc.scalar.activation(rn_m, ss_m, ACT.Ln, bias=EPS))
            own0.need()
            own0.done(nc.scalar.activation(rn_m, rn_m, ACT.Exp, scale=-0.5))
            own0.need()

            def scale_memory():
                for m in range(M):
                    nc.scalar.activation(MN[m], MEMX[:, m, :].rearrange("p (d k) -> p k d", k=K), ACT.Copy,
                                         scale=rn_m[:, m:m + 1]).then_inc(mem_scaled, 1)
            scale_memory()
            act.wait_ge(ropes, 1)
            own0.done(nc.scalar.activation(KIN[:, :, 0:96], KIN[:, :, 0:96], ACT.Sin))
            own0.done(nc.scalar.activation(HT[:, 0:T, 0:96], HT[:, 0:T, 0:96], ACT.Sin))
            own0.done(nc.scalar.activation(lb_all, lb_all, ACT.Exp))
            act.wait_ge(table_in, 16)
            with act.Fori(0, DEPTH) as L:
                extra_before = act.value_load(table[0:1, bass.ds(L + TAB_BEFORE, 1)], min_val=0, max_val=DEPTH * MAX_EXTRA)
                own = Own(act, sem["act_own"])
                em = Emptier(act, "act", sem, banks)
                act.dma_start(rows, rowparams[bass.ds(L, 1), :].rearrange("l n -> (l n)").partition_broadcast(P))\
                    .then_inc(sem["params"], 16)
                act.dma_start(wr_sb, w_re.rearrange("l (p k) n -> (l p) k n", k=K)[bass.ds(L * P, P), :, :])\
                    .then_inc(sem["params"], 16)
                act.wait_ge(consts_in, 5 * 16)
                act.preload_act_table_set("natural_log_exp_and_others")

                def squares(src, scale, dst, junk):
                    own.need()
                    own.done(nc.scalar.activation(junk, src, ACT.Square, scale=scale, accum_out=dst))

                def reciprocal_norm(ss, rn, signal):
                    own.need()
                    own.done(nc.scalar.activation(rn, ss, ACT.Ln, bias=EPS))
                    own.need()
                    nc.scalar.activation(rn, rn, ACT.Exp, scale=-0.5).then_inc(sem[signal], 1)

                def head_norms(src, slot, signal):
                    for h in range(HEADS):
                        squares(src[:, h * P:(h + 1) * P], SCALE, ss_h[:, slot, h:h + 1], JUNK[:, 0:P])
                    reciprocal_norm(ss_h[:, slot, :], rn_h[:, slot, :], signal)

                def token_norms(junk):
                    def tile(t):
                        squares(X[:, t, :], D_MODEL ** -0.5, ss_x[:, t:t + 1], junk)
                        reciprocal_norm(ss_x[:, t:t + 1], rn_x[:, t:t + 1], "rn_x")
                    return tile

                def copy(dst, bank, *name, scale=None):
                    ins = nc.scalar.activation(dst, bank, ACT.Copy) if scale is None else \
                        nc.scalar.activation(dst, bank, ACT.Identity, scale=scale)
                    em.empty(ins, *name)

                def heads_of(bank):
                    return bank.rearrange("p (h t) -> p h t", h=HEADS)

                norm_tile = token_norms(PTMP)
                act.wait_ge(cols_in, 16)
                nc.scalar.activation(cols, cols_all.rearrange("p l n -> p (l n)")[:, bass.ds(L * N_COL, N_COL)], ACT.Copy)\
                    .then_inc(sem["cols_ready"], 1)
                act.wait_ge(sem["cols_ready"], 1)
                for j in range(K // 2):
                    bank = em.take("mT", j)
                    own.done(nc.scalar.activation(MT[:, 2 * j, :], bank[:, 0:N_MEM], ACT.Identity,
                                                  scale=cols[:, G_MEM + 2 * j:G_MEM + 2 * j + 1]))
                    copy(MT[:, 2 * j + 1, :], bank[:, N_MEM:2 * N_MEM], "mT", j,
                         scale=cols[:, G_MEM + 2 * j + 1:G_MEM + 2 * j + 2])

                def head_tile(key, t, slot):
                    bank = em.take(key, t)
                    copy(TOK[:, slot, :], bank, key, t)
                    act.wait_ge(sem["act_emptied"], em.count)
                    head_norms(TOK[:, slot, :], slot, "rn_" + key)
                for m in range(M):
                    head_tile("kx", m, m)
                for t in range(T):
                    act.wait_ge(combined, L * T + t + 1)
                    norm_tile(t)
                for m in range(M):
                    copy(VX[:, m, :], em.take("vx", m), "vx", m)
                for m in range(M):
                    copy(KXT[:, :, m * P:(m + 1) * P], heads_of(em.take("kxT", m)), "kxT", m,
                         scale=cols[:, G_XK:G_XK + 1])
                act.wait_ge(mem_scaled, L * M + M)
                for t in range(T):
                    bank = em.take("ql", t)
                    own.done(nc.scalar.activation(C[:, t, :], bank[:, 0:Q_LORA], ACT.Copy))
                    copy(KI[:, t, :], bank[:, Q_LORA:N_QL], "ql", t)
                    squares(C[:, t, :], Q_LORA ** -0.5, ss_ql[:, t, 0:1], JUNK[:, 0:Q_LORA])
                    act.wait_ge(sem["act_emptied"], em.count)
                    squares(KI[:, t, 0:IDX_DIM], IDX_DIM ** -0.5, ss_ql[:, t, 1:2], JUNK[:, 0:IDX_DIM])
                    reciprocal_norm(ss_ql[:, t, :], rn_ql[:, t, :], "rn_ql")
                for c in range(2):
                    copy(CT[:, c, :], em.take("cT", c), "cT", c, scale=cols[:, G_QLAT + c:G_QLAT + c + 1])
                copy(KIT, em.take("kiT"), "kiT")
                for t in LATER:
                    for n in range(2):
                        copy(QI[:, t - 1, n * 512:(n + 1) * 512], em.take("qi", t, n), "qi", t, n)
                def transposed_tile(key, dst, t):
                    copy(dst[:, :, t * P:(t + 1) * P], heads_of(em.take(key + "T", t)), key + "T", t)

                def values(t):
                    copy(VBt[:, t, :], em.take("vb", t), "vb", t)
                for t in range(T):
                    head_tile("kb", t, t % 2)
                    if t:
                        transposed_tile("kb", KT, t - 1)
                values(0)
                transposed_tile("kb", KT, T - 1)
                for t in range(T):
                    head_tile("qb", t, t % 2)
                    if t:
                        transposed_tile("qb", QT, t - 1)
                    if t + 1 < T:
                        values(t + 1)
                for t in LATER:
                    for n in range(2):
                        copy(QIT[:, t - 1, 4 * n:4 * n + 4, :],
                             em.take("qiT", t, n).rearrange("p (g t) -> p g t", g=4), "qiT", t, n)
                transposed_tile("qb", QT, T - 1)
                for t in LATER:
                    for h in range(IDX_HEADS):
                        n = (t - 1) * IDX_HEADS + h
                        bank = em.take("si", t, h)
                        if n >= 2:
                            act.wait_ge(sem["relu_used"], n - 1)
                        em.empty(nc.scalar.activation(RELU[:, n % 2, 0:(t + 1) * P], bank[:, 0:(t + 1) * P], ACT.Relu),
                                 "si", t, h)
                for t in range(T):
                    copy(VAt[:, t, :], em.take("vA", t), "vA", t)

                act.wait_ge(sem["lb_ready"], 1)

                def forget(h):
                    bank = em.take("f", h)
                    if h:
                        act.wait_ge(sem["b_ready"], h)
                    em.empty(nc.scalar.activation(E1, bank, ACT.Exp, scale=-1.0), "f", h)
                    act.wait_ge(sem["act_emptied"], em.count)
                    own.done(nc.scalar.activation(L1, E1, ACT.Ln, bias=1.0))
                    own.done(nc.scalar.activation(L2, E1, ACT.Ln, bias=1.0, scale=lb[:, h:h + 1]))
                    own.need()
                    nc.scalar.activation(S1, L1, ACT.Exp, scale=-1.0).then_inc(sem["forget"], 1)

                def queries(h):
                    bank = em.take("q", h)
                    if h:
                        act.wait_ge(sem["kd_ready"], h)
                    own.done(nc.scalar.activation(EQ, bank, ACT.Exp, scale=-1.0))
                    own.need()
                    own.done(nc.scalar.activation(EQ, EQ, ACT.Ln, bias=1.0))
                    own.need()
                    nc.scalar.activation(EQ, EQ, ACT.Exp, scale=-1.0).then_inc(sem["queries"], 1)
                forget(0)
                queries(0)

                def gate(t):
                    bank = em.take("g", t)
                    if t:
                        act.wait_ge(sem["g_ready"], t)
                    own.done(nc.scalar.activation(SIGMA, bank, ACT.Exp, scale=-1.0))
                    copy(G[:, t, :], bank, "g", t)
                    own.need()
                    own.done(nc.scalar.activation(SIGMA, SIGMA, ACT.Ln, bias=1.0))
                    own.need()
                    nc.scalar.activation(SIGMA, SIGMA, ACT.Exp, scale=-1.0).then_inc(sem["sigma_g"], 1)
                gate(0)
                for h in range(HEADS):
                    for n, half in enumerate(HALVES):
                        d = (DE, EQ)[n % 2].rearrange("p (b two i) -> p b two i", two=2, i=half)
                        act.wait_ge(sem["diff"], h * (LEVELS + 1) + n + 1)
                        own.done(nc.scalar.activation(d[:, :, 0, :], d[:, :, 0, :], ACT.Exp, scale=-1.0))
                        nc.scalar.activation(d[:, :, 1, :], d[:, :, 1, :], ACT.Exp).then_inc(sem["decay"], 1)
                        if h and n == 1:
                            gate(h)
                        if h + 1 < HEADS and n == K // 2 + 1:
                            forget(h + 1)
                    act.wait_ge(sem["diff"], (h + 1) * (LEVELS + 1))
                    act.wait_ge(sem["kL"], (h + 1) * LEVELS)
                    act.wait_ge(sem["qL"], (h + 1) * LEVELS)
                    own.done(nc.scalar.activation(DE, BB, ACT.Exp))
                    own.done(nc.scalar.activation(e_end, BB.rearrange("p (t i) -> p t i", t=T)[:, :, P - 1], ACT.Exp))
                    nc.scalar.activation(EQ, EQ, ACT.Exp, scale=-1.0).then_inc(sem["ends"], 1)
                    copy(KDT, em.take("kdT", h), "kdT", h)
                    if h + 1 < HEADS:
                        queries(h + 1)
                    copy(O[:, :, h * P:(h + 1) * P], em.take("o", h).rearrange("p (t n) -> p t n", t=T), "o", h)
                act.wait_ge(sem["act_emptied"], em.count)
                for t in range(T):
                    if t >= 2:
                        act.wait_ge(sem["og_ready"], t - 1)
                    head_norms(O[:, t, :], t % 2, "rn_o")
                for t in range(T):
                    copy(OAB[:, 0:HEADS, t * P:(t + 1) * P], heads_of(em.take("oaT", t)), "oaT", t,
                         scale=cols[:, G_AG:G_AG + 1])

                for m in range(T * HEADS + 1):
                    w = (m // HEADS + 1) * P
                    if m < T * HEADS:
                        act.wait_ge(sem["logits"], m + 1)
                        nc.scalar.activation(PR[:, m % 2, 0:w], PR[:, m % 2, 0:w], ACT.Exp, bias=mx[:, m % 4, 0:1],
                                             accum_out=sm[:, m % 4, 0:1]).then_inc(sem["exps"], 1)
                    if m:
                        w = ((m - 1) // HEADS + 1) * P
                        copy(PT[:, (m - 1) % 2, 0:w], em.take("pT", m - 1)[:, 0:w], "pT", m - 1)
                act.wait_ge(sem["act_emptied"], em.count)

                norm_tile = token_norms(CB[:, 0:1024])
                for t in range(T):
                    emptied(act, sem, "xo", t, 1)
                    if t == 0:
                        act.wait_ge(sem["dve_emptied"], EMPTIED["dve"].index(("pv", T * HEADS - 1)) + 1)
                    norm_tile(t)
                for t in range(T + 1):
                    if t < T:
                        head_tile("qx", t, t % 2)
                    if t:
                        copy(QT[:, :, (t - 1) * P:t * P], heads_of(em.take("qxT", t - 1)), "qxT", t - 1,
                             scale=cols[:, G_XQ:G_XQ + 1])
                px = 0
                for m in range(2 * T):
                    act.wait_ge(sem["max_x"], m + 1)
                    bank = em.take("lx", m)
                    if m >= 2:
                        em.take("pxT", m - 2)
                    for a in range(2):
                        s = slice(a * N_MEM, (a + 1) * N_MEM)
                        ins = nc.scalar.activation(PR[:, m % 2, s], bank[:, s], ACT.Exp, bias=mx[:, m % 4, a:a + 1],
                                                   scale=SCALE, accum_out=sm[:, m % 4, a:a + 1])
                        if a:
                            em.empty(ins, "lx", m)
                        else:
                            own.done(ins)
                    if m >= 4 and m % 2 == 0:
                        copy(OXT[:, :, px * P:(px + 1) * P], heads_of(em.take("px", px)), "px", px)
                        px += 1
                while px < T:
                    copy(OXT[:, :, px * P:(px + 1) * P], heads_of(em.take("px", px)), "px", px)
                    px += 1
                act.wait_ge(sem["act_emptied"], em.count)

                for t in range(T):
                    emptied(act, sem, "xx", t, 1)
                    norm_tile(t)
                act.wait_ge(sem["router_logits"], 1)
                nc.scalar.activation(rw[:, 1], rw[:, 1], ACT.Exp).then_inc(sem["router_exp"], 1)
                act.wait_ge(sem["router_logits"], 2)
                nc.scalar.activation(rw[:, 8, :, 0], rw[:, 8, :, 0], ACT.Exp).then_inc(sem["router_exp"], 1)
                assert em.count == len(EMPTIED["act"])
                act.wait_ge(sem["router_exp"], 2)

                act.dma_start(MEMX, mem.rearrange("b (m p) d -> p (b m) d", p=P)).then_inc(mem_in, 16)
                act.wait_ge(mem_in, L * 16 + 32)
                scale_memory()
                act.sem_inc(sem["moe_act_emptied"], A_AHEAD)
                act.wait_ge(sem["slots_ready"], 2)
                act.sem_inc(sem["in_moe"], 1)
                more_turns = act.value_load(table[0:1, TAB_TURNS:TAB_TURNS + 1], min_val=MOE_TURNS - 1,
                                            max_val=MOE_TURNS - 1 + MAX_EXTRA)

                def silu(i, q):
                    at = PER_TILE * q if q else 2
                    act.wait_ge(sem["moe_product"], i * (TURN * PER_TILE) + at + 1)
                    nc.scalar.activation(SILU[:, q % 2, :], banks[at % BANKS][:, 0:D_EXPERT], ACT.Silu)\
                        .then_inc(sem["silu"], 1)

                def output(i, q, at):
                    act.wait_ge(y_out[q % 2], L * (MOE_TURNS * 32) + extra_before * 32 + i * 32 + q // 2 * 16 + 16)
                    for n in range(2):
                        act.wait_ge(sem["moe_product"], i * (TURN * PER_TILE) + at + n + 1)
                        nc.scalar.activation(YB[:, q % 2, n * 512:(n + 1) * 512], banks[(at + n) % BANKS], ACT.Copy)\
                            .then_inc(sem["moe_act_emptied"], 1)
                silu(0, 0)
                with act.Fori(0, more_turns) as i:
                    for q in range(1, TURN + 1):
                        silu(i, q)
                        output(i, q - 1, PER_TILE * q + 3)
                for q in range(1, TURN):
                    silu(more_turns, q)
                    output(more_turns, q - 1, PER_TILE * q + (1 if q == TURN - 1 else 3))
                output(more_turns, TURN - 1, PER_TILE * (TURN - 1) + 4)
                act.wait_ge(sem["moe_act_emptied"], more_turns * (TURN * A_TILE) + TURN * A_TILE + A_AHEAD)
                act.sem_inc(sem["layer_end"], 1)
                act.wait_ge(cleared, L + 1)

        @block.gpsimd
        def _(pool):
            zeros_tile = SC[:, 1:3, :].rearrange("p t n -> p (t n)")
            nc.gpsimd.memset(zeros_tile, 0.0).then_inc(zero_tile, 1)
            pool.wait_ge(zero_tile, 1)
            pool.wait_ge(w_used, U_LAYER + 2)
            for n in range(0, TILES, FILL):
                pool.dma_start(XG[n * P:(n + FILL) * P, :].rearrange("(n p) d -> p n d", p=P), over(zeros_tile, FILL))\
                    .then_inc(zero_filled, 16)
            for n in range(2):
                some = (TILES - N_EXPERTS) // 2
                at = (N_EXPERTS + n * some) * P
                pool.dma_start(YG[at:at + some * P, :].rearrange("(n p) d -> p n d", p=P), over(zeros_tile, some))\
                    .then_inc(y_out[n], 16)
            pool.wait_ge(table_in, 16)
            with pool.Fori(0, DEPTH) as L:
                extra_before = pool.value_load(table[0:1, bass.ds(L + TAB_BEFORE, 1)], min_val=0, max_val=DEPTH * MAX_EXTRA)
                own = Own(pool, sem["pool_own"])
                pool.wait_ge(prologue, 1)
                for t in LATER:
                    emptied(pool, sem, "qi", t, 1)
                    q = QI[:, t - 1, :].rearrange("p (h two i) -> p h two i", h=IDX_HEADS, two=2)
                    r = PTMP.rearrange("p (h two i) -> p h two i", h=IDX_HEADS, two=2)
                    if t == LATER[0]:
                        pool.wait_ge(sem["rn_x"], T)
                    own.need() if own.count else None
                    for a in range(2):
                        own.done(nc.gpsimd.tensor_tensor(r[:, :, a, :], q[:, :, 1 - a, :],
                                                         over(sin_i[:, t, a, :], IDX_HEADS), ALU.mult))
                    own.need()
                    for a in range(2):
                        own.done(nc.gpsimd.tensor_tensor(q[:, :, a, :], q[:, :, a, :],
                                                         over(cos_i[:, t, :], IDX_HEADS), ALU.mult))
                    own.need()
                    nc.gpsimd.tensor_tensor(QI[:, t - 1, :], QI[:, t - 1, :], PTMP, ALU.add).then_inc(sem["qi_ready"], 1)
                    pool.wait_ge(sem["qi_ready"], t)
                def gate(t):
                    pool.wait_ge(sem["sigma_g"], t + 1)
                    emptied(pool, sem, "g", t)
                    nc.gpsimd.tensor_tensor(G[:, t, :], G[:, t, :], SIGMA, ALU.mult).then_inc(sem["g_ready"], 1)
                gate(0)
                for h in range(HEADS):
                    for n, half in enumerate(HALVES):
                        v = [a.rearrange("p (b two i) -> p b two i", two=2, i=half)[:, :, 0, :] for a in (KLS[n % 2], KK, (DE, EQ)[n % 2])]
                        pool.wait_ge(sem["decay"], h * LEVELS + n + 1)
                        pool.wait_ge(sem["b_ready"], h + 1)
                        if n >= 2:
                            pool.wait_ge(sem["product"], PRODUCTS.index(("lv", h, n - 2)) + 1)
                        elif h:
                            pool.wait_ge(sem["product"], PRODUCTS.index(("kdT", h - 1)) + 1)
                        if h * LEVELS + n:
                            pool.wait_ge(sem["kL"], h * LEVELS + n)
                        else:
                            pool.wait_ge(sem["levels_zero"], 1)
                        nc.gpsimd.tensor_tensor(v[0], v[1], v[2], ALU.mult).then_inc(sem["kL"], 1)
                    pool.wait_ge(sem["ends"], h + 1)
                    pool.wait_ge(sem["product"], PRODUCTS.index(("lv", h, LEVELS - 2)) + 1)
                    pool.wait_ge(sem["kL"], (h + 1) * LEVELS)
                    nc.gpsimd.tensor_tensor(XX, KK, EQ, ALU.mult).then_inc(sem["kd_ready"], 1)
                    if h:
                        gate(h)
                    pool.wait_ge(sem["kd_ready"], h + 1)
                pool.wait_ge(sem["slots_ready"], 1)
                pool.wait_ge(zero_filled, FILLS * 16)
                for n in range(ACTIVE):
                    for t in range(T):
                        nc.gpsimd.indirect_dma_start(
                            out=XG, out_offset=bass.IndirectOffsetOnAxis(ap=slots[:, n, t:t + 1], axis=0),
                            in_=XB[:, t, :], in_offset=None).then_inc(scattered, 16)
                pool.wait_ge(sem["slots_ready"], 2)
                more_turns = pool.value_load(table[0:1, TAB_TURNS:TAB_TURNS + 1], min_val=MOE_TURNS - 1,
                                             max_val=MOE_TURNS - 1 + MAX_EXTRA)
                pool.wait_ge(scattered, L * (ACTIVE * T * 16) + ACTIVE * T * 16)
                pool.sem_inc(sem["moe_loads"], 1)
                for q in range(TURN):
                    pool.dma_start(XB[:, q, :], XG[q * P:(q + 1) * P, :]).then_inc(x_in[q], 16)

                pool.wait_ge(sem["in_moe"], 2)
                for name in SIGNALS:
                    if name not in LATE_SIGNALS:
                        pool.sem_clear(sem[name])

                def load(i, q):
                    pool.wait_ge(sem["moe_product"], i * (TURN * PER_TILE) + PER_TILE * q + 3)
                    pool.sem_inc(sem["moe_loads"], 1)
                    pool.dma_start(XB[:, q, :], XG[bass.ds(i * (TURN * P) + (TURN + q) * P, P), :])\
                        .then_inc(x_in[q], 16)

                def store(i, q):
                    pool.wait_ge(sem["moe_act_emptied"], i * (TURN * A_TILE) + A_TILE * (q + 1) + A_AHEAD)
                    pool.sem_inc(sem["moe_loads"], 1)
                    pool.dma_start(YG[bass.ds(i * (TURN * P) + q * P, P), :], YB[:, q % 2, :])\
                        .then_inc(y_out[q % 2], 16)
                with pool.Fori(0, more_turns) as i:
                    for q in range(TURN):
                        load(i, q)
                        store(i, q)
                for q in range(TURN):
                    store(more_turns, q)
                pool.wait_ge(sem["layer_end"], 4)
                for name in LATE_SIGNALS:
                    pool.sem_clear(sem[name])
                pool.sem_inc(cleared, 1)
                for n in range(2):
                    pool.wait_ge(y_out[n], L * (MOE_TURNS * 32) + extra_before * 32 + more_turns * 32 + 32 + 16)
                    pool.sem_inc(outputs_stored, 1)
                for t in range(T):
                    for n in range(ACTIVE):
                        nc.gpsimd.indirect_dma_start(
                            out=GOT[n][:, t, :], out_offset=None, in_=YG,
                            in_offset=bass.IndirectOffsetOnAxis(ap=slots[:, n, t:t + 1], axis=0))\
                            .then_inc(gathered[t], 16)

        @block.vector
        def _(dve):
            pi, two_pi = float(np.float32(3.1415925)), 2 * np.pi
            c1 = 6.28125
            c2 = float(np.float32(two_pi - c1))
            c3 = float(two_pi - c1 - c2)
            magic = 12582912.0
            own0 = Own(dve, prologue_own)
            dve.wait_ge(consts_in, 5 * 16)
            posf, ang, rounds, sine, cosine = rn_x, HT[:, 0:T, 0:96], HT[:, T:2 * T, 0:96], KIN[:, :, 0:96], HT[:, 0:T, 0:96]

            def step(ins):
                own0.done(ins)
                own0.need()
            dve.wait_ge(table_in, 16)
            step(nc.vector.tensor_copy(posf, pos))
            step(nc.vector.tensor_copy(iota, ROT[:, 96:96 + N_EXPERTS]))
            step(nc.vector.tensor_copy(powers, ROT[:, 96 + N_EXPERTS:96 + 2 * N_EXPERTS]))
            step(nc.vector.tensor_scalar(own_shift, iota, -float(P), float(P * (N_EXPERTS - 1)), ALU.mult, ALU.add))
            step(nc.vector.memset(extra_sum, 0.0))
            for t in range(T):
                step(nc.vector.tensor_scalar(ang[:, t, :], ROT[:, 0:96], posf[:, t:t + 1], None, ALU.mult))
            step(nc.vector.tensor_scalar(rounds, ang, 1 / two_pi, magic, ALU.mult, ALU.add))
            step(nc.vector.tensor_scalar(rounds, rounds, magic, None, ALU.subtract))
            for c in (c1, c2, c3):
                step(nc.vector.scalar_tensor_tensor(ang, rounds, -c, ang, ALU.mult, ALU.add))
            step(nc.vector.tensor_scalar(sine, ang, pi, -pi, ALU.min, ALU.max))
            step(nc.vector.tensor_scalar(ang, ang, pi / 2, None, ALU.add))
            step(nc.vector.tensor_scalar(rounds, ang, pi, -two_pi, ALU.is_gt, ALU.mult))
            step(nc.vector.tensor_tensor(ang, ang, rounds, ALU.add))
            step(nc.vector.tensor_scalar(ang, ang, pi, -pi, ALU.min, ALU.max))
            peak = small[:, 248:248 + HEADS]
            step(nc.vector.tensor_copy(peak, lb_all[:, 0, :]))
            for l in range(1, DEPTH):
                step(nc.vector.tensor_tensor(peak, peak, lb_all[:, l, :], ALU.max))
            own0.done(nc.vector.tensor_tensor(lb_all, lb_all, over(peak, DEPTH), ALU.subtract))
            own0.need()
            dve.sem_inc(ropes, 1)
            dve.wait_ge(pro_act, M + 5)
            half_m, half_i = DH // 2, IDX_DIM // 2
            step(nc.vector.tensor_copy(cos_m, cosine[:, :, 0:half_m]))
            step(nc.vector.tensor_copy(cos_i, cosine[:, :, half_m:half_m + half_i]))
            step(nc.vector.tensor_copy(sin_m[:, :, 1, :], sine[:, :, 0:half_m]))
            step(nc.vector.tensor_scalar(sin_m[:, :, 0, :], sine[:, :, 0:half_m], -1.0, None, ALU.mult))
            step(nc.vector.tensor_copy(sin_i[:, :, 1, :], sine[:, :, half_m:half_m + half_i]))
            step(nc.vector.tensor_scalar(sin_i[:, :, 0, :], sine[:, :, half_m:half_m + half_i], -1.0, None, ALU.mult))
            whole = small[:, 252:252 + HEADS]
            step(nc.vector.tensor_copy(whole, lb_all[:, 0, :]))
            for l in range(1, DEPTH):
                step(nc.vector.tensor_tensor(whole, whole, lb_all[:, l, :], ALU.add))
            step(nc.vector.reciprocal(whole, whole))
            step(nc.vector.memset(lb_all[:, 0, :], 0.0))
            for l in range(1, DEPTH):
                step(nc.vector.tensor_tensor(lb_all[:, l, :], lb_all[:, l, :], lb_all[:, l - 1, :], ALU.add))
            step(nc.vector.tensor_tensor(lb_all, lb_all, over(whole, DEPTH), ALU.mult))
            step(nc.vector.tensor_copy(mask, masks_in))
            step(nc.vector.memset(ones, 1.0))
            step(nc.vector.memset(bias0, 0.0))
            step(nc.vector.memset(bias0[0:CHUNK, CHUNK:P], REFUSED))
            dve.sem_inc(prologue, 1)
            dve.wait_ge(x_loaded, 16)
            dve.sem_inc(combined, T)

            with dve.Fori(0, DEPTH) as L:
                own = Own(dve, sem["dve_own"])
                em = Emptier(dve, "dve", sem, banks)
                own.done(nc.vector.tensor_copy(lb, lb_all.rearrange("p l h -> p (l h)")[:, bass.ds(L * HEADS, HEADS)]))
                own.need()
                nc.vector.tensor_scalar(one_lb, lb, -1.0, 1.0, ALU.mult, ALU.add).then_inc(sem["lb_ready"], 1)

                def scale_tokens(t, base, dst=XN):
                    dve.wait_ge(sem["rn_x"], base + t + 1)
                    nc.vector.tensor_scalar(dst[:, t], X[:, t, :].rearrange("p (d k) -> p k d", k=K),
                                            rn_x[:, t:t + 1], None, ALU.mult).then_inc(sem["x_scaled"], 1)

                def transposed_tokens(key, t, gain):
                    for n in range(2):
                        bank = em.take(key, t, n).rearrange("p (k t) -> p k t", k=4)
                        em.empty(nc.vector.tensor_tensor(HT[:, 4 * n:4 * n + 4, t * P:(t + 1) * P], bank,
                                                         each(cols[:, gain + 4 * n:gain + 4 * n + 4], P), ALU.mult),
                                 key, t, n)
                for m in range(M):
                    dve.wait_ge(sem["rn_kx"], m + 1)
                    v = TOK[:, m, :].rearrange("p (h d) -> p h d", h=HEADS)
                    nc.vector.tensor_tensor(v, v, each(rn_h[:, m, :], P), ALU.mult).then_inc(sem["kx_ready"], 1)
                dve.wait_ge(sem["params"], 32)
                dve.wait_ge(sem["cols_ready"], 1)
                for t in range(T):
                    scale_tokens(t, 0)
                    if t:
                        transposed_tokens("hT", t - 1, G_MIX)
                transposed_tokens("hT", T - 1, G_MIX)

                rot = ROT
                for t in range(T):
                    dve.wait_ge(sem["rn_ql"], t + 1)
                    nc.vector.tensor_scalar(C[:, t, :], C[:, t, :], rn_ql[:, t, 0:1], None, ALU.mult)\
                        .then_inc(sem["c_ready"], 1)
                for t in range(T):
                    own.done(nc.vector.tensor_scalar(widx[:, t, :], KI[:, t, IDX_DIM:N_KI], W_IDX, None, ALU.mult))
                    ki = KI[:, t, 0:IDX_DIM]
                    own.done(nc.vector.scalar_tensor_tensor(ki, ki, rn_ql[:, t, 1:2], rows[:, R_KI:R_KI + IDX_DIM],
                                                            ALU.mult, ALU.mult))
                    own.need()
                    half = IDX_DIM // 2
                    r = rot[:, 128 * t:128 * t + 128]
                    for a in range(2):
                        own.done(nc.vector.tensor_tensor(r[:, a * half:(a + 1) * half], ki[:, (1 - a) * half:(2 - a) * half],
                                                         sin_i[:, t, a, :], ALU.mult))
                    for a in range(2):
                        own.done(nc.vector.tensor_tensor(r[:, 64 + a * half:64 + (a + 1) * half],
                                                         ki[:, a * half:(a + 1) * half], cos_i[:, t, :], ALU.mult))
                    own.need()
                    nc.vector.tensor_tensor(KIN[:, t, :].rearrange("p (n i) -> p n i", n=2), over(r[:, 64:128], 2),
                                            over(r[:, 0:64], 2), ALU.add).then_inc(sem["ki_ready"], 1)
                for key, gain in (("kb", R_K), ("qb", R_Q)):
                    for t in range(T):
                        s = t % 2
                        dve.wait_ge(sem["rn_" + key], t + 1)
                        for h in range(HEADS):
                            v = TOK[:, s, h * P:(h + 1) * P]
                            own.done(nc.vector.scalar_tensor_tensor(v, v, rn_h[:, s, h:h + 1], rows[:, gain:gain + DH],
                                                                    ALU.mult, ALU.mult))
                        own.need()
                        v = TOK[:, s, :].rearrange("p (h two i) -> p h two i", h=HEADS, two=2)
                        r = rot.rearrange("p (h two i) -> p h two i", h=HEADS, two=2)
                        for a in range(2):
                            own.done(nc.vector.tensor_tensor(r[:, :, a, :], v[:, :, 1 - a, :],
                                                             over(sin_m[:, t, a, :], HEADS), ALU.mult))
                        own.need()
                        vv = TOK[:, s, :].rearrange("p (n i) -> p n i", i=DH // 2)
                        own.done(nc.vector.tensor_tensor(vv, vv, over(cos_m[:, t, :], 2 * HEADS), ALU.mult))
                        own.need()
                        nc.vector.tensor_tensor(TOK[:, s, :], TOK[:, s, :], rot, ALU.add).then_inc(sem[key + "_ready"], 1)
                        dve.wait_ge(sem[key + "_ready"], t + 1)

                dve.wait_ge(zero_filled, FILLS * 16)
                for n in range(2):
                    dve.wait_ge(y_out[n], 16)
                for t in LATER:
                    sc = SC[:, t - 1, 0:(t + 1) * P]
                    for h in range(IDX_HEADS):
                        n = (t - 1) * IDX_HEADS + h
                        emptied(dve, sem, "si", t, h)
                        r = RELU[:, n % 2, 0:(t + 1) * P]
                        if h == 0:
                            ins = nc.vector.tensor_scalar(sc, r, widx[:, t, h:h + 1], None, ALU.mult)
                        else:
                            dve.wait_ge(sem["relu_used"], n)
                            ins = nc.vector.scalar_tensor_tensor(sc, r, widx[:, t, h:h + 1], sc, ALU.mult, ALU.add)
                        ins.then_inc(sem["relu_used"], 1)
                    dve.wait_ge(sem["relu_used"], t * IDX_HEADS)
                    last = own.done(nc.vector.memset(sc[0:CHUNK, t * P + CHUNK:(t + 1) * P], REFUSED))
                step_of = {t: last for t in LATER}
                for r in range(TOPK // 8):
                    for t in LATER:
                        own.need(step_of[t])
                        step_of[t] = own.done(nc.vector.max(top8[:, t - 1, :], SC[:, t - 1, 0:(t + 1) * P]))
                    for t in LATER:
                        sc = SC[:, t - 1, 0:(t + 1) * P]
                        own.need(step_of[t])
                        step_of[t] = own.done(nc.vector.match_replace(sc, top8[:, t - 1, :], sc, TAKEN))
                for t in LATER:
                    sc = SC[:, t - 1, 0:(t + 1) * P]
                    own.need(step_of[t])
                    own.done(nc.vector.tensor_scalar(sc, sc, TAKEN / 1.5, REFUSED, ALU.is_ge, ALU.mult))

                nc.vector.memset(CB[:, 1024:2048], 0.0).then_inc(sem["levels_zero"], 1)
                dve.wait_ge(sem["levels_zero"], 1)
                for h in range(HEADS):
                    dve.wait_ge(sem["forget"], h + 1)
                    own.done(nc.vector.tensor_tensor(L2, L2, L1, ALU.subtract))
                    if h:
                        dve.wait_ge(sem["product"], PRODUCTS.index(("lv", h - 1, LEVELS)) + 1)
                        dve.wait_ge(sem["kd_ready"], h)
                    own.done(nc.vector.scalar_tensor_tensor(KK, E1, one_lb[:, h:h + 1], S1, ALU.mult, ALU.mult))
                    own.need(own.count - 1)
                    for t in range(T):
                        s = slice(t * P, (t + 1) * P)
                        own.done(nc.vector.tensor_tensor_scan(BB[:, s], ones, L2[:, s], 0.0, ALU.mult, ALU.add))
                    dve.wait_ge(sem["queries"], h + 1)
                    em.empty(nc.vector.tensor_tensor(QQ, em.take("q", h), EQ, ALU.mult), "q", h)
                    own.need()
                    dve.wait_ge(sem["dve_emptied"], em.count)
                    if h:
                        dve.wait_ge(sem["product"], PRODUCTS.index(("o", h - 1)) + 1)

                    def halves(a, half):
                        return a.rearrange("p (b two i) -> p b two i", two=2, i=half)

                    def diff(n):
                        half = HALVES[n]
                        d = (DE, EQ)[n % 2].rearrange("p (b i) -> p b i", i=2 * half)
                        b = BB.rearrange("p (b i) -> p b i", i=2 * half)
                        ref = b[:, :, half - 1:half].broadcast_to((P, SEQ // (2 * half), 2 * half))
                        return nc.vector.tensor_tensor(d, b, ref, ALU.subtract)

                    def level_queries(n):
                        half = HALVES[n]
                        dve.wait_ge(sem["decay"], h * LEVELS + n + 1)
                        if n >= 2:
                            dve.wait_ge(sem["product"], PRODUCTS.index(("lv", h, n - 2)) + 1)
                            dve.wait_ge(sem["qL"], h * LEVELS + n)
                        nc.vector.tensor_tensor(halves(QLS[n % 2], half)[:, :, 1, :], halves(QQ, half)[:, :, 1, :],
                                                halves((DE, EQ)[n % 2], half)[:, :, 1, :], ALU.mult)\
                            .then_inc(sem["qL"], 1)

                    def level_scores(n):
                        bank = em.take("lv", h, n).rearrange("p (t s) -> p t s", t=T)
                        out4 = SCT.rearrange("p (t s) -> p t s", t=T)
                        dve.wait_ge(sem["dve_emptied"], em.count)
                        em.empty(nc.vector.copy_predicated(out4, over(mask[:, n, :], T), bank), "lv", h, n)
                    diff(0).then_inc(sem["b_ready"], 1)
                    dve.wait_ge(sem["b_ready"], h + 1)
                    own.done(nc.vector.memset(SCT, 0.0))
                    own.need()
                    dve.sem_inc(sem["diff"], 1)
                    for n in range(LEVELS):
                        if n + 1 < LEVELS:
                            if n:
                                dve.wait_ge(sem["kL"], h * LEVELS + n)
                                dve.wait_ge(sem["qL"], h * LEVELS + n)
                            diff(n + 1).then_inc(sem["diff"], 1)
                        level_queries(n)
                        if n:
                            level_scores(n - 1)
                    dve.wait_ge(sem["kL"], h * LEVELS + LEVELS - 1)
                    b = BB.rearrange("p (t i) -> p t i", t=T)
                    nc.vector.tensor_tensor(EQ.rearrange("p (t i) -> p t i", t=T), b,
                                            b[:, :, P - 1:P].broadcast_to((P, T, P)), ALU.subtract).then_inc(sem["diff"], 1)
                    level_scores(LEVELS - 1)
                    level_scores(LEVELS)
                    dve.wait_ge(sem["ends"], h + 1)
                    nc.vector.tensor_tensor(QL, QQ, DE, ALU.mult).then_inc(sem["qe_ready"], 1)
                    bank = em.take("dS", h)
                    dve.wait_ge(sem["qe_ready"], h + 1)
                    own.done(nc.vector.tensor_copy(ST[:, 1, :], bank[:, 0:P]))
                    for t in range(1, T - 1):
                        own.need()
                        ins = nc.vector.scalar_tensor_tensor(ST[:, t + 1, :], ST[:, t, :], e_end[:, t:t + 1],
                                                             bank[:, t * P:(t + 1) * P], ALU.mult, ALU.add)
                        if t == T - 2:
                            em.empty(ins, "dS", h)
                        else:
                            own.done(ins)
                for t in range(T):
                    dve.wait_ge(sem["rn_o"], t + 1)
                    dve.wait_ge(sem["g_ready"], t + 1)
                    for h in range(HEADS):
                        s = slice(h * P, (h + 1) * P)
                        ins = nc.vector.scalar_tensor_tensor(O[:, t, s], O[:, t, s], rn_h[:, t % 2, h:h + 1], G[:, t, s],
                                                             ALU.mult, ALU.mult)
                        if h == HEADS - 1:
                            ins.then_inc(sem["og_ready"], 1)
                        else:
                            own.done(ins)

                def masked(m):
                    t, h = divmod(m, HEADS)
                    w = (t + 1) * P
                    bank = em.take("lg", m)
                    if m >= 2:
                        em.take("pT", m - 2)
                    bias = SC[:, t - 1, 0:w] if t else bias0
                    em.empty(nc.vector.scalar_tensor_tensor(PR[:, m % 2, 0:w], bank[:, 0:w], SCALE, bias,
                                                            ALU.mult, ALU.add), "lg", m)
                    dve.wait_ge(sem["dve_emptied"], em.count)
                    nc.vector.tensor_reduce(mx[:, m % 4, 0:1], PR[:, m % 2, 0:w], AX.X, ALU.max, negate=True)\
                        .then_inc(sem["logits"], 1)

                def normalised(m):
                    w = (m // HEADS + 1) * P
                    dve.wait_ge(sem["exps"], m + 1)
                    own.done(nc.vector.reciprocal(sm[:, m % 4, 1:2], sm[:, m % 4, 0:1]))
                    own.need()
                    nc.vector.tensor_scalar(PR[:, m % 2, 0:w], PR[:, m % 2, 0:w], sm[:, m % 4, 1:2], None, ALU.mult)\
                        .then_inc(sem["probs"], 1)

                def attended(m):
                    t, h = divmod(m, HEADS)
                    em.empty(nc.vector.tensor_copy(OAB[:, HEADS + h, t * P:(t + 1) * P], em.take("pv", m)[:, 0:P]), "pv", m)
                def projected(m):
                    t, n = m // 4, m // 2 % 2
                    s = slice(n * 512, (n + 1) * 512)
                    if m % 2:
                        dve.wait_ge(sem["dve_emptied"], xa_count[m - 1])
                    em.empty(nc.vector.tensor_tensor(X[:, t, s], X[:, t, s], em.take("xa", m), ALU.add), "xa", m)
                    xa_count[m] = em.count
                xa_count = {}
                dve.wait_ge(sem["og_ready"], T)
                last_m = T * HEADS
                for m in range(last_m + 3):
                    if m < last_m:
                        masked(m)
                    if 0 <= m - 1 < last_m:
                        normalised(m - 1)
                    if m - 3 >= 0:
                        attended(m - 3)
                    if 0 <= m - 2 < last_m:
                        projected(m - 2)
                dve.wait_ge(sem["dve_emptied"], xa_count[last_m - 1])

                def add_to_tokens(key, m):
                    t, n = divmod(m, 2)
                    s = slice(n * 512, (n + 1) * 512)
                    em.empty(nc.vector.tensor_tensor(X[:, t, s], X[:, t, s], em.take(key, t, n), ALU.add), key, t, n)
                for t in range(T):
                    add_to_tokens("xo", 2 * t)
                    add_to_tokens("xo", 2 * t + 1)
                    if t:
                        transposed_tokens("hxT", t - 1, G_X)
                    scale_tokens(t, T, XNX)
                transposed_tokens("hxT", T - 1, G_X)

                for t in range(T):
                    dve.wait_ge(sem["rn_qx"], t + 1)
                    v = TOK[:, t % 2, :].rearrange("p (h d) -> p h d", h=HEADS)
                    nc.vector.tensor_tensor(v, v, each(rn_h[:, t % 2, :], P), ALU.mult).then_inc(sem["qx_ready"], 1)

                def peak_x(m):
                    bank = em.take("lx", m).rearrange("p (a s) -> p a s", a=2)
                    own.done(nc.vector.tensor_reduce(mx[:, m % 4, :], bank, AX.X, ALU.max, negate=True))
                    own.need()
                    nc.vector.tensor_scalar(mx[:, m % 4, :], mx[:, m % 4, :], SCALE, None, ALU.mult)\
                        .then_inc(sem["max_x"], 1)

                def normalised_x(m):
                    emptied(dve, sem, "lx", m)
                    own.done(nc.vector.reciprocal(sm[:, m % 4, :], sm[:, m % 4, :]))
                    own.need()
                    v = PR[:, m % 2, :].rearrange("p (a s) -> p a s", a=2)
                    nc.vector.tensor_tensor(v, v, each(sm[:, m % 4, :], N_MEM), ALU.mult).then_inc(sem["probs_x"], 1)

                def transposed_x(m):
                    bank = em.take("pxT", m)
                    if m >= 2 and m % 2 == 0:
                        em.take("px", m // 2 - 1)
                    em.empty(nc.vector.tensor_copy(PT[:, m % 2, :], bank), "pxT", m)
                for m in range(2 * T + 2):
                    if m < 2 * T:
                        peak_x(m)
                    if 0 <= m - 1 < 2 * T:
                        normalised_x(m - 1)
                    if m >= 2:
                        transposed_x(m - 2)
                    if m >= 5:
                        add_to_tokens("xx", m - 5)
                scale_tokens(0, 2 * T)
                for t in range(3):
                    add_to_tokens("xx", 2 * T - 3 + t)
                    if t + 1 < 3:
                        scale_tokens(t + 1, 2 * T)
                    transposed_tokens("hfT", t, G_FFN)
                scale_tokens(T - 1, 2 * T)
                transposed_tokens("hfT", T - 1, G_FFN)

                def do(ins):
                    own.done(ins)
                    own.need()
                tt, ts, red = nc.vector.tensor_tensor, nc.vector.tensor_scalar, nc.vector.tensor_reduce
                bank = em.take("rt")
                em.empty(tt(rlog, bank[:, 0:T * N_ROUTE].rearrange("p (t n) -> p t n", t=T),
                            over(rows[:, R_BIAS:N_ROW], T), ALU.add), "rt")
                dve.wait_ge(sem["dve_emptied"], em.count)
                groups = rlog[:, :, 0:N_GROUPS]

                def first_best(scores, width, best, chosen, marked, peak):
                    do(red(best, scores, AX.X, ALU.max))
                    do(tt(marked, scores, best.broadcast_to((P, T, width)), ALU.is_equal))
                    do(tt(marked, marked, over(powers[:, 0:width], T), ALU.mult))
                    do(red(peak, marked, AX.X, ALU.max))
                    do(tt(chosen, marked, peak.broadcast_to((P, T, width)), ALU.is_equal))
                best_g, best_1, best_2, peak = (rw[:, n, :, 0:1] for n in (0, 3, 4, 5))
                first_best(groups, N_GROUPS, best_g, rw[:, 2], rw[:, 6], peak)
                tt(rw[:, 1], groups, best_g.broadcast_to((P, T, N_GROUPS)), ALU.subtract).then_inc(sem["router_logits"], 1)
                do(ts(rw[:, 6], rw[:, 2], -REFUSED, REFUSED, ALU.mult, ALU.add))
                do(tt(scores16.rearrange("p t (g e) -> p t g e", g=N_GROUPS),
                      rlog[:, :, N_GROUPS:].rearrange("p t (g e) -> p t g e", g=N_GROUPS),
                      rw[:, 6].unsqueeze(3).broadcast_to((P, T, N_GROUPS, EXP_PER_GROUP)), ALU.add))
                first_best(scores16, N_EXPERTS, best_1, chosen1, marked16, peak)
                do(nc.vector.scalar_tensor_tensor(scores16, chosen1, REFUSED, scores16, ALU.mult, ALU.add))
                first_best(scores16, N_EXPERTS, best_2, chosen2, marked16, peak)
                own.done(nc.vector.tensor_copy(tri, mask[:, LEVELS + 1, :]))
                own.need()
                tt(chosen, chosen1, chosen2, ALU.add).then_inc(sem["chosen"], 1)
                tt(rw[:, 8, :, 0:1], best_2, best_1, ALU.subtract).then_inc(sem["router_logits"], 1)
                bank = em.take("rank")
                per_tile = bank[:, 64:128].rearrange("p (t e) -> p t e", t=T)
                do(nc.vector.memset(base[:, 0, :], 0.0))
                for t in range(1, T):
                    do(tt(base[:, t, :], base[:, t - 1, :], per_tile[:, t - 1, :], ALU.add))
                do(tt(total, base[:, T - 1, :], per_tile[:, T - 1, :], ALU.add))
                em.empty(tt(rank, base, bank[:, 0:64].rearrange("p (t e) -> p t e", t=T), ALU.add), "rank")
                do(ts(over_e, total, float(P), None, ALU.is_gt))
                for n in range(2, T):
                    do(nc.vector.scalar_tensor_tensor(over_e, total, float(n * P), over_e, ALU.is_gt, ALU.add))
                do(nc.vector.tensor_tensor_scan(cum, ones[:, 0:N_EXPERTS], over_e, 0.0, ALU.mult, ALU.add))
                do(tt(shift, cum, over_e, ALU.subtract))
                do(nc.vector.scalar_tensor_tensor(shift, shift, float(P), own_shift, ALU.mult, ALU.add))
                dve.wait_ge(sem["dve_emptied"], em.count)
                do(nc.vector.scalar_tensor_tensor(place, over(iota, T), float(P), rank, ALU.mult, ALU.add))
                do(nc.vector.scalar_tensor_tensor(rank, rank, float(P), over(shift, T), ALU.is_ge, ALU.mult))
                do(tt(place, place, rank, ALU.add))
                both = SC[:, 2, 0:2 * T * N_EXPERTS].rearrange("p (n t e) -> p n t e", n=2, t=T)
                do(tt(both, both, place.unsqueeze(1).broadcast_to((P, ACTIVE, T, N_EXPERTS)), ALU.mult))
                do(red(placef.rearrange("p (n t) -> p n t", n=ACTIVE), both, AX.X, ALU.add))
                do(nc.vector.tensor_copy(slots.rearrange("p n t -> p (n t)"), placef))
                dve.sem_inc(sem["slots_ready"], 1)
                do(tt(before_j, over(cum, 8), each(iota[:, 0:8], N_EXPERTS), ALU.is_le))
                do(red(expert_j, before_j, AX.X, ALU.add))
                do(ts(table[:, 0:8], expert_j, float(N_EXPERTS - 1), None, ALU.min))
                do(ts(extra, cum[:, N_EXPERTS - 1:], 0.0, None, ALU.is_gt))
                for n in range(1, MAX_EXTRA):
                    do(nc.vector.scalar_tensor_tensor(extra, cum[:, N_EXPERTS - 1:], float(n * TURN), extra,
                                                      ALU.is_gt, ALU.add))
                do(nc.vector.tensor_copy(table[:, TAB_EXTRA:TAB_EXTRA + 1], extra))
                do(ts(table[:, TAB_TURNS:TAB_TURNS + 1], extra, float(MOE_TURNS - 1), None, ALU.add))
                do(tt(extra_sum, extra_sum, extra, ALU.add))
                do(nc.vector.tensor_copy(table[:, bass.ds(L + TAB_BEFORE + 1, 1)], extra_sum))
                dve.wait_ge(sem["router_exp"], 2)
                do(red(rw[:, 10, :, 0:1], rw[:, 1], AX.X, ALU.add))
                do(ts(rw[:, 10, :, 1:2], rw[:, 8, :, 0:1], 1.0, None, ALU.add))
                do(tt(rw[:, 10, :, 0:1], rw[:, 10, :, 0:1], rw[:, 10, :, 1:2], ALU.mult))
                do(nc.vector.reciprocal(rw[:, 10, :, 0:1], rw[:, 10, :, 0:1]))
                do(tt(rw[:, 10, :, 1:2], rw[:, 10, :, 0:1], rw[:, 8, :, 0:1], ALU.mult))
                assert em.count == len(EMPTIED["dve"])
                dve.sem_inc(sem["slots_ready"], 1)

                more_turns = dve.value_load(table[0:1, TAB_TURNS:TAB_TURNS + 1], min_val=MOE_TURNS - 1,
                                            max_val=MOE_TURNS - 1 + MAX_EXTRA)

                def made(i, at):
                    dve.wait_ge(sem["moe_product"], i * (TURN * PER_TILE) + at + 1)
                    return banks[at % BANKS]

                def tokens(i, q, at):
                    for n in range(2):
                        gain = cols[:, G_FFN + 4 * n:G_FFN + 4 * n + 4]
                        bank = made(i, at + n).rearrange("p (k t) -> p k t", k=4)
                        tt(XT[:, q % 2, 4 * n:4 * n + 4, :], bank, each(gain, P), ALU.mult)\
                            .then_inc(sem["moe_dve_emptied"], 1)

                def hidden(i, q):
                    at = PER_TILE * q if q else 2
                    dve.wait_ge(sem["silu"], i * TURN + q + 1)
                    tt(HID[:, q % 2, :], SILU[:, q % 2, :], banks[at % BANKS][:, D_EXPERT:2 * D_EXPERT], ALU.mult)\
                        .then_inc(sem["moe_dve_emptied"], 1)

                def tile(i, q, last=False):
                    at = PER_TILE * q
                    hidden(i, q)
                    if not last:
                        tokens(i, q + 1, at + 1 if q else 3)
                    bank = made(i, at + 3 if last else at + 5)[:, 0:2 * P]
                    nc.vector.tensor_copy(HIDT[:, q % 2].rearrange("p f t -> p (f t)"), bank)\
                        .then_inc(sem["moe_dve_emptied"], 1)
                tokens(0, 0, 0)
                tile(0, 0)
                with dve.Fori(0, more_turns) as i:
                    for q in range(1, TURN + 1):
                        tile(i, q)
                for q in range(1, TURN):
                    tile(more_turns, q, last=q == TURN - 1)
                dve.sem_inc(sem["layer_end"], 1)

                def second(t):
                    dve.wait_ge(first_added, L * T + t + 1)
                    nc.vector.scalar_tensor_tensor(X[:, t, :], GOT[1][:, t, :], rw[:, 10, t, 1:2], X[:, t, :],
                                                   ALU.mult, ALU.add).then_inc(combined, 1)
                for t in range(T):
                    dve.wait_ge(gathered[t], L * (ACTIVE * 16) + ACTIVE * 16)
                    nc.vector.scalar_tensor_tensor(X[:, t, :], GOT[0][:, t, :], rw[:, 10, t, 0:1], X[:, t, :],
                                                   ALU.mult, ALU.add).then_inc(first_added, 1)
                    if t:
                        second(t - 1)
                second(T - 1)
                dve.wait_ge(cleared, L + 1)


def kernel(x, mem, positions, norm_mix, w_in, lb_raw, a_gnorm, b_qlat_gain, b_wqb, b_wqidx, b_qnorm, b_knorm,
           b_kidx_norm, w_out, norm_x, norm_mem, x_wq, x_wk, x_wv, x_wo, x_qnorm, x_knorm, norm_ffn, w_rg, b_rg,
           w_re, b_re, w_gu, w_dn):
    import concourse.bacc as bacc
    from concourse.bass_utils import run_bass_kernel_spmd

    a = {k: np.asarray(v) for k, v in locals().items() if k not in ("bacc", "run_bass_kernel_spmd")}
    by_row = lambda v: v.reshape(DEPTH, P, K)
    by_block = lambda v: np.transpose(v.reshape(DEPTH, -1, P), (0, 2, 1))
    col = np.concatenate([by_row(a["norm_mix"]), by_row(a["norm_x"]), by_row(a["norm_mem"]), by_row(a["norm_ffn"]),
                          by_block(a["b_qlat_gain"]), by_block(a["a_gnorm"]), by_block(a["x_qnorm"]),
                          by_block(a["x_knorm"])], axis=2)
    row = np.concatenate([a["b_qnorm"], a["b_knorm"], a["b_kidx_norm"], a["b_rg"], a["b_re"].reshape(DEPTH, -1)], axis=1)
    router = np.concatenate([a["w_rg"], a["w_re"].reshape(DEPTH, D_MODEL, N_EXPERTS)], axis=2)
    lb0 = np.transpose(a["lb_raw"].reshape(DEPTH, HEADS, P), (2, 0, 1))
    freq = np.concatenate([ROPE_THETA ** (-np.arange(0, d, 2) / d) for d in (DH, IDX_DIM)]
                          + [np.arange(N_EXPERTS), 2.0 ** np.arange(N_EXPERTS)[::-1]]).astype(np.float32)
    s, t = np.arange(P)[:, None], np.arange(P)[None, :]
    masks = np.stack([(s // (2 * h) == t // (2 * h)) & (s // h < t // h) for h in HALVES] + [s == t, s < t], axis=1).astype(np.int32)
    feed = {
        "x": a["x"], "mem": a["mem"], "positions": a["positions"].reshape(T, P).T, "w_in": a["w_in"], "b_wqb": a["b_wqb"],
        "b_wqidx": a["b_wqidx"], "w_out": a["w_out"], "x_wq": a["x_wq"], "x_wk": a["x_wk"], "x_wv": a["x_wv"],
        "x_wo": a["x_wo"], "router": router, "w_gu": a["w_gu"], "w_dn": a["w_dn"], "colparams": col,
        "rowparams": row, "lb_raw": lb0, "freqs": freq, "ident": np.eye(P, dtype=np.float32), "masks": masks,
        "zeros": np.zeros((P, 16), np.int32),
    }
    feed = {k: np.ascontiguousarray(v) for k, v in feed.items()}
    nc = bacc.Bacc("TRN2", target_bir_lowering=False, num_devices=1)
    ap = {k: nc.dram_tensor("in_" + k, v.shape, mybir.dt.from_np(v.dtype), kind="ExternalInput").ap()
          for k, v in feed.items()}
    out = nc.dram_tensor("out_0", (1, SEQ, D_MODEL), F32, kind="ExternalOutput").ap()
    hybrid_block(nc, ap["x"], ap["mem"], ap["positions"], ap["w_in"], ap["b_wqb"], ap["b_wqidx"], ap["w_out"],
                 ap["x_wq"], ap["x_wk"], ap["x_wv"], ap["x_wo"], ap["router"], ap["w_gu"], ap["w_dn"],
                 ap["colparams"], ap["rowparams"], ap["lb_raw"], ap["freqs"], ap["ident"], ap["masks"], ap["zeros"], out)
    r = run_bass_kernel_spmd(nc, [{"in_" + k: v for k, v in feed.items()}], core_ids=[0])
    return r.results[0]["out_0"]
```
